# Optimizing a Trainium2 kernel written in Bass

```python
import math
import jax, jax.numpy as jnp
from jax import lax
import numpy as np

D_MODEL = 1024
BATCH = 1
SEQ = 256
DEPTH = 2

N_MEM = 256
EPS = 1e-5
N_EVEN = (DEPTH + 1) // 2
N_ODD = DEPTH // 2

SSD_HEADS = 16
SSD_HEAD_DIM = 64
SSD_INNER = SSD_HEADS * SSD_HEAD_DIM
SSD_GROUPS = 2
SSD_STATE = 64
SSD_CONV = 4
SSD_CHUNK = 128
SSD_XBC = SSD_INNER + 2 * SSD_GROUPS * SSD_STATE

GLA_HEADS = 4
GLA_KEY = D_MODEL // 2
GLA_VAL = D_MODEL
GLA_HK = GLA_KEY // GLA_HEADS
GLA_HV = GLA_VAL // GLA_HEADS
GLA_RANK = 16
GLA_TAU = 16.0
GLA_CHUNK = 64

IN_SPLITS = (SSD_INNER, SSD_XBC, SSD_HEADS, GLA_KEY, GLA_KEY, GLA_VAL, GLA_RANK, GLA_VAL)
IN_WIDTH = sum(IN_SPLITS)
MIX_WIDTH = SSD_INNER + GLA_VAL

DIFF_HEADS = 8
DIFF_HEAD_DIM = 64
DIFF_V_DIM = 2 * DIFF_HEAD_DIM
DIFF_QK = DIFF_HEADS * 2 * DIFF_HEAD_DIM
DIFF_QKV = 2 * DIFF_QK + DIFF_HEADS * DIFF_V_DIM
Q_BLOCK = 128

X_HEADS = 4
X_HEAD_DIM = D_MODEL // X_HEADS

D_FF = 4 * D_MODEL

kernel_name = "hybrid_ssd_gla_diffattn_trunk"

def rmsnorm(x, w):
    xf = x.astype(jnp.float32)
    y = xf * lax.rsqrt(jnp.mean(xf * xf, axis=-1, keepdims=True) + EPS)
    return (y * w.astype(jnp.float32)).astype(x.dtype)

def causal_dwconv(x, w, b):
    k = w.shape[0]
    y = lax.conv_general_dilated(
        x, w[:, None, :].astype(x.dtype), window_strides=(1,), padding=[(k - 1, 0)],
        dimension_numbers=("NWC", "WIO", "NWC"), feature_group_count=x.shape[-1])
    return y + b.astype(x.dtype)

def to_chunks(t, size):
    b, l = t.shape[:2]
    return jnp.moveaxis(t.reshape(b, l // size, size, *t.shape[2:]), 1, 0)

def from_chunks(t):
    nc, b, q = t.shape[:3]
    return jnp.moveaxis(t, 0, 1).reshape(b, nc * q, *t.shape[3:])

def ssd_chunked(x, dt, a, bmat, cmat):
    f32 = jnp.float32
    b, l, h, p = x.shape
    g, n = bmat.shape[2:]
    e = h // g
    xdt = (x.astype(f32) * dt.astype(f32)[..., None]).reshape(b, l, g, e, p)
    loga = (dt.astype(f32) * a.astype(f32)).reshape(b, l, g, e)
    mask = jnp.tril(jnp.ones((SSD_CHUNK, SSD_CHUNK), dtype=bool))[None, :, :, None, None]

    def step(state, inp):
        xc, ac, bc, cc = inp
        cum = jnp.cumsum(ac, axis=1)
        seg = cum[:, :, None] - cum[:, None, :]
        decay = jnp.exp(jnp.where(mask, seg, -jnp.inf))
        scores = jnp.einsum("bqgn,bsgn->bqsg", cc, bc)
        y = jnp.einsum("bqsg,bqsge,bsgep->bqgep", scores, decay, xc)
        y = y + jnp.einsum("bqgn,bgepn->bqgep", cc, state) * jnp.exp(cum)[..., None]
        last = cum[:, -1]
        wts = jnp.exp(last[:, None] - cum)
        state = state * jnp.exp(last)[..., None, None] + jnp.einsum("bsge,bsgep,bsgn->bgepn", wts, xc, bc)
        return state, y

    state0 = jnp.zeros((b, g, e, p, n), f32)
    inputs = (to_chunks(xdt, SSD_CHUNK), to_chunks(loga, SSD_CHUNK),
              to_chunks(bmat.astype(f32), SSD_CHUNK), to_chunks(cmat.astype(f32), SSD_CHUNK))
    _, ys = lax.scan(step, state0, inputs)
    return from_chunks(ys).reshape(b, l, h, p).astype(x.dtype)

def gla_chunked(q, k, v, logg):
    f32 = jnp.float32
    b, l, h, dk = q.shape
    dv = v.shape[-1]
    mask = jnp.tril(jnp.ones((GLA_CHUNK, GLA_CHUNK), dtype=bool))[None, :, :, None, None]

    def step(s_state, inp):
        qc, kc, vc, gc = inp
        cum = jnp.cumsum(gc, axis=1)
        seg = cum[:, :, None] - cum[:, None, :]
        decay = jnp.exp(jnp.where(mask, seg, -jnp.inf))
        scores = jnp.einsum("bqhk,bshk,bqshk->bqsh", qc, kc, decay)
        o = jnp.einsum("bqsh,bshv->bqhv", scores, vc)
        o = o + jnp.einsum("bqhk,bhkv->bqhv", qc * jnp.exp(cum), s_state)
        last = cum[:, -1]
        s_state = s_state * jnp.exp(last)[..., None] + jnp.einsum(
            "bshk,bshv->bhkv", kc * jnp.exp(last[:, None] - cum), vc)
        return s_state, o

    s0 = jnp.zeros((b, h, dk, dv), f32)
    inputs = tuple(to_chunks(t.astype(f32), GLA_CHUNK) for t in (q, k, v, logg))
    _, os_ = lax.scan(step, s0, inputs)
    return from_chunks(os_).astype(v.dtype)

def ssd_gla_mixer(h, w_in, conv_w, conv_b, dt_bias, a_log, d_skip, ssd_norm, gla_w2, gla_b, gla_norm, w_out):
    b, l, _ = h.shape
    proj = h @ w_in
    z, xbc, dt, q, k, v, glr, r = jnp.split(proj, list(np.cumsum(IN_SPLITS)[:-1]), axis=-1)

    xbc = jax.nn.silu(causal_dwconv(xbc, conv_w, conv_b))
    xs, bm, cm = jnp.split(xbc, [SSD_INNER, SSD_INNER + SSD_GROUPS * SSD_STATE], axis=-1)
    xs = xs.reshape(b, l, SSD_HEADS, SSD_HEAD_DIM)
    bm = bm.reshape(b, l, SSD_GROUPS, SSD_STATE)
    cm = cm.reshape(b, l, SSD_GROUPS, SSD_STATE)
    dt = jax.nn.softplus((dt + dt_bias).astype(jnp.float32))
    a = -jnp.exp(a_log.astype(jnp.float32))
    y = ssd_chunked(xs, dt, a, bm, cm) + d_skip[:, None] * xs
    y = y.reshape(b, l, SSD_INNER) * jax.nn.silu(z)
    y = rmsnorm(y.reshape(b, l, SSD_GROUPS, SSD_INNER // SSD_GROUPS),
                ssd_norm.reshape(SSD_GROUPS, SSD_INNER // SSD_GROUPS)).reshape(b, l, SSD_INNER)

    q = q.reshape(b, l, GLA_HEADS, GLA_HK) * (GLA_HK ** -0.5)
    k = k.reshape(b, l, GLA_HEADS, GLA_HK)
    v = v.reshape(b, l, GLA_HEADS, GLA_HV)
    logg = jax.nn.log_sigmoid((glr @ gla_w2 + gla_b).astype(jnp.float32)) / GLA_TAU
    logg = logg.reshape(b, l, GLA_HEADS, GLA_HK)
    o = gla_chunked(q, k, v, logg)
    o = rmsnorm(o, gla_norm).reshape(b, l, GLA_VAL) * jax.nn.silu(r)

    return jnp.concatenate([y, o], axis=-1) @ w_out

def alibi_slopes(n):
    start = 2.0 ** (-8.0 / n)
    return np.array([start ** (i + 1) for i in range(n)], dtype=np.float32)

def diff_attention(h, w_qkv, lam_q1, lam_k1, lam_q2, lam_k2, subln, w_o, lambda_init):
    f32 = jnp.float32
    b, l, _ = h.shape
    qkv = h @ w_qkv
    q, k, v = jnp.split(qkv, [DIFF_QK, 2 * DIFF_QK], axis=-1)
    q = q.reshape(b, l, DIFF_HEADS, 2, DIFF_HEAD_DIM) * (DIFF_HEAD_DIM ** -0.5)
    k = k.reshape(b, l, DIFF_HEADS, 2, DIFF_HEAD_DIM)
    v = v.reshape(b, l, DIFF_HEADS, DIFF_V_DIM)
    lam = (jnp.exp(jnp.sum(lam_q1.astype(f32) * lam_k1.astype(f32)))
           - jnp.exp(jnp.sum(lam_q2.astype(f32) * lam_k2.astype(f32))) + lambda_init)
    slopes = jnp.asarray(alibi_slopes(DIFF_HEADS))[:, None, None]
    nb = l // Q_BLOCK
    qb = jnp.moveaxis(q.reshape(b, nb, Q_BLOCK, DIFF_HEADS, 2, DIFF_HEAD_DIM), 1, 0)
    kpos = jnp.arange(l)

    def block(args):
        qblk, i = args
        qpos = i * Q_BLOCK + jnp.arange(Q_BLOCK)
        dist = (qpos[:, None] - kpos[None, :]).astype(f32)
        bias = jnp.where(dist >= 0, -slopes * dist, -jnp.inf)
        s = jnp.einsum("bqhmd,bkhmd->bhmqk", qblk, k).astype(f32) + bias[None, :, None]
        p = jax.nn.softmax(s, axis=-1)
        attn = p[:, :, 0] - lam * p[:, :, 1]
        return jnp.einsum("bhqk,bkhv->bqhv", attn.astype(v.dtype), v)

    o = from_chunks(lax.map(block, (qb, jnp.arange(nb))))
    o = rmsnorm(o, subln) * (1.0 - lambda_init)
    return o.reshape(b, l, DIFF_HEADS * DIFF_V_DIM) @ w_o

def cross_attention(h, mem_n, wq, wkv, wo):
    b, l, _ = h.shape
    m = mem_n.shape[1]
    q = (h @ wq).reshape(b, l, X_HEADS, X_HEAD_DIM)
    k, v = jnp.split(mem_n @ wkv, 2, axis=-1)
    k = k.reshape(b, m, X_HEADS, X_HEAD_DIM)
    v = v.reshape(b, m, X_HEADS, X_HEAD_DIM)
    s = jnp.einsum("bqhd,bmhd->bhqm", q, k).astype(jnp.float32) * (X_HEAD_DIM ** -0.5)
    p = jax.nn.softmax(s, axis=-1)
    o = jnp.einsum("bhqm,bmhd->bqhd", p.astype(v.dtype), v)
    return o.reshape(b, l, D_MODEL) @ wo

def sq_relu_mlp(h, w1, w2):
    return jnp.square(jax.nn.relu(h @ w1)) @ w2

def setup_inputs(seed: int = 0) -> dict:
    key = jax.random.key(seed)
    ks = iter(jax.random.split(key, 40))

    def nrm(shape, scale):
        return jax.random.normal(next(ks), shape, jnp.float32) * scale

    def gain(shape):
        return 1.0 + nrm(shape, 0.02)

    x = nrm((BATCH, SEQ, D_MODEL), 1.0)
    mem = nrm((BATCH, N_MEM, D_MODEL), 1.0)
    ev_norm = gain((N_EVEN, D_MODEL))
    ev_w_in = nrm((N_EVEN, D_MODEL, IN_WIDTH), D_MODEL ** -0.5)
    ev_conv_w = nrm((N_EVEN, SSD_CONV, SSD_XBC), SSD_CONV ** -0.5)
    ev_conv_b = nrm((N_EVEN, SSD_XBC), 0.01)
    dt0 = jnp.exp(jax.random.uniform(next(ks), (N_EVEN, SSD_HEADS), jnp.float32,
                                     minval=math.log(1e-3), maxval=math.log(1e-1)))
    ev_dt_bias = dt0 + jnp.log(-jnp.expm1(-dt0))
    ev_a_log = jnp.log(jax.random.uniform(next(ks), (N_EVEN, SSD_HEADS), jnp.float32, minval=1.0, maxval=16.0))
    ev_d_skip = gain((N_EVEN, SSD_HEADS))
    ev_ssd_norm = gain((N_EVEN, SSD_INNER))
    ev_gla_w2 = nrm((N_EVEN, GLA_RANK, GLA_KEY), GLA_RANK ** -0.5)
    ev_gla_b = nrm((N_EVEN, GLA_KEY), 0.1)
    ev_gla_norm = gain((N_EVEN, GLA_HV))
    ev_w_out = nrm((N_EVEN, MIX_WIDTH, D_MODEL), MIX_WIDTH ** -0.5)
    od_norm = gain((N_ODD, D_MODEL))
    od_w_qkv = nrm((N_ODD, D_MODEL, DIFF_QKV), D_MODEL ** -0.5)
    od_lam_q1 = nrm((N_ODD, DIFF_HEAD_DIM), 0.1)
    od_lam_k1 = nrm((N_ODD, DIFF_HEAD_DIM), 0.1)
    od_lam_q2 = nrm((N_ODD, DIFF_HEAD_DIM), 0.1)
    od_lam_k2 = nrm((N_ODD, DIFF_HEAD_DIM), 0.1)
    od_subln = gain((N_ODD, DIFF_V_DIM))
    od_w_o = nrm((N_ODD, DIFF_HEADS * DIFF_V_DIM, D_MODEL), (DIFF_HEADS * DIFF_V_DIM) ** -0.5)
    xa_norm = gain((DEPTH, D_MODEL))
    xa_mem_norm = gain((DEPTH, D_MODEL))
    xa_wq = nrm((DEPTH, D_MODEL, D_MODEL), D_MODEL ** -0.5)
    xa_wkv = nrm((DEPTH, D_MODEL, 2 * D_MODEL), D_MODEL ** -0.5)
    xa_wo = nrm((DEPTH, D_MODEL, D_MODEL), D_MODEL ** -0.5)
    mlp_norm = gain((DEPTH, D_MODEL))
    mlp_w1 = nrm((DEPTH, D_MODEL, D_FF), D_MODEL ** -0.5)
    mlp_w2 = nrm((DEPTH, D_FF, D_MODEL), D_FF ** -0.5)
    final_norm = gain((D_MODEL,))
    return {"x": x, "mem": mem,
            "ev_norm": ev_norm, "ev_w_in": ev_w_in, "ev_conv_w": ev_conv_w, "ev_conv_b": ev_conv_b,
            "ev_dt_bias": ev_dt_bias, "ev_a_log": ev_a_log, "ev_d_skip": ev_d_skip, "ev_ssd_norm": ev_ssd_norm,
            "ev_gla_w2": ev_gla_w2, "ev_gla_b": ev_gla_b, "ev_gla_norm": ev_gla_norm, "ev_w_out": ev_w_out,
            "od_norm": od_norm, "od_w_qkv": od_w_qkv, "od_lam_q1": od_lam_q1, "od_lam_k1": od_lam_k1,
            "od_lam_q2": od_lam_q2, "od_lam_k2": od_lam_k2, "od_subln": od_subln, "od_w_o": od_w_o,
            "xa_norm": xa_norm, "xa_mem_norm": xa_mem_norm, "xa_wq": xa_wq, "xa_wkv": xa_wkv, "xa_wo": xa_wo,
            "mlp_norm": mlp_norm, "mlp_w1": mlp_w1, "mlp_w2": mlp_w2, "final_norm": final_norm}

def reference(x, mem, ev_norm, ev_w_in, ev_conv_w, ev_conv_b, ev_dt_bias, ev_a_log, ev_d_skip, ev_ssd_norm,
              ev_gla_w2, ev_gla_b, ev_gla_norm, ev_w_out, od_norm, od_w_qkv, od_lam_q1, od_lam_k1, od_lam_q2,
              od_lam_k2, od_subln, od_w_o, xa_norm, xa_mem_norm, xa_wq, xa_wkv, xa_wo, mlp_norm, mlp_w1,
              mlp_w2, final_norm):
    for layer in range(DEPTH):
        i = layer // 2
        if layer % 2 == 0:
            x = x + ssd_gla_mixer(rmsnorm(x, ev_norm[i]), ev_w_in[i], ev_conv_w[i], ev_conv_b[i],
                                  ev_dt_bias[i], ev_a_log[i], ev_d_skip[i], ev_ssd_norm[i],
                                  ev_gla_w2[i], ev_gla_b[i], ev_gla_norm[i], ev_w_out[i])
        else:
            lambda_init = 0.8 - 0.6 * math.exp(-0.3 * layer)
            x = x + diff_attention(rmsnorm(x, od_norm[i]), od_w_qkv[i], od_lam_q1[i], od_lam_k1[i],
                                   od_lam_q2[i], od_lam_k2[i], od_subln[i], od_w_o[i], lambda_init)
        x = x + cross_attention(rmsnorm(x, xa_norm[layer]), rmsnorm(mem, xa_mem_norm[layer]),
                                xa_wq[layer], xa_wkv[layer], xa_wo[layer])
        x = x + sq_relu_mlp(rmsnorm(x, mlp_norm[layer]), mlp_w1[layer], mlp_w2[layer])
    return rmsnorm(x, final_norm)


_drawn_inputs = setup_inputs


def setup_inputs(seed=0):
    import zlib

    import numpy as np

    out = dict(_drawn_inputs(seed))
    spreads = {}
    factors = {'ev_conv_b': 6.781,
     'ev_d_skip': 6.316,
     'ev_ssd_norm': 4.523,
     'ev_gla_b': 3.475,
     'ev_gla_norm': 7.816,
     'od_norm': 5.709,
     'od_subln': 8.0,
     'xa_norm': 8.0,
     'xa_mem_norm': 8.0,
     'mlp_norm': 2.671,
     'final_norm': 2.799}
    for name, (base, spread) in spreads.items():
        noise = np.random.default_rng([zlib.crc32(name.encode()), seed]).standard_normal(out[name].shape)
        drawn = base * np.exp(spread * noise) if base else spread * noise
        out[name] = __import__('jax').numpy.asarray(drawn.astype(out[name].dtype))
    for name, factor in factors.items():
        out[name] = (out[name] * factor).astype(out[name].dtype)
    return out
```

```python
import math
from contextlib import ExitStack

import concourse.bass as bass
import numpy as np
from concourse import mybir

F32 = mybir.dt.float32
F32R = mybir.dt.float32r
I32 = mybir.dt.int32
ALU = mybir.AluOpType
ACT = mybir.ActivationFunctionType
AX = mybir.AxisListType.X

P = 128
D = 1024
L = 256
NT = L // P
KT = D // P
EPS = 1e-5
FF = 4 * D
PIECES = 4
SH, SP_, SG, SN = 16, 64, 2, 64
XBC = SH * SP_ + 2 * SG * SN
XT = XBC // P
TAPS = 4
GH, GK, GV, RANK, TAU = 4, 128, 256, 16, 16.0
DH, DHD = 8, 64
LAMBDA_INIT = 0.8 - 0.6 * math.exp(-0.3 * 1)
XH, XHD, NM = 4, 256, 256
Z0, XBC0 = 0, 1024
DT0 = XBC0 + XBC
Q0 = DT0 + SH
K0 = Q0 + GH * GK
V0 = K0 + GH * GK
GLR0 = V0 + GH * GV
R0 = GLR0 + RANK

COLS = {}
_n = 0
for _name, _count in [("ev", 8), ("od", 8), ("xa0", 8), ("xa1", 8), ("mem0", 8), ("mem1", 8), ("mlp0", 8),
                      ("mlp1", 8), ("ssdn", 8), ("glan", 2), ("subln", 1), ("convw", TAPS * XT), ("convb", XT)]:
    COLS[_name] = _n
    _n += _count
NCOLS = _n

ROW = {"dtb": 0, "alog": 16, "dskip": 32, "lam": 48}
NROW = 48 + 4 * DHD

C_ID, C_TRI, C_ONE, C_NEG = 0, P, 2 * P, 3 * P
NCONST = 3 * P + 16
LEVELS = [64, 32, 16, 8, 4, 2, 1]

REG = 16672
XB, CV, TT, ZZ, MM, GG, QK, VV = 0, 2592, 5152, 7712, 9760, 11808, 12576, 14624
XBW = L + TAPS - 1
XS, XDT, WX, YC = XB, TT, CV, CV + 1024
CC2, GXA, GXB, STT_, SXT, RR, OO = 0, 2048, 3072, 4096, 5120, 5632, 7680
XN, MEMN = 12576, 9760
DQ, DK, DV, BIAS, SC, AN, AT = 0, 2048, 4096, 6144, 8192, 12288, 13312
CQ, CP, CPT = 0, 2048, 4096


def groups_of(w):
    out = []

    def add(name, mode, weights, columns, rows=(0,), width=512):
        for n, c in enumerate(columns):
            out.append((f"{name}{n}", mode, [(weights, r, c, width) for r in rows]))

    def cross(layer):
        add(f"xk{layer}_", "T", w["xa_wkv"][layer], (0, 512))
        add(f"xv{layer}_", "N", w["xa_wkv"][layer], (1024, 1536))

    def tail(layer):
        add(f"xq{layer}_", "T", w["xa_wq"][layer], (0, 512))
        add(f"xo{layer}_", "N", w["xa_wo"][layer], (0, 512))
        add(f"up{layer}_", "T", w["mlp_w1"][layer], range(0, FF, 512))
        add(f"down{layer}_", "N", w["mlp_w2"][layer], (0, 512), range(0, FF, D))

    w_in, w_out = w["ev_w_in"][0], w["ev_w_out"][0]
    cross(0)
    add("xbc", "T", w_in, (XBC0, XBC0 + 512))
    out.append(("xbc2", "T", [(w_in, 0, XBC0 + 1024, 256)]))
    add("z", "N", w_in, (Z0, Z0 + 512))
    add("q", "T", w_in, (Q0,))
    add("k", "T", w_in, (K0,))
    add("v", "N", w_in, (V0, V0 + 512))
    add("r", "N", w_in, (R0, R0 + 512))
    add("outy", "N", w_out, (0, 512))
    add("outo", "N", w_out, (0, 512), (1024,))
    tail(0)
    w_qkv = w["od_w_qkv"][0]
    add("dq", "T", w_qkv, (0, 512))
    add("dk", "T", w_qkv, (1024, 1536))
    add("dv", "N", w_qkv, (2048, 2560))
    cross(1)
    add("dout", "N", w["od_w_o"][0], (0, 512))
    tail(1)
    return out


def trunk(nc, w):
    groups = groups_of(w)
    number = {g[0]: n for n, g in enumerate(groups)}
    chunks = [c for g in groups for c in g[2]]
    first_chunk = []
    for g in groups:
        first_chunk.append(first_chunk[-1] + len(groups[len(first_chunk) - 1][2]) if first_chunk else 0)

    ctx = ExitStack()
    with ctx:
        def sb(name, shape, dt=F32):
            return ctx.enter_context(nc.sbuf_tensor(name, shape, dt))

        norms = ["mem", "n0", "y", "o", "xn0", "mn0", "n1", "do", "xn1", "mn1", "fin"]
        shared = {
            "squares": [(k + "_sq", {"y": 4, "o": 8, "do": 4}.get(k, 2)) for k in norms],
            "rstd": [(k + "_rstd", 1) for k in norms],
            "normed": [(k + "_xn", 2) for k in ("mem", "n0", "xn0", "mn0", "n1", "xn1", "mn1")],
            "turned": [(k + "_T", 4) for k in ("mem", "n0", "y", "o", "xn0", "c0", "mn0", "n1", "d", "xn1", "c1", "mn1")],
            "act_hi": [(k + "_hi", 4 if k[0] == "c" else 8) for k in
                       ("mg0", "n0", "y", "o", "xn0", "c0", "mn0", "n1", "mg1", "d", "xn1", "c1", "mn1")],
            "act_lo": [(k + "_lo", 4 if k[0] == "c" else 8) for k in
                       ("mg0", "n0", "y", "o", "xn0", "c0", "mn0", "n1", "mg1", "d", "xn1", "c1", "mn1")],
            "cross_score": [("c0_score", 4), ("c1_score", 4)],
            "cross_exp": [("c0_exp", 8), ("c1_exp", 8)],
            "cross_max": [("c0_max", 4), ("c1_max", 4)],
            "cross_p": [("c0_p", 8), ("c1_p", 8)],
            "cross_pT": [("c0_pT", 4), ("c1_pT", 4)],
            "cross_pt": [("c0_pt", 4), ("c1_pt", 4)],
            "hid_lo_ready": [("hid0", 16), ("hid1", 16)],
        }
        stage = {}
        for family, parts_ in shared.items():
            base = 0
            for name_, steps in parts_:
                stage[name_] = (family, base)
                base += steps
        sems = {}

        def sem(name):
            if name not in sems:
                sems[name] = ctx.enter_context(nc.semaphore(name))
            return sems[name]

        def after(name, n):
            family, base = stage.get(name, (name, 0))
            return sem(family), base + n

        with nc.sbuf_tensor("region", [P, REG], F32) as region:
            pass
        with nc.sbuf_tensor("hid_hi", [P, FF // P, L], F32R) as hid_hi, \
                nc.sbuf_tensor("hid_lo", [P, FF // P, L], F32R) as hid_lo:
            pass
        keep = sb("keep_region", [P, REG])
        raw = sb("raw", [P, PIECES, 2, 512])
        w_hi = sb("w_hi", [P, PIECES, 2, 512], F32R)
        w_lo = sb("w_lo", [P, PIECES, 2, 512], F32R)
        x = sb("x", [P, NT, D])
        a_hi, a_lo = sb("a_hi", [P, KT, L], F32R), sb("a_lo", [P, KT, L], F32R)
        b_hi, b_lo = sb("b_hi", [P, KT, L], F32R), sb("b_lo", [P, KT, L], F32R)
        mem_t = sb("mem_t", [P, KT, NM])
        xk = sb("xk", [P, KT, NM])
        xv = sb("xv", [P, NM // P, D])
        junk = sb("junk", [P, 2, 512])
        sp = sb("sp", [P, NT, 512])
        const = sb("const", [P, NCONST])
        mask = sb("mask", [P, len(LEVELS), P], I32)
        prow = sb("prow", [NCOLS, P])
        cols = sb("cols", [P, NCOLS])
        half = sb("half", [P, (TAPS + 1) * XT])
        row = sb("row", [P, NROW])
        sw = sb("sw", [P, KT, 32])
        sw_hi, sw_lo = sb("sw_hi", [P, KT, 32], F32R), sb("sw_lo", [P, KT, 32], F32R)
        w2g = sb("w2g", [RANK + 1, 512])
        glr_t = sb("glr_t", [RANK + 1, L])
        dgs = sb("dgs", [P, NT, 32])
        small = sb("small", [P, 832])
        L_ = [ctx.enter_context(nc.psum_tensor(f"lin{n}", [P, 512], F32)) for n in range(4)]
        X_ = [ctx.enter_context(nc.psum_tensor(f"mix{n}", [P, 512], F32)) for n in range(4)]

        def R(off, *dims):
            return bass.AP(tensor=region, offset=off, ap=[[REG, P], *[list(d) for d in dims]])

        small_at = {}

        def sm(name, n):
            if name not in small_at:
                small_at[name] = (sum(v[1] for v in small_at.values()), n)
            at, n = small_at[name]
            return small[:, at:at + n]

        ident, tri, ones = const[:, C_ID:C_ID + P], const[:, C_TRI:C_TRI + P], const[:, C_ONE:C_ONE + P]
        neghalf = const[:, C_NEG:C_NEG + 16]

        def col(name, k=0):
            return cols[:, COLS[name] + k:COLS[name] + k + 1]

        last_piece = {first_chunk[g] + len(grp[2]) - 1: g for g, grp in enumerate(groups)}

        def piece_free(eng, c, j):
            before = sum(1 for q in last_piece if q < c)
            if j == PIECES - 1 and c in last_piece:
                eng.wait_ge(*after("group_done", last_piece[c] + 1))
            else:
                eng.wait_ge(*after("mm_done", PIECES * c + j + 1 - before))

        def bank_view(g, b, dst):
            bank = banks_of(g)[b][:, :]
            return bank if len(dst.shape) == 2 else bank.rearrange("p (a b) -> p a b", a=2)

        def banks_of(g):
            return L_[2 * (g % 2)], L_[2 * (g % 2) + 1]

        def evac(g, b):
            return sem(f"evac{g % 2}{b}"), g // 2 + 1

        def tracker(eng, own):
            tally, last = {}, []

            def op(ins, name=None, value=None):
                name = name or own
                tally[name] = tally.get(name, 0) + 1
                s, v = after(name, value or tally[name])
                ins.then_inc(s, 1)
                last[:] = [s, v]
                return ins

            def settle():
                eng.wait_ge(last[0], last[1])

            def link(ins, name=None):
                op(ins, name)
                settle()

            return op, settle, link

        block = ctx.enter_context(nc.Block())

        @block.sync
        def _(e):
            def load(dst, src, name):
                e.dma_start(dst, src).then_inc(sem(name), 16)

            load(R(MEMN, (D, NT), (1, D)), w["mem"][0].rearrange("(t p) d -> p t d", p=P), "mem_loaded")
            load(x[:], w["x"][0].rearrange("(t p) d -> p t d", p=P), "x_loaded")
            load(const[:], w["const"], "const_loaded")
            load(prow[:], w["prow"], "prow_loaded")
            load(row[:], w["row"].to_broadcast([P, NROW]), "row_loaded")
            load(sw[:], w["w_small"].rearrange("(k p) n -> p k n", p=P), "sw_loaded")
            load(w2g[:], w["gla_w2b"], "w2g_loaded")
            load(mask[:], w["mask"], "mask_loaded")
            for c, (wt, r0, c0, width) in enumerate(chunks):
                for j in range(PIECES):
                    if c > 0:
                        e.wait_ge(*after("hi_ready", 4 * (c - 1) + j + 1))
                        e.wait_ge(*after("lo_dve" if j % 2 == 0 else "lo_pool", 2 * (c - 1) + j // 2 + 1))
                    src = wt[r0 + 256 * j:r0 + 256 * (j + 1), c0:c0 + width].rearrange("(k p) n -> p k n", p=P)
                    e.dma_start(raw[:, j, :, 0:width], src).then_inc(sem(f"raw_ready{j}"), 16)
                if c == first_chunk[number["dq0"]] + 1:
                    e.wait_ge(*after("group_done", number["down0_1"] + 1))
                    load(R(BIAS, (1, 2048)), w["bias"], "bias_loaded")
                if c == first_chunk[number["up1_2"]]:
                    e.wait_ge(*after("c1_score", 4))
                    load(xk[:, 0:4, :], w["fnorm"].to_broadcast([P, D]).rearrange("p (a b) -> p a b", a=4), "fnorm_loaded")
            for t in range(NT):
                e.wait_ge(*after("final", t + 1))
                e.dma_start(w["out"][0, t * P:(t + 1) * P, :], R(XN + t * D, (1, D))).then_inc(sem("stored"), 16)
            e.wait_ge(*after("stored", 16 * NT))

        @block.tensor
        def _(e):
            freed = [None] * 4

            def take(b):
                if freed[b]:
                    e.wait_ge(*after(freed[b][0], freed[b][1]))
                return X_[b]

            def product(name, act, ready, per=2):
                g = number[name]
                _, mode, parts = groups[g]
                bank = banks_of(g)
                hi, lo = act
                if g >= 2:
                    for b in range(2):
                        s, v = evac(g - 2, b)
                        e.wait_ge(s, v)
                for n, (_, _, _, width) in enumerate(parts):
                    c = first_chunk[g] + n
                    for j in range(PIECES):
                        e.wait_ge(*after(ready, per * (PIECES * n + j + 1)))
                        e.wait_ge(*after("hi_ready", 4 * c + j + 1))
                        e.wait_ge(*after("lo_dve" if j % 2 == 0 else "lo_pool", 2 * c + j // 2 + 1))
                        begin, end = n == 0 and j == 0, n == len(parts) - 1 and j == PIECES - 1
                        if mode == "T":
                            for f in range(width // P):
                                out = bank[f // 2][:, (f % 2) * L:(f % 2 + 1) * L]
                                for kk in range(2):
                                    k = 2 * j + kk
                                    wh, wl = (t[:, j, kk, f * P:(f + 1) * P] for t in (w_hi, w_lo))
                                    e.matmul(out, wh, hi[:, k, :], start=begin and kk == 0 and f % 2 == 0,
                                             stop=False, skip_group_check=True)
                                    e.matmul(out, wh, lo[:, k, :], start=False, stop=False, skip_group_check=True)
                                    m = e.matmul(out, wl, hi[:, k, :], start=False, stop=end and kk == 1,
                                                 skip_group_check=True)
                        else:
                            for kk in range(2):
                                k = KT * n + 2 * j + kk
                                for t in range(NT):
                                    ah, al = (a[:, k, t * P:(t + 1) * P] for a in (hi, lo))
                                    out = bank[t][:, :]
                                    e.matmul(out, ah, w_hi[:, j, kk, :], start=begin and kk == 0, stop=False)
                                    e.matmul(out, ah, w_lo[:, j, kk, :], start=False, stop=False)
                                    m = e.matmul(out, al, w_hi[:, j, kk, :], start=False, stop=end and kk == 1)
                        if end:
                            m.then_inc(after("group_done", 0)[0], 1)
                        else:
                            m.then_inc(after("mm_done", 0)[0], 1)

            def turn(key, src, done=None):
                for b in range(4):
                    bank = take(b)
                    for kk in range(2):
                        for t in range(NT):
                            at = (kk * NT + t) * P
                            m = e.transpose(bank[:, at:at + P], src(t, 2 * b + kk), ident)
                    m.then_inc(after(key + "_T", 0)[0], 1)
                    freed[b] = (done or key + "_lo", b + 1 if done else 2 * (b + 1))

            A, B = (a_hi, a_lo), (b_hi, b_lo)

            e.wait_ge(*after("const_loaded", 16))
            e.wait_ge(*after("prow_loaded", 16))
            e.transpose(take(0)[:, 0:NCOLS], prow[:], const[0:NCOLS, 0:NCOLS]).then_inc(after("cols_T", 0)[0], 1)
            freed[0] = ("cols_ready", 1)
            e.wait_ge(*after("mem_xn", 2))
            turn("mem", lambda t, k: R(MEMN + t * D + k * P, (1, P)), "mem_copy")
            e.wait_ge(*after("n0_xn", 2))
            turn("n0", lambda t, k: R(XN + t * D + k * P, (1, P)))

            for n in ("xk0_0", "xk0_1", "xv0_0", "xv0_1"):
                product(n, B, "mg0_lo")

            e.wait_ge(*after("n0_lo", 8))
            e.wait_ge(*after("sw_lo", 1))
            bank = take(0)
            for t in range(NT):
                for k in range(KT):
                    ah, al = (a[:, k, t * P:(t + 1) * P] for a in A)
                    out = bank[:, t * 32:(t + 1) * 32]
                    e.matmul(out, ah, sw_hi[:, k, :], start=k == 0, stop=False)
                    e.matmul(out, ah, sw_lo[:, k, :], start=False, stop=False)
                    m = e.matmul(out, al, sw_hi[:, k, :], start=False, stop=k == KT - 1)
            m.then_inc(after("dg_mm", 0)[0], 1)
            freed[0] = ("dg_copy", 1)
            product("xbc0", A, "n0_lo")
            e.wait_ge(*after("dg_copy", 1))
            bank = take(1)
            for t in range(NT):
                m = e.transpose(bank[0:RANK, t * P:(t + 1) * P], dgs[:, t, 16:32], ident)
            m.then_inc(after("glr_T", 0)[0], 1)
            freed[1] = ("glrt_ready", 1)
            product("xbc1", A, "n0_lo")
            e.wait_ge(*after("glrt_ready", 1))
            e.wait_ge(*after("w2g_loaded", 16))
            for t in range(NT):
                e.matmul(take(2 + t)[:, :], glr_t[:, t * P:(t + 1) * P], w2g[:], start=True,
                         stop=True).then_inc(after("g_mm", 0)[0], 1)
                freed[2 + t] = ("g_max", t + 1)
            product("xbc2", A, "n0_lo")
            product("z0", A, "n0_lo")
            product("z1", A, "n0_lo")

            e.wait_ge(*after("conv_silu", 1))
            for b in range(4):
                bank = take(b)
                t, hh = b // 2, b % 2
                for i in range(4):
                    m = e.transpose(bank[:, i * P:(i + 1) * P], R(CV + (4 * hh + i) * L + t * P, (1, P)), ident)
                m.then_inc(after("xs_T", 0)[0], 1)
                freed[b] = ("xs_ready", b + 1)
            for g in range(SG):
                bank = take(g)
                lo_, hi_ = g * SN, (g + 1) * SN
                bt, ct = R(CV + 8 * L, (1, L)), R(CV + 9 * L, (1, L))
                e.matmul(bank[:, 0:L], bt[lo_:hi_, 0:P], ct[lo_:hi_, :], start=True, stop=True)
                e.matmul(bank[:, L:L + P], bt[lo_:hi_, P:L], ct[lo_:hi_, P:L], start=True,
                         stop=True).then_inc(after("ssd_score", 0)[0], 1)
                freed[g] = ("ssd_g", 3 * (g + 1))
            e.wait_ge(*after("loga", 1))
            la = sm("loga", 32)
            bank = take(2)
            for t in range(NT):
                e.matmul(bank[:, t * SH:(t + 1) * SH], tri, la[:, t * SH:(t + 1) * SH], start=True, stop=True)
            e.matmul(bank[:, 2 * SH:3 * SH], ones, la[:, 0:SH], start=True, stop=True).then_inc(after("cum_mm", 0)[0], 1)
            freed[2] = ("cum_ready", 1)

            def decay_rows(t):
                for b in range(4):
                    bank = take(b)
                    for i in range(4):
                        h = 4 * b + i
                        m = e.matmul(bank[:, i * P:(i + 1) * P],
                                     la[:, t * SH + h:t * SH + h + 1].to_broadcast([P, P]), tri, start=True, stop=True)
                    m.then_inc(after("cumb_mm", 0)[0], 1)
                    freed[b] = ("seg", 4 * t + b + 1)

            def ssd_y(t):
                e.wait_ge(*after("ssd_m", 2 * (t + 1)))
                for b in range(2):
                    bank = take(2 * t + b)
                    for i in range(8):
                        h = 8 * b + i
                        m = e.matmul(bank[:, i * SP_:(i + 1) * SP_], R(MM + h * P, (1, P)),
                                     R(XDT + t * D + h * SP_, (1, SP_)), start=True, stop=True)
                    m.then_inc(after("y_mm", 0)[0], 1)
                    freed[2 * t + b] = ("y_add", 2 * t + b + 1)

            decay_rows(0)
            product("q0", A, "n0_lo")
            e.wait_ge(*after("xdt", 2))
            ssd_y(0)
            decay_rows(1)
            product("k0", A, "n0_lo")
            ssd_y(1)
            e.wait_ge(*after("wx", 1))
            for g in range(SG):
                e.matmul(take(g)[:, :], R(GG + g * 384 + P, (1, P)), R(WX + g * 512, (1, 512)), start=True,
                         stop=True).then_inc(after("yc_mm", 0)[0], 1)
                freed[g] = ("yc_scaled", g + 1)
            product("v0", A, "n0_lo")
            product("v1", A, "n0_lo")
            e.wait_ge(*after("yn", 4))
            turn("y", lambda t, k: R(XS + t * D + k * P, (1, P)))
            product("r0", A, "n0_lo")

            e.wait_ge(*after("sp_ready", 2))
            for b in range(2):
                bank = take(b)
                for i in range(2):
                    h = 2 * b + i
                    for t in range(NT):
                        at = (i * NT + t) * P
                        m = e.matmul(bank[:, at:at + P], sp[:, t, h * GK:(h + 1) * GK], tri, start=True, stop=True)
                m.then_inc(after("gcum_mm", 0)[0], 1)
                freed[b] = ("gcum", b + 1)
            e.wait_ge(evac(number["q0"], 0)[0], evac(number["q0"], 0)[1])
            e.wait_ge(evac(number["q0"], 1)[0], evac(number["q0"], 1)[1])
            e.wait_ge(evac(number["k0"], 0)[0], evac(number["k0"], 0)[1])
            e.wait_ge(evac(number["k0"], 1)[0], evac(number["k0"], 1)[1])
            for t in range(NT):
                bank = take(2 + t)
                for h in range(GH):
                    at = h * L + t * P
                    m = e.matmul(bank[:, h * P:(h + 1) * P], R(QK + at, (1, P)), R(QK + 1024 + at, (1, P)),
                                 start=True, stop=True)
                m.then_inc(after("diag_mm", 0)[0], 1)
                freed[2 + t] = ("gla_diag", t + 1)
            product("r1", A, "n0_lo")

            def gla_level(n):
                buf = GXA if n % 2 == 0 else GXB
                e.wait_ge(*after("gx", n + 1))
                if n == 0:
                    bank = take(0)
                    for h in range(GH):
                        m = e.matmul(bank[:, h * P:(h + 1) * P], R(buf + h * L, (1, P)), R(buf + h * L + P, (1, P)),
                                     start=True, stop=True)
                    m.then_inc(after("level_mm", 0)[0], 1)
                    freed[0] = ("gla_cross", 1)
                    return
                for t in range(NT):
                    b = 2 * (n % 2) + t
                    bank = take(b)
                    for h in range(GH):
                        xx = R(buf + h * L + t * P, (1, P))
                        m = e.matmul(bank[:, h * P:(h + 1) * P], xx, xx, start=True, stop=True)
                    m.then_inc(after("level_mm", 0)[0], 1)
                    freed[b] = ("gla_s", 2 * (n - 1) + t + 1)

            for n in range(0, 4):
                gla_level(n)
            product("outy0", B, "y_lo")
            for n in range(4, 8):
                gla_level(n)
            product("outy1", B, "y_lo")
            for n in ("v0", "v1"):
                for b in range(2):
                    e.wait_ge(*evac(number[n], b))
            e.wait_ge(*after("gla_s", 14))
            for t in range(NT):
                for b in range(2):
                    bank = take(2 * t + b)
                    for i in range(2):
                        h = 2 * b + i
                        out = bank[:, i * GV:(i + 1) * GV]
                        m = e.matmul(out, R(STT_ + t * 512 + h * P, (1, P)), R(VV + t * D + h * GV, (1, GV)),
                                     start=True, stop=t == 0)
                        if t == 1:
                            m = e.matmul(out, R(SXT + h * P, (1, P)), R(VV + h * GV, (1, GV)), start=False, stop=True)
                    m.then_inc(after("o_mm", 0)[0], 1)
                    freed[2 * t + b] = ("on", 2 * (2 * t + b + 1))
            e.wait_ge(*after("on", 8))
            turn("o", lambda t, k: R(OO + t * D + k * P, (1, P)))
            product("outo0", A, "o_lo")
            product("outo1", A, "o_lo")

            def attend(l, act):
                product(f"xq{l}_0", act, f"xn{l}_lo")
                product(f"xq{l}_1", act, f"xn{l}_lo")
                for n in (f"xq{l}_0", f"xq{l}_1"):
                    for b in range(2):
                        e.wait_ge(*evac(number[n], b))
                for b in range(4):
                    t, hh = b // 2, b % 2
                    bank = take(b)
                    for i in range(2):
                        h = 2 * hh + i
                        for dd in range(2):
                            m = e.matmul(bank[:, i * NM:(i + 1) * NM], R(CQ + (2 * h + dd) * L + t * P, (1, P)),
                                         xk[:, 2 * h + dd, :], start=dd == 0, stop=dd == 1)
                    m.then_inc(after(f"c{l}_score", 0)[0], 1)
                    freed[b] = (f"c{l}_exp", 2 * (b + 1))
                e.wait_ge(*after(f"c{l}_p", 8))
                for b in range(4):
                    mt, hh = b // 2, b % 2
                    bank = take(b)
                    for i in range(2):
                        h = 2 * hh + i
                        for t in range(NT):
                            at = (i * NT + t) * P
                            m = e.transpose(bank[:, at:at + P], R(CP + (t * XH + h) * NM + mt * P, (1, P)), ident)
                    m.then_inc(after(f"c{l}_pT", 0)[0], 1)
                    freed[b] = (f"c{l}_pt", b + 1)
                e.wait_ge(*after(f"c{l}_pt", 4))
                for h in range(XH):
                    bank = take(h)
                    for vv in range(2):
                        for mt in range(2):
                            m = e.matmul(bank[:, vv * L:(vv + 1) * L], xv[:, mt, h * XHD + vv * P:h * XHD + (vv + 1) * P],
                                         R(CPT + (mt * XH + h) * L, (1, L)), start=mt == 0, stop=mt == 1)
                    m.then_inc(after(f"c{l}_T", 0)[0], 1)
                    freed[h] = (f"c{l}_lo", h + 1)

            def tail(l, one, two):
                e.wait_ge(*after(f"xn{l}_xn", 2))
                turn(f"xn{l}", lambda t, k: R(XN + t * D + k * P, (1, P)))
                attend(l, one)
                product(f"xo{l}_0", two, f"c{l}_lo", 1)
                product(f"xo{l}_1", two, f"c{l}_lo", 1)
                e.wait_ge(*after(f"mn{l}_xn", 2))
                turn(f"mn{l}", lambda t, k: R(XN + t * D + k * P, (1, P)))
                for n in range(8):
                    product(f"up{l}_{n}", one, f"mn{l}_lo")
                for n in range(2):
                    product(f"down{l}_{n}", (hid_hi, hid_lo), f"hid{l}", 1)

            tail(0, B, A)

            e.wait_ge(*after("n1_xn", 2))
            turn("n1", lambda t, k: R(XN + t * D + k * P, (1, P)))
            for n in ("dq0", "dq1", "dk0", "dk1"):
                product(n, A, "n1_lo")
            for n in ("dq0", "dq1", "dk0", "dk1"):
                for b in range(2):
                    e.wait_ge(*evac(number[n], b))

            def diff_scores(r):
                t, per = (0, 4) if r == 0 else (1, 2)
                keys = (t + 1) * P
                for b in range(4):
                    pair, m_ = b // 2, b % 2
                    bank = take(b)
                    for i in range(per):
                        h = per * pair + i + (4 if r == 2 else 0)
                        q = R(DQ + h * L + t * P, (1, P))[m_ * DHD:(m_ + 1) * DHD, :]
                        k = R(DK + h * L, (1, keys))[m_ * DHD:(m_ + 1) * DHD, :]
                        m = e.matmul(bank[:, i * keys:(i + 1) * keys], q, k, start=True, stop=True)
                    m.then_inc(after("d_score", 0)[0], 1)
                    freed[b] = ("d_bias", 4 * r + b + 1)

            def diff_turn(r):
                e.wait_ge(*after("d_an", (8, 12, 16)[r]))
                for b in range(2):
                    bank = take(b)
                    for i in range(4):
                        n = 4 * b + i
                        m = e.transpose(bank[:, i * P:(i + 1) * P], R(AN + n * P, (1, P)), ident)
                    m.then_inc(after("d_anT", 0)[0], 1)
                    freed[b] = ("d_at", 2 * r + b + 1)

            diff_scores(0)
            product("dv0", A, "n1_lo")
            diff_turn(0)
            diff_scores(1)
            product("dv1", A, "n1_lo")
            diff_turn(1)
            diff_scores(2)
            for n in ("xk1_0", "xk1_1"):
                product(n, B, "mg1_lo")
            diff_turn(2)
            product("xv1_0", B, "mg1_lo")
            product("xv1_1", B, "mg1_lo")
            for n in ("dv0", "dv1"):
                for b in range(2):
                    e.wait_ge(*evac(number[n], b))
            e.wait_ge(*after("d_at", 6))
            for t in range(NT):
                for b in range(2):
                    bank = take(2 * t + b)
                    for i in range(4):
                        h = 4 * b + i
                        for s in range(t + 1):
                            slot = h if t == 0 else 8 + 2 * h + s
                            m = e.matmul(bank[:, i * P:(i + 1) * P], R(AT + slot * P, (1, P)),
                                         R(DV + s * D + h * P, (1, P)), start=s == 0, stop=s == t)
                    m.then_inc(after("do_mm", 0)[0], 1)
                    freed[2 * t + b] = ("d_on", 2 * t + b + 1)
            e.wait_ge(*after("d_on", 4))
            turn("d", lambda t, k: R(SC + t * D + k * P, (1, P)))
            product("dout0", B, "d_lo")
            product("dout1", B, "d_lo")
            tail(1, A, B)

        @block.scalar
        def _(e):
            op, settle, link = tracker(e, "act_step")

            def split(c):
                if c >= len(chunks):
                    return
                width = chunks[c][3]
                for j in range(PIECES):
                    e.wait_ge(*after(f"raw_ready{j}", 16 * (c + 1)))
                    if c > 0:
                        piece_free(e, c - 1, j)
                    op(e.activation(w_hi[:, j, :, 0:width], raw[:, j, :, 0:width], ACT.Copy), "hi_ready")

            def done(g):
                e.wait_ge(*after("group_done", g + 1))

            def ahead(name):
                g = number[name]
                for c in range(first_chunk[g], first_chunk[g] + len(groups[g][2])):
                    split(c + 1)
                return g

            def copy0(name, dst, scale=1.0):
                g = ahead(name)
                done(g)
                s, v = evac(g, 0)
                op(e.activation(dst, bank_view(g, 0, dst), ACT.Copy, scale=scale), s.name, v)

            def added(name):
                ahead(name)

            def sumsq(key, srcs, wait, width):
                ss = sm(key + "_ss", len(srcs))
                for n, (src, ready) in enumerate(srcs):
                    if ready:
                        e.wait_ge(*ready)
                    link(e.activation(junk[:].rearrange("p a b -> p (a b)")[:, 0:width], src, ACT.Square,
                                      accum_out=ss[:, n:n + 1]), key + "_sq")

            def hi_parts(key, act, gain, gains=KT):
                for b in range(4):
                    e.wait_ge(*after(key + "_T", b + 1))
                    for kk in range(2):
                        k = 2 * b + kk
                        op(e.activation(act[:, k, :], X_[b][:, kk * L:(kk + 1) * L], ACT.Copy, scale=gain(k)),
                           key + "_hi")

            split(0)
            sumsq("mem", [(R(MEMN + t * D, (1, D)), (sem("mem_loaded"), 16)) for t in range(NT)], None, D)
            sumsq("n0", [(x[:, t, :], (sem("x_loaded"), 16)) for t in range(NT)], None, D)
            e.wait_ge(*after("cols_T", 1))
            link(e.activation(cols[:], X_[0][:, 0:NCOLS], ACT.Copy), "cols_ready")
            e.wait_ge(*after("sw_loaded", 16))
            op(e.activation(sw_hi[:], sw[:], ACT.Copy), "sw_hi")
            for k in range(KT):
                e.wait_ge(*after("mem_copy", k // 2 + 1))
                op(e.activation(b_hi[:, k, :], mem_t[:, k, :], ACT.Copy, scale=col("mem0", k)), "mg0_hi")
            hi_parts("n0", a_hi, lambda k: col("ev", k))
            e.wait_ge(*after("row_loaded", 16))
            op(e.activation(sm("ea", 16), row[:, 16:32], ACT.Exp), "ea")
            copy0("xk0_0", xk[:, 0:2, :])
            copy0("xk0_1", xk[:, 4:6, :])
            copy0("xv0_0", xv[:, 0, 0:512])
            copy0("xv0_1", xv[:, 0, 512:1024])
            e.wait_ge(*after("dg_mm", 1))
            link(e.activation(dgs[:].rearrange("p a b -> p (a b)"), X_[0][:, 0:64], ACT.Copy), "dg_copy")
            e.wait_ge(*after("ones_ready", 1))
            e.wait_ge(*after("pad_ready", 1))
            copy0("xbc0", R(XB + 3, (XBW, 2), (1, L)))
            e.wait_ge(*after("glr_T", 1))
            op(e.activation(glr_t[0:RANK, :], X_[1][0:RANK, 0:L], ACT.Copy), "glrt_ready")
            e.wait_ge(*after("dt_na", 1))
            op(e.activation(sm("dt_u", 32), sm("dt_n", 32), ACT.Exp), "dt_u")
            copy0("xbc1", R(XB + 4 * XBW + 3, (XBW, 2), (1, L)))
            for t in range(NT):
                e.wait_ge(*after("g_mm", t + 1))
                link(e.activation(junk[:, t, :], X_[2 + t][:, :], ACT.Abs), "g_abs")
            link(e.activation(junk[:], junk[:], ACT.Exp, scale=-1.0))
            op(e.activation(junk[:], junk[:], ACT.Ln, bias=1.0), "g_ln")
            copy0("xbc2", R(XB + 8 * XBW + 3, (XBW, 2), (1, L)))
            for n in range(2):
                g = ahead(f"z{n}")
                done(g)
                for t in range(NT):
                    op(e.activation(R(ZZ + t * D + n * 512, (1, 512)), banks_of(g)[t][:, :], ACT.Tanh, scale=0.5),
                       "z_tanh")
            e.wait_ge(*after("conv", 10))
            op(e.activation(R(TT, (1, XT * L)), R(CV, (1, XT * L)), ACT.Tanh), "conv_tanh")
            for b in range(4):
                e.wait_ge(*after("xs_T", b + 1))
                op(e.activation(R(XS + b * 512, (1, 512)), X_[b][:, :], ACT.Copy), "xs_ready")
            e.wait_ge(*after("cum_ready", 2))
            op(e.activation(sm("wts", 16), sm("wts", 16), ACT.Exp), "wts")
            op(e.activation(sm("e1", 16), sm("cc", 48)[:, 16:32], ACT.Exp), "e1")
            e.wait_ge(*after("seg_min", 1))
            link(e.activation(R(MM, (1, 2048)), R(MM, (1, 2048)), ACT.Exp), "ssd_exp")
            copy0("q0", R(QK + 1024, (L, 2), (1, L)), GK ** -0.5)
            e.wait_ge(*after("seg_min", 2))
            link(e.activation(R(MM, (1, 2048)), R(MM, (1, 2048)), ACT.Exp), "ssd_exp")
            copy0("k0", R(QK, (L, 2), (1, L)))
            copy0("v0", R(VV, (1, 512)))
            copy0("v1", R(VV + 512, (1, 512)))
            e.wait_ge(*after("yz", 2))
            sumsq("y", [(R(XS + t * D + g * 512, (1, 512)), None) for t in range(NT) for g in range(SG)], None, 512)
            hi_parts("y", b_hi, lambda k: col("ssdn", k))

            def r_tanh(n):
                g = ahead(f"r{n}")
                done(g)
                for t in range(NT):
                    op(e.activation(R(RR + t * D + n * 512, (1, 512)), banks_of(g)[t][:, :], ACT.Tanh, scale=0.5),
                       "r_tanh")

            r_tanh(0)
            e.wait_ge(*after("gcum", 2))
            op(e.activation(R(CC2, (1, 1024)), R(CC2 + 1024, (1, 1024)), ACT.Copy, scale=-1.0), "gneg")
            r_tanh(1)

            def gla_exp(n):
                buf = GXA if n % 2 == 0 else GXB
                e.wait_ge(*after("gd", n + 1))
                if n == 0:
                    op(e.activation(R(buf + P, (L, GH), (1, P)), R(CC2 + 1024 + P, (L, GH), (1, P)), ACT.Exp))
                    link(e.activation(R(buf, (L, GH), (1, P)), R(buf, (L, GH), (1, P)), ACT.Exp), "ge")
                else:
                    link(e.activation(R(buf, (1, 1024)), R(buf, (1, 1024)), ACT.Exp), "ge")

            for n in range(4):
                gla_exp(n)
            added("outy0")
            for n in range(4, 8):
                gla_exp(n)
            added("outy1")
            ss = sm("o_ss", 8)
            for b in range(4):
                e.wait_ge(*after("o_mm", b + 1))
                for i in range(2):
                    link(e.activation(junk[:, 0, 0:GV], X_[b][:, i * GV:(i + 1) * GV], ACT.Square,
                                      accum_out=ss[:, 2 * b + i:2 * b + i + 1]), "o_sq")
            hi_parts("o", a_hi, lambda k: col("glan", k % 2))
            added("outo0")
            added("outo1")

            def tail(l, one, two):
                last = number["outo1"] if l == 0 else number["dout1"]
                s, v = evac(last, 1)
                sumsq(f"xn{l}", [(x[:, 0, :], evac(last, 0)), (x[:, 1, :], (s, v))], None, D)
                hi_parts(f"xn{l}", one[0], lambda k: col(f"xa{l}", k))
                for n in range(2):
                    copy0(f"xq{l}_{n}", R(CQ + 4 * n * L, (L, 2), (1, L)))
                rs = sm(f"c{l}_sum", 8)
                for b in range(4):
                    e.wait_ge(*after(f"c{l}_max", b + 1))
                    for i in range(2):
                        n = 2 * b + i
                        op(e.activation(R(CP + n * NM, (1, NM)), X_[b][:, i * NM:(i + 1) * NM], ACT.Exp,
                                        bias=sm(f"c{l}_nmax", 8)[:, n:n + 1], scale=XHD ** -0.5,
                                        accum_out=rs[:, n:n + 1]), f"c{l}_exp")
                for b in range(4):
                    e.wait_ge(*after(f"c{l}_pT", b + 1))
                    op(e.activation(R(CPT + b * 512, (1, 512)), X_[b][:, :], ACT.Copy), f"c{l}_pt")
                for h in range(XH):
                    e.wait_ge(*after(f"c{l}_T", h + 1))
                    op(e.activation(two[0][:, 2 * h:2 * h + 2, :], X_[h][:, :].rearrange("p (a b) -> p a b", a=2),
                                    ACT.Copy), f"c{l}_hi")
                added(f"xo{l}_0")
                added(f"xo{l}_1")
                last = number[f"xo{l}_1"]
                sumsq(f"mn{l}", [(x[:, t, :], evac(last, t)) for t in range(NT)], None, D)
                hi_parts(f"mn{l}", one[0], lambda k: col(f"mlp{l}", k))
                for n in range(8):
                    g = ahead(f"up{l}_{n}")
                    done(g)
                    for b in range(2):
                        if n > 0:
                            e.wait_ge(*after("hid_sq", 16 * l + 2 * n + b - 1))
                        s, v = evac(g, b)
                        op(e.activation(junk[:, b, :], banks_of(g)[b][:, :], ACT.Relu), s.name, v)
                    for b in range(2):
                        e.wait_ge(*after("hid_sq", 16 * l + 2 * n + b + 1))
                        op(e.activation(hid_hi[:, 4 * n + 2 * b:4 * n + 2 * b + 2, :],
                                        sp[:, b, :].rearrange("p (a c) -> p a c", a=2), ACT.Copy), "hid_hi")
                added(f"down{l}_0")
                added(f"down{l}_1")

            tail(0, (b_hi, b_lo), (a_hi, a_lo))

            last = number["down0_1"]
            sumsq("n1", [(x[:, t, :], evac(last, t)) for t in range(NT)], None, D)
            hi_parts("n1", a_hi, lambda k: col("od", k))
            for k in range(KT):
                op(e.activation(b_hi[:, k, :], mem_t[:, k, :], ACT.Copy, scale=col("mem1", k)), "mg1_hi")
            e.wait_ge(*after("lam_dot", 1))
            op(e.activation(sm("lam_e", 2), sm("lam_d", 2), ACT.Exp), "lam_e")
            for n in range(2):
                copy0(f"dq{n}", R(DQ + 4 * n * L, (L, 2), (1, L)), DHD ** -0.5)
            for n in range(2):
                copy0(f"dk{n}", R(DK + 4 * n * L, (L, 2), (1, L)))

            def diff_exp(r):
                t, per = (0, 4) if r == 0 else (1, 2)
                keys = (t + 1) * P
                at = (0, 16, 24)[r]
                e.wait_ge(*after("d_max", r + 1))
                base = SC + 2048 * (r % 2)
                for n in range(4 * per):
                    v = R(base + n * keys, (1, keys))
                    op(e.activation(v, v, ACT.Exp, bias=sm("d_nmax", 32)[:, at + n:at + n + 1],
                                    accum_out=sm("d_sum", 32)[:, at + n:at + n + 1]), "d_exp")

            def at_copy(r):
                for b in range(2):
                    e.wait_ge(*after("d_anT", 2 * r + b + 1))
                    op(e.activation(R(AT + (2 * r + b) * 512, (1, 512)), X_[b][:, :], ACT.Copy), "d_at")

            diff_exp(0)
            copy0("dv0", R(DV, (1, 512)))
            at_copy(0)
            diff_exp(1)
            copy0("dv1", R(DV + 512, (1, 512)))
            at_copy(1)
            diff_exp(2)
            copy0("xk1_0", xk[:, 0:2, :])
            copy0("xk1_1", xk[:, 4:6, :])
            at_copy(2)
            copy0("xv1_0", xv[:, 0, 0:512])
            copy0("xv1_1", xv[:, 0, 512:1024])
            for b in range(4):
                e.wait_ge(*after("do_mm", b + 1))
                if b >= 2:
                    e.wait_ge(*after("do_sum", b - 1))
                op(e.activation(junk[:, b % 2, :], X_[b][:, :], ACT.Square), "do_sq")
            hi_parts("d", b_hi, lambda k: col("subln"))
            added("dout0")
            added("dout1")
            tail(1, (a_hi, a_lo), (b_hi, b_lo))
            last = number["down1_1"]
            sumsq("fin", [(x[:, t, :], evac(last, t)) for t in range(NT)], None, D)

        @block.vector
        def _(e):
            op, settle, link = tracker(e, "dve_step")

            def split(c):
                if c >= len(chunks):
                    return
                width = chunks[c][3]
                for j in range(0, PIECES, 2):
                    e.wait_ge(*after("hi_ready", 4 * c + j + 1))
                    op(e.tensor_tensor(w_lo[:, j, :, 0:width], raw[:, j, :, 0:width],
                                       w_hi[:, j, :, 0:width].bitcast(F32), ALU.subtract), "lo_dve")

            def ahead(name):
                g = number[name]
                for c in range(first_chunk[g], first_chunk[g] + len(groups[g][2])):
                    split(c + 1)
                return g

            def done(g):
                e.wait_ge(*after("group_done", g + 1))

            def copy1(name, dst, scale=None):
                g = ahead(name)
                done(g)
                s, v = evac(g, 1)
                src = bank_view(g, 1, dst)
                if scale is None:
                    op(e.tensor_copy(dst, src), s.name, v)
                else:
                    op(e.tensor_scalar(dst, src, scale, None, ALU.mult), s.name, v)

            def add_x(name, n):
                g = ahead(name)
                done(g)
                for t in range(NT):
                    s, v = evac(g, t)
                    xx = x[:, t, n * 512:(n + 1) * 512]
                    op(e.tensor_tensor(xx, xx, banks_of(g)[t][:, :], ALU.add), s.name, v)

            def lo_parts(key, act, gain):
                for b in range(4):
                    e.wait_ge(*after(key + "_hi", 2 * (b + 1)))
                    for kk in range(2):
                        k = 2 * b + kk
                        op(e.scalar_tensor_tensor(out=act[1][:, k, :], in0=X_[b][:, kk * L:(kk + 1) * L],
                                                  scalar=gain(k), in1=act[0][:, k, :].bitcast(F32), op0=ALU.mult,
                                                  op1=ALU.subtract), key + "_lo")

            def scaled(key, src, dst):
                e.wait_ge(*after(key + "_rstd", 1))
                for t in range(NT):
                    op(e.tensor_scalar(dst(t), src(t), sm(key + "_r", 2)[:, t:t + 1], None, ALU.mult), key + "_xn")

            split(0)
            scaled("mem", lambda t: R(MEMN + t * D, (1, D)), lambda t: R(MEMN + t * D, (1, D)))
            scaled("n0", lambda t: x[:, t, :], lambda t: R(XN + t * D, (1, D)))
            for b in range(4):
                e.wait_ge(*after("mem_T", b + 1))
                op(e.tensor_copy(mem_t[:, 2 * b:2 * b + 2, :], X_[b][:, :].rearrange("p (a b) -> p a b", a=2)),
                   "mem_copy")
            e.wait_ge(*after("cols_ready", 1))
            op(e.tensor_scalar(half[:], cols[:, COLS["convw"]:COLS["convw"] + 50], 0.5, None, ALU.mult), "half")
            e.wait_ge(*after("sw_hi", 1))
            op(e.tensor_tensor(sw_lo[:], sw[:], sw_hi[:].bitcast(F32), ALU.subtract), "sw_lo")
            for k in range(KT):
                e.wait_ge(*after("mg0_hi", k + 1))
                op(e.scalar_tensor_tensor(out=b_lo[:, k, :], in0=mem_t[:, k, :], scalar=col("mem0", k),
                                          in1=b_hi[:, k, :].bitcast(F32), op0=ALU.mult, op1=ALU.subtract), "mg0_lo")
            lo_parts("n0", (a_hi, a_lo), lambda k: col("ev", k))
            copy1("xk0_0", xk[:, 2:4, :])
            copy1("xk0_1", xk[:, 6:8, :])
            copy1("xv0_0", xv[:, 1, 0:512])
            copy1("xv0_1", xv[:, 1, 512:1024])
            copy1("xbc0", R(XB + 2 * XBW + 3, (XBW, 2), (1, L)))

            e.wait_ge(*after("dg_copy", 1))
            v, n_, u, s1, s2, pp = (sm(k, 32) for k in ("dt_v", "dt_n", "dt_u", "dt_s", "dt_s2", "dt_p"))
            dtb = row[:, 0:16].unsqueeze(1).to_broadcast([P, NT, 16])

            def two(a):
                return a.rearrange("p (t h) -> p t h", t=NT)

            link(e.tensor_tensor(two(v), dgs[:, :, 0:16], dtb, ALU.add))
            link(e.scalar_tensor_tensor(out=n_, in0=v, scalar=-1.0, in1=v, op0=ALU.mult, op1=ALU.min), "dt_na")
            e.wait_ge(*after("dt_u", 1))
            link(e.tensor_scalar(s1, u, 2.0, None, ALU.add))
            link(e.reciprocal(s2, s1))
            link(e.tensor_tensor(s1, u, s2, ALU.mult))
            link(e.tensor_tensor(s2, s1, s1, ALU.mult))
            link(e.tensor_scalar(pp, s2, 1.0 / 17, None, ALU.mult))
            for k in (15, 13, 11, 9, 7, 5, 3):
                link(e.scalar_tensor_tensor(out=pp, in0=pp, scalar=1.0 / k, in1=s2, op0=ALU.add, op1=ALU.mult))
            link(e.scalar_tensor_tensor(out=pp, in0=pp, scalar=1.0, in1=s1, op0=ALU.add, op1=ALU.mult))
            link(e.tensor_scalar(v, v, 0.0, None, ALU.max))
            dt = sm("dt", 32)
            link(e.scalar_tensor_tensor(out=dt, in0=pp, scalar=2.0, in1=v, op0=ALU.mult, op1=ALU.add))
            e.wait_ge(*after("ea", 1))
            ea = sm("ea", 16).unsqueeze(1).to_broadcast([P, NT, 16])
            link(e.tensor_tensor(two(pp), two(dt), ea, ALU.mult))
            link(e.tensor_scalar(sm("loga", 32), pp, -1.0, None, ALU.mult), "loga")

            copy1("xbc1", R(XB + 6 * XBW + 3, (XBW, 2), (1, L)))
            for t in range(NT):
                e.wait_ge(*after("g_abs", t + 1))
                op(e.tensor_scalar(sp[:, t, :], X_[2 + t][:, :], -1.0, 0.0, ALU.mult, ALU.max), "g_max")
            g = ahead("xbc2")
            done(g)
            e.wait_ge(*evac(g, 0))
            op(e.memset(sm("spare", 1), 0.0), evac(g, 1)[0].name, evac(g, 1)[1])
            settle()
            e.wait_ge(*after("g_ln", 1))
            for t in range(NT):
                op(e.tensor_tensor(sp[:, t, :], sp[:, t, :], junk[:, t, :], ALU.add), "sp_ready")

            def tap(j, c):
                return half[:, j * XT + c:j * XT + c + 1]

            for n in ("xbc0", "xbc1", "xbc2"):
                e.wait_ge(*evac(number[n], 0))
            settle()
            for j in range(TAPS):
                for c in range(XT):
                    src, dst = R(XB + c * XBW + j, (1, L)), R(CV + c * L, (1, L))
                    if j == 0:
                        op(e.tensor_scalar(dst, src, tap(0, c), half[:, 40 + c:41 + c], ALU.mult, ALU.add))
                    else:
                        if c == 0:
                            settle()
                        op(e.scalar_tensor_tensor(out=dst, in0=src, scalar=tap(j, c), in1=dst, op0=ALU.mult,
                                                  op1=ALU.add), "conv" if j == TAPS - 1 else None)

            def gate(name, n, base):
                g = ahead(f"{name}{n}")
                for t in range(NT):
                    e.wait_ge(*after(name + "_tanh", 2 * n + t + 1))
                    s, v = evac(g, t)
                    dst = R(base + t * D + n * 512, (1, 512))
                    op(e.scalar_tensor_tensor(out=dst, in0=dst, scalar=1.0, in1=banks_of(g)[t][:, :], op0=ALU.add,
                                              op1=ALU.mult), s.name, v)

            gate("z", 0, ZZ)
            gate("z", 1, ZZ)
            e.wait_ge(*after("conv_tanh", 1))
            link(e.scalar_tensor_tensor(out=R(CV, (1, XT * L)), in0=R(TT, (1, XT * L)), scalar=1.0,
                                        in1=R(CV, (1, XT * L)), op0=ALU.add, op1=ALU.mult), "conv_silu")
            for g in range(SG):
                e.wait_ge(*after("ssd_score", g + 1))
                G = GG + g * 384
                op(e.tensor_tensor(R(G, (1, P)), X_[g][:, 0:P], tri, ALU.mult), "ssd_g")
                op(e.tensor_copy(R(G + P, (1, P)), X_[g][:, P:2 * P]), "ssd_g")
                op(e.tensor_tensor(R(G + 2 * P, (1, P)), X_[g][:, 2 * P:3 * P], tri, ALU.mult), "ssd_g")
            cc = sm("cc", 48)
            e.wait_ge(*after("cum_mm", 1))
            link(e.tensor_copy(cc, X_[2][:, 0:48]), "cum_ready")
            link(e.tensor_tensor(sm("wts", 16), cc[:, 32:48], cc[:, 0:16], ALU.subtract), "cum_ready")

            def heads(ap, n=SP_):
                return ap.unsqueeze(2).to_broadcast([P, ap.shape[1], n])

            def decay(t):
                for b in range(4):
                    e.wait_ge(*after("cumb_mm", 4 * t + b + 1))
                    op(e.tensor_tensor(R(MM + b * 512, (P, 4), (1, P)), X_[b][:, :].rearrange("p (h q) -> p h q", h=4),
                                       heads(cc[:, t * SH + 4 * b:t * SH + 4 * b + 4], P), ALU.subtract), "seg")
                settle()
                link(e.tensor_scalar(R(MM, (1, 2048)), R(MM, (1, 2048)), 0.0, None, ALU.min), "seg_min")

            def weigh(t):
                e.wait_ge(*after("ssd_exp", t + 1))
                for g in range(SG):
                    m = R(MM + g * 1024, (P, 8), (1, P))
                    op(e.tensor_tensor(m, m, R(GG + g * 384 + 2 * P * t, (0, 8), (1, P)), ALU.mult), "ssd_m")

            decay(0)
            for t in range(NT):
                e.wait_ge(*after("xs_ready", 2 * (t + 1)))
                op(e.tensor_tensor(R(XDT + t * D, (SP_, SH), (1, SP_)), R(XS + t * D, (SP_, SH), (1, SP_)),
                                   heads(dt[:, t * SH:(t + 1) * SH]), ALU.mult), "xdt")
            weigh(0)
            settle()
            e.wait_ge(*after("wts", 1))
            op(e.tensor_tensor(R(WX, (SP_, SH), (1, SP_)), R(XDT, (SP_, SH), (1, SP_)), heads(sm("wts", 16)), ALU.mult),
               "wx")
            dsk = row[:, 32:48]
            settle()
            for t in range(NT):
                op(e.tensor_tensor(R(XS + t * D, (SP_, SH), (1, SP_)), R(XS + t * D, (SP_, SH), (1, SP_)), heads(dsk),
                                   ALU.mult))
            copy1("q0", R(QK + 1024 + 512, (L, 2), (1, L)), GK ** -0.5)

            def y_add(t):
                settle()
                for b in range(2):
                    e.wait_ge(*after("y_mm", 2 * t + b + 1))
                    y = R(XS + t * D + b * 512, (1, 512))
                    op(e.tensor_tensor(y, y, X_[2 * t + b][:, :], ALU.add), "y_add")

            y_add(0)
            decay(1)
            weigh(1)
            copy1("k0", R(QK + 512, (L, 2), (1, L)))
            y_add(1)
            e.wait_ge(*after("e1", 1))
            for g in range(SG):
                e.wait_ge(*after("yc_mm", g + 1))
                op(e.tensor_tensor(R(YC + g * 512, (SP_, 8), (1, SP_)), X_[g][:, :].rearrange("p (h q) -> p h q", h=8),
                                   heads(sm("e1", 16)[:, 8 * g:8 * g + 8]), ALU.mult), "yc_scaled")
            settle()
            link(e.tensor_tensor(R(XS + D, (1, D)), R(XS + D, (1, D)), R(YC, (1, D)), ALU.add))
            for t in range(NT):
                y = R(XS + t * D, (1, D))
                op(e.scalar_tensor_tensor(out=y, in0=y, scalar=0.5, in1=R(ZZ + t * D, (1, D)), op0=ALU.mult,
                                          op1=ALU.mult), "yz")
            copy1("v0", R(VV + D, (1, 512)))
            copy1("v1", R(VV + D + 512, (1, 512)))
            e.wait_ge(*after("y_rstd", 1))
            for t in range(NT):
                for g in range(SG):
                    y = R(XS + t * D + g * 512, (1, 512))
                    op(e.tensor_scalar(y, y, sm("y_r", 4)[:, 2 * t + g:2 * t + g + 1], None, ALU.mult), "yn")
            lo_parts("y", (b_hi, b_lo), lambda k: col("ssdn", k))
            gate("r", 0, RR)

            for b in range(2):
                e.wait_ge(*after("gcum_mm", b + 1))
                op(e.tensor_scalar(R(CC2 + 1024 + b * 512, (1, 512)), X_[b][:, :], -1.0 / TAU, None, ALU.mult), "gcum")
            for t in range(NT):
                e.wait_ge(*after("diag_mm", t + 1))
                op(e.tensor_tensor(R(STT_ + t * 512, (P, GH), (1, P)), X_[2 + t][:, :].rearrange("p (h q) -> p h q", h=4),
                                   ident.unsqueeze(1).to_broadcast([P, GH, P]), ALU.mult), "gla_diag")
            gate("r", 1, RR)
            e.wait_ge(*after("gneg", 1))
            e.wait_ge(*after("mask_loaded", 16))

            def gla_diff(n):
                buf = GXA if n % 2 == 0 else GXB
                if n >= 2:
                    e.wait_ge(*after("level_mm", 2 * (n - 2) + 1))
                if n == 0:
                    op(e.tensor_tensor(R(buf, (L, GH), (1, P)), R(CC2, (L, GH), (1, P)), R(CC2 + P - 1, (L, GH), (0, P)),
                                       ALU.subtract), "gd")
                else:
                    b = LEVELS[n - 1]
                    m = 1024 // (2 * b)
                    op(e.tensor_tensor(R(buf, (2 * b, m), (b, 2), (1, b)), R(CC2, (2 * b, m), (1024 + b, 2), (1, b)),
                                       R(CC2 + b - 1, (2 * b, m), (1024, 2), (0, b)), ALU.subtract), "gd")

            def gla_mult(n):
                buf = GXA if n % 2 == 0 else GXB
                b = P if n == 0 else LEVELS[n - 1]
                m = 1024 // (2 * b)
                e.wait_ge(*after("ge", n + 1))
                v = R(buf, (2 * b, m), (b, 2), (1, b))
                op(e.tensor_tensor(v, v, R(QK, (2 * b, m), (1024 + b, 2), (1, b)), ALU.mult), "gx")

            def gla_take(n):
                if n == 0:
                    e.wait_ge(*after("level_mm", 1))
                    op(e.tensor_copy(R(SXT, (1, 512)), X_[0][:, :]), "gla_cross")
                    return
                settle()
                for t in range(NT):
                    e.wait_ge(*after("level_mm", 2 * (n - 1) + t + 2))
                    op(e.copy_predicated(R(STT_ + t * 512, (P, GH), (1, P)),
                                         mask[:, n - 1, :].unsqueeze(1).to_broadcast([P, GH, P]),
                                         X_[2 * (n % 2) + t][:, :].rearrange("p (h q) -> p h q", h=4)), "gla_s")

            e.wait_ge(evac(number["k0"], 0)[0], evac(number["k0"], 0)[1])
            gla_diff(0)
            for n in range(8):
                if n < 7:
                    gla_diff(n + 1)
                gla_mult(n)
                if n > 0:
                    gla_take(n - 1)
                if n == 4:
                    add_x("outy0", 0)
            gla_take(7)
            add_x("outy1", 1)
            e.wait_ge(*after("o_rstd", 1))
            for b in range(4):
                e.wait_ge(*after("o_sq", 2 * (b + 1)))
                for i in range(2):
                    t, h = b // 2, 2 * (b % 2) + i
                    op(e.scalar_tensor_tensor(out=R(OO + t * D + h * GV, (1, GV)), in0=X_[b][:, i * GV:(i + 1) * GV],
                                              scalar=sm("o_r", 8)[:, 2 * b + i:2 * b + i + 1],
                                              in1=R(RR + t * D + h * GV, (1, GV)), op0=ALU.mult, op1=ALU.mult), "on")
            lo_parts("o", (a_hi, a_lo), lambda k: col("glan", k % 2))
            add_x("outo0", 0)
            add_x("outo1", 1)

            def tail(l, one, two):
                scaled(f"xn{l}", lambda t: x[:, t, :], lambda t: R(XN + t * D, (1, D)))
                lo_parts(f"xn{l}", one, lambda k: col(f"xa{l}", k))
                for n in range(2):
                    copy1(f"xq{l}_{n}", R(CQ + (4 * n + 2) * L, (L, 2), (1, L)))
                nm = sm(f"c{l}_nmax", 8)
                for b in range(4):
                    e.wait_ge(*after(f"c{l}_score", b + 1))
                    v = nm[:, 2 * b:2 * b + 2]
                    link(e.tensor_reduce(v, X_[b][:, :].rearrange("p (h m) -> p h m", h=2), AX, ALU.max, negate=True))
                    op(e.tensor_scalar(v, v, XHD ** -0.5, None, ALU.mult), f"c{l}_max")
                e.wait_ge(*after(f"c{l}_exp", 8))
                link(e.reciprocal(sm(f"c{l}_ri", 8), sm(f"c{l}_sum", 8)))
                for n in range(8):
                    v = R(CP + n * NM, (1, NM))
                    op(e.tensor_scalar(v, v, sm(f"c{l}_ri", 8)[:, n:n + 1], None, ALU.mult), f"c{l}_p")
                for h in range(XH):
                    e.wait_ge(*after(f"c{l}_hi", h + 1))
                    op(e.tensor_tensor(two[1][:, 2 * h:2 * h + 2, :], X_[h][:, :].rearrange("p (a b) -> p a b", a=2),
                                       two[0][:, 2 * h:2 * h + 2, :].bitcast(F32), ALU.subtract), f"c{l}_lo")
                add_x(f"xo{l}_0", 0)
                add_x(f"xo{l}_1", 1)
                scaled(f"mn{l}", lambda t: x[:, t, :], lambda t: R(XN + t * D, (1, D)))
                lo_parts(f"mn{l}", one, lambda k: col(f"mlp{l}", k))
                for n in range(8):
                    g = ahead(f"up{l}_{n}")
                    for b in range(2):
                        e.wait_ge(*evac(g, b))
                        settle()
                        op(e.tensor_tensor(sp[:, b, :], junk[:, b, :], junk[:, b, :], ALU.mult), "hid_sq")
                    for b in range(2):
                        e.wait_ge(*after("hid_hi", 16 * l + 2 * n + b + 1))
                        lo = hid_lo[:, 4 * n + 2 * b:4 * n + 2 * b + 2, :]
                        hi = hid_hi[:, 4 * n + 2 * b:4 * n + 2 * b + 2, :].bitcast(F32)
                        op(e.tensor_tensor(lo, sp[:, b, :].rearrange("p (a c) -> p a c", a=2), hi, ALU.subtract),
                           f"hid{l}")
                add_x(f"down{l}_0", 0)
                add_x(f"down{l}_1", 1)

            tail(0, (b_hi, b_lo), (a_hi, a_lo))

            scaled("n1", lambda t: x[:, t, :], lambda t: R(XN + t * D, (1, D)))
            lo_parts("n1", (a_hi, a_lo), lambda k: col("od", k))
            for k in range(KT):
                e.wait_ge(*after("mg1_hi", k + 1))
                op(e.scalar_tensor_tensor(out=b_lo[:, k, :], in0=mem_t[:, k, :], scalar=col("mem1", k),
                                          in1=b_hi[:, k, :].bitcast(F32), op0=ALU.mult, op1=ALU.subtract), "mg1_lo")
            ld, lam = sm("lam_d", 2), row[:, 48:48 + 4 * DHD].rearrange("p (m a d) -> p m a d", m=2, a=2)
            lp = sm("lam_p", 2 * DHD).rearrange("p (m d) -> p m d", m=2)
            link(e.tensor_tensor(lp, lam[:, :, 0, :], lam[:, :, 1, :], ALU.mult))
            op(e.tensor_reduce(ld, lp, AX, ALU.add), "lam_dot")
            e.wait_ge(*after("lam_e", 1))
            le, nl = sm("lam_e", 2), sm("nlam", 1)
            link(e.tensor_tensor(nl, le[:, 1:2], le[:, 0:1], ALU.subtract))
            link(e.tensor_scalar(nl, nl, LAMBDA_INIT, None, ALU.subtract))
            for n in range(2):
                copy1(f"dq{n}", R(DQ + (4 * n + 2) * L, (L, 2), (1, L)), DHD ** -0.5)
            for n in range(2):
                copy1(f"dk{n}", R(DK + (4 * n + 2) * L, (L, 2), (1, L)))
            e.wait_ge(*after("bias_loaded", 16))
            nm, rs = sm("d_nmax", 32), sm("d_sum", 32)

            def diff_bias(r):
                t, per = (0, 4) if r == 0 else (1, 2)
                keys = (t + 1) * P
                at, base = (0, 16, 24)[r], SC + 2048 * (r % 2)
                for b in range(4):
                    e.wait_ge(*after("d_score", 4 * r + b + 1))
                    h0 = per * (b // 2) + (4 if r == 2 else 0)
                    op(e.tensor_tensor(R(base + b * 512, (keys, per), (1, keys)),
                                       X_[b][:, :].rearrange("p (h k) -> p h k", h=per),
                                       R(BIAS + h0 * L + L - keys, (L, per), (1, keys)), ALU.add), "d_bias")
                settle()
                link(e.tensor_reduce(nm[:, at:at + 4 * per], R(base, (keys, 4 * per), (1, keys)), AX, ALU.max,
                                     negate=True), "d_max")

            def diff_mix(r):
                t, per = (0, 4) if r == 0 else (1, 2)
                keys = (t + 1) * P
                at, base = (0, 16, 24)[r], SC + 2048 * (r % 2)
                e.wait_ge(*after("d_exp", (16, 24, 32)[r]))
                ri, rl = sm("d_ri", 32), sm("d_rl", 32)
                link(e.reciprocal(ri[:, at:at + 4 * per], rs[:, at:at + 4 * per]))
                link(e.tensor_scalar(rl[:, at:at + 4 * per], ri[:, at:at + 4 * per], nl, None, ALU.mult))
                if r > 0:
                    e.wait_ge(*after("d_anT", 2 * r))
                for pair in range(2):
                    for i in range(per):
                        n = per * pair + i
                        c0 = at + 2 * per * pair + i
                        c1 = c0 + per
                        p0 = R(base + (c0 - at) * keys, (1, keys))
                        op(e.tensor_scalar(R(AN + n * keys, (1, keys)), p0, ri[:, c0:c0 + 1], None, ALU.mult))
                settle()
                for pair in range(2):
                    for i in range(per):
                        n = per * pair + i
                        c1 = at + 2 * per * pair + i + per
                        an = R(AN + n * keys, (1, keys))
                        p1 = R(base + (c1 - at) * keys, (1, keys))
                        op(e.scalar_tensor_tensor(out=an, in0=p1, scalar=rl[:, c1:c1 + 1], in1=an, op0=ALU.mult,
                                                  op1=ALU.add), "d_an")

            diff_bias(0)
            diff_mix(0)
            copy1("dv0", R(DV + D, (1, 512)))
            diff_bias(1)
            diff_mix(1)
            copy1("dv1", R(DV + D + 512, (1, 512)))
            diff_bias(2)
            diff_mix(2)
            copy1("xk1_0", xk[:, 2:4, :])
            copy1("xk1_1", xk[:, 6:8, :])
            copy1("xv1_0", xv[:, 1, 0:512])
            copy1("xv1_1", xv[:, 1, 512:1024])
            for b in range(4):
                e.wait_ge(*after("do_sq", b + 1))
                op(e.tensor_reduce(sm("do_ss", 16)[:, 4 * b:4 * b + 4], junk[:, b % 2, :].rearrange("p (h v) -> p h v", h=4),
                                   AX, ALU.add), "do_sum")
            e.wait_ge(*after("do_rstd", 1))
            for b in range(4):
                op(e.tensor_tensor(R(SC + b * 512, (P, 4), (1, P)), X_[b][:, :].rearrange("p (h v) -> p h v", h=4),
                                   heads(sm("do_r", 16)[:, 4 * b:4 * b + 4], P), ALU.mult), "d_on")
            lo_parts("d", (b_hi, b_lo), lambda k: col("subln"))
            add_x("dout0", 0)
            add_x("dout1", 1)
            tail(1, (a_hi, a_lo), (b_hi, b_lo))
            e.wait_ge(*after("fin_rstd", 1))
            e.wait_ge(*after("fnorm_loaded", 16))
            for t in range(NT):
                op(e.scalar_tensor_tensor(out=R(XN + t * D, (1, D)), in0=x[:, t, :], scalar=sm("fin_r", 2)[:, t:t + 1],
                                          in1=xk[:, 0:4, :].rearrange("p a b -> p (a b)"), op0=ALU.mult, op1=ALU.mult),
                   "final")

        @block.gpsimd
        def _(e):
            op, settle, link = tracker(e, "pool_step")

            def split(c):
                if c >= len(chunks):
                    return
                width = chunks[c][3]
                for j in range(1, PIECES, 2):
                    e.wait_ge(*after("hi_ready", 4 * c + j + 1))
                    op(e.tensor_tensor(w_lo[:, j, :, 0:width], raw[:, j, :, 0:width],
                                       w_hi[:, j, :, 0:width].bitcast(F32), ALU.subtract), "lo_pool")

            def ahead(*names):
                for name in names:
                    g = number[name]
                    for c in range(first_chunk[g], first_chunk[g] + len(groups[g][2])):
                        split(c + 1)

            def rstd(key, n, width, count, post=None, wait="_sq"):
                e.wait_ge(*after(key + wait, count))
                r = sm(key + "_r", n)
                link(e.tensor_scalar(r, sm(key + "_ss", n), 1.0 / width, EPS, ALU.mult, ALU.add))
                if post is None:
                    link(e.tensor_tensor(r, r, neghalf[:, 0:n], ALU.pow), key + "_rstd")
                else:
                    link(e.tensor_tensor(r, r, neghalf[:, 0:n], ALU.pow))
                    link(e.tensor_scalar(r, r, post, None, ALU.mult), key + "_rstd")

            op(e.memset(glr_t[:], 1.0), "ones_ready")
            split(0)
            e.wait_ge(*after("const_loaded", 16))
            rstd("mem", 2, D, 2)
            rstd("n0", 2, D, 2)
            op(e.memset(R(XB, (XBW, XT), (1, 3)), 0.0), "pad_ready")
            ahead("xk0_0", "xk0_1", "xv0_0", "xv0_1", "xbc0", "xbc1", "xbc2", "z0", "z1", "q0", "k0", "v0", "v1")
            rstd("y", 4, 512, 4)
            ahead("r0", "r1", "outy0", "outy1")
            rstd("o", 8, GV, 8, 0.5)
            ahead("outo0", "outo1")

            def tail(l):
                rstd(f"xn{l}", 2, D, 2)
                ahead(f"xq{l}_0", f"xq{l}_1", f"xo{l}_0", f"xo{l}_1")
                rstd(f"mn{l}", 2, D, 2)
                ahead(*[f"up{l}_{n}" for n in range(8)], f"down{l}_0", f"down{l}_1")

            tail(0)
            rstd("n1", 2, D, 2)
            ahead("dq0", "dq1", "dk0", "dk1", "dv0", "dv1", "xk1_0", "xk1_1", "xv1_0", "xv1_1")
            rstd("do", 16, P, 4, 1.0 - LAMBDA_INIT, "_sum")
            ahead("dout0", "dout1")
            tail(1)
            rstd("fin", 2, D, 2)


def kernel(x, mem, ev_norm, ev_w_in, ev_conv_w, ev_conv_b, ev_dt_bias, ev_a_log, ev_d_skip, ev_ssd_norm, ev_gla_w2,
           ev_gla_b, ev_gla_norm, ev_w_out, od_norm, od_w_qkv, od_lam_q1, od_lam_k1, od_lam_q2, od_lam_k2, od_subln,
           od_w_o, xa_norm, xa_mem_norm, xa_wq, xa_wkv, xa_wo, mlp_norm, mlp_w1, mlp_w2, final_norm):
    import concourse.bacc as bacc
    from concourse.bass_utils import run_bass_kernel_spmd

    def rows(*arrays):
        return np.concatenate([np.asarray(a).reshape(-1, P) for a in arrays], axis=0)

    prow = rows(ev_norm[0], od_norm[0], xa_norm[0], xa_norm[1], xa_mem_norm[0], xa_mem_norm[1], mlp_norm[0],
                mlp_norm[1], ev_ssd_norm[0], ev_gla_norm[0], od_subln[0], ev_conv_w[0], ev_conv_b[0])
    row = np.concatenate([np.asarray(a).reshape(-1) for a in
                          (ev_dt_bias[0], ev_a_log[0], ev_d_skip[0], od_lam_q1[0], od_lam_k1[0], od_lam_q2[0],
                           od_lam_k2[0])])[None]
    w_in = np.asarray(ev_w_in)[0]
    w_small = np.concatenate([w_in[:, DT0:DT0 + SH], w_in[:, GLR0:GLR0 + RANK]], axis=1)
    gla_w2b = np.concatenate([np.asarray(ev_gla_w2)[0], np.asarray(ev_gla_b)], axis=0)

    i, j = np.arange(P)[:, None], np.arange(P)[None, :]
    const = np.concatenate([i == j, i <= j, np.ones((P, P)), np.full((P, 16), -0.5)], axis=1).astype(np.float32)
    mask = np.stack([(i // (2 * b) == j // (2 * b)) & (i % (2 * b) < b) & (j % (2 * b) >= b) for b in LEVELS],
                    axis=1).astype(np.int32)
    dist = P + np.arange(P)[:, None] - np.arange(L)[None, :]
    slopes = np.array([2.0 ** -(h + 1) for h in range(DH)], np.float32)
    bias = np.where(dist[:, None, :] >= 0, -slopes[None, :, None] * dist[:, None, :], -3e38)
    bias = bias.astype(np.float32).reshape(P, DH * L)

    arrays = {
        "x": x, "mem": mem, "ev_w_in": ev_w_in, "ev_w_out": ev_w_out, "od_w_qkv": od_w_qkv, "od_w_o": od_w_o,
        "xa_wq": xa_wq, "xa_wkv": xa_wkv, "xa_wo": xa_wo, "mlp_w1": mlp_w1, "mlp_w2": mlp_w2,
        "prow": prow, "row": row, "w_small": w_small, "gla_w2b": gla_w2b, "fnorm": np.asarray(final_norm)[None],
        "const": const, "mask": mask, "bias": bias,
    }
    nc = bacc.Bacc("TRN2", target_bir_lowering=False, num_devices=1)
    given, w = {}, {}
    for name, a in arrays.items():
        a = np.ascontiguousarray(a)
        given["in_" + name] = a
        w[name] = nc.dram_tensor("in_" + name, a.shape, mybir.dt.from_np(a.dtype), kind="ExternalInput").ap()
    w["out"] = nc.dram_tensor("out", (1, L, D), F32, kind="ExternalOutput").ap()
    trunk(nc, w)
    result = run_bass_kernel_spmd(nc, [given], core_ids=[0])
    return result.results[0]["out"]
```

```python
import math
from contextlib import ExitStack

import concourse.bass as bass
import numpy as np
from concourse import mybir

F32 = mybir.dt.float32
F32R = mybir.dt.float32r
I32 = mybir.dt.int32
ALU = mybir.AluOpType
ACT = mybir.ActivationFunctionType
AX = mybir.AxisListType.X

P = 128
D = 1024
L = 256
NT = L // P
KT = D // P
EPS = 1e-5
FF = 4 * D
PIECES = 4
SH, SP_, SG, SN = 16, 64, 2, 64
XBC = SH * SP_ + 2 * SG * SN
XT = XBC // P
TAPS = 4
GH, GK, GV, RANK, TAU = 4, 128, 256, 16, 16.0
DH, DHD = 8, 64
PAIRS = ("xo0_0", "xo1_0")
LAMBDA_INIT = 0.8 - 0.6 * math.exp(-0.3 * 1)
XH, XHD, NM = 4, 256, 256
Z0, XBC0 = 0, 1024
DT0 = XBC0 + XBC
Q0 = DT0 + SH
K0 = Q0 + GH * GK
V0 = K0 + GH * GK
GLR0 = V0 + GH * GV
R0 = GLR0 + RANK

COLS = {}
_n = 0
for _name, _count in [("ev", 8), ("od", 8), ("xa0", 8), ("xa1", 8), ("mem0", 8), ("mem1", 8), ("mlp0", 8),
                      ("mlp1", 8), ("ssdn", 8), ("glan", 2), ("subln", 1), ("convw", TAPS * XT), ("convb", XT)]:
    COLS[_name] = _n
    _n += _count
NCOLS = _n

ROW = {"dtb": 0, "alog": 16, "dskip": 32, "lam": 48}
NROW = 48 + 4 * DHD

C_ID, C_TRI, C_ONE, C_NEG = 0, P, 2 * P, 3 * P
NCONST = 3 * P + 16
LEVELS = [64, 32, 16, 8, 4, 2, 1]

REG = 16672
XB, CV, TT, ZZ, MM, GG, QK, VV = 0, 2592, 5152, 7712, 9760, 11808, 12576, 14624
XBW = L + TAPS - 1
XS, XDT, WX, YC = XB, TT, CV, CV + 1024
CC2, GXA, GXB, STT_, SXT, RR, OO = MM, TT, TT + 1024, CV, CV + 1024, ZZ, XB
MEM = VV
DQ, DK, DV, BIAS, SC, AN, AT = 0, 2048, 4096, 6144, 8192, 12288, 13312
CQ, CP, CPT = 0, 2048, 4096
ROUNDS = [(1, 2, 0), (0, 4, 0), (1, 2, 4)]
AT_TILE0 = 8


def groups_of(w):
    out = []

    def add(name, mode, weights, columns, rows=(0,), width=512):
        for n, c in enumerate(columns):
            out.append((f"{name}{n}", mode, [(weights, r, c, width) for r in rows]))

    def cross(layer):
        add(f"xk{layer}_", "T", w["xa_wkv"][layer], (0, 512))
        add(f"xv{layer}_", "N", w["xa_wkv"][layer], (1024, 1536))

    def tail(layer):
        add(f"xq{layer}_", "T", w["xa_wq"][layer], (0, 512))
        add(f"xo{layer}_", "N", w["xa_wo"][layer], (0, 512))
        add(f"up{layer}_", "T", w["mlp_w1"][layer], range(0, FF, 512))
        add(f"down{layer}_", "N", w["mlp_w2"][layer], (0, 512), range(0, FF, D))

    w_in, w_out = w["ev_w_in"][0], w["ev_w_out"][0]
    add("xbc", "T", w_in, (XBC0, XBC0 + 512))
    out.append(("xbc2", "T", [(w_in, 0, XBC0 + 1024, 256)]))
    add("q", "T", w_in, (Q0,))
    add("k", "T", w_in, (K0,))
    add("z", "N", w_in, (Z0, Z0 + 512))
    cross(0)
    add("v", "N", w_in, (V0, V0 + 512))
    add("r", "N", w_in, (R0, R0 + 512))
    add("outy", "N", w_out, (0, 512))
    add("outo", "N", w_out, (0, 512), (1024,))
    tail(0)
    w_qkv = w["od_w_qkv"][0]
    for n in range(2):
        out.append((f"dq{n}", "T", [(w_qkv, 0, n * 512, 512)]))
        out.append((f"dk{n}", "T", [(w_qkv, 0, 1024 + n * 512, 512)]))
    add("dv", "N", w_qkv, (2048, 2560))
    cross(1)
    add("dout", "N", w["od_w_o"][0], (0, 512))
    tail(1)
    return out


def trunk(nc, w):
    groups = groups_of(w)
    number = {g[0]: n for n, g in enumerate(groups)}
    chunks = [c for g in groups for c in g[2]]
    first_chunk = []
    for g in groups:
        first_chunk.append(first_chunk[-1] + len(groups[len(first_chunk) - 1][2]) if first_chunk else 0)

    ctx = ExitStack()
    with ctx:
        def sb(name, shape, dt=F32):
            return ctx.enter_context(nc.sbuf_tensor(name, shape, dt))

        norms = ["n0", "mem", "y", "o", "xn0", "mn0", "n1", "do", "xn1", "mn1", "fin"]
        halves = ["n0", "mem", "y", "o", "xn0", "c0", "mn0", "n1", "d", "xn1", "c1", "mn1"]
        splits = ["n0", "mg0", "y", "o", "xn0", "c0", "mn0", "n1", "mg1", "d", "xn1", "c1", "mn1"]
        shared = {
            "squares": [(k + "_sq", 8 if k == "o" else 4) for k in norms],
            "rstd": [(k + "_rstd", 1) for k in norms],
            "turned": [(k + "_T", 4) for k in halves],
            "act_hi": [(k + "_hi", 4 if k[0] == "c" else 8) for k in splits],
            "act_lo": [(k + "_lo", 4 if k[0] == "c" else 8) for k in splits],
            "cross_score": [("c0_score", 4), ("c1_score", 4)],
            "cross_exp": [("c0_exp", 8), ("c1_exp", 8)],
            "cross_max": [("c0_max", 4), ("c1_max", 4)],
            "cross_p": [("c0_p", 8), ("c1_p", 8)],
            "cross_pT": [("c0_pT", 4), ("c1_pT", 4)],
            "cross_pt": [("c0_pt", 4), ("c1_pt", 4)],
            "hid_lo_ready": [("hid0", 16), ("hid1", 16)],
            "rbc_mm": [("n0_rbcmm", 1), ("mem_rbcmm", 1), ("n1_rbcmm", 1)],
            "rbc": [("n0_rbc", 1), ("mem_rbc", 1), ("n1_rbc", 1)],
        }
        stage = {}
        for family, parts_ in shared.items():
            base = 0
            for name_, steps in parts_:
                stage[name_] = (family, base)
                base += steps
        sems = {}

        def sem(name):
            if name not in sems:
                sems[name] = ctx.enter_context(nc.semaphore(name))
            return sems[name]

        def after(name, n):
            family, base = stage.get(name, (name, 0))
            return sem(family), base + n

        with nc.sbuf_tensor("region", [P, REG], F32) as region:
            pass
        with nc.sbuf_tensor("hid_hi", [P, FF // P, L], F32R) as hid_hi, \
                nc.sbuf_tensor("hid_lo", [P, FF // P, L], F32R) as hid_lo:
            pass
        keep = sb("keep_region", [P, REG])
        raw = sb("raw", [P, PIECES, 2, 512])
        w_hi = sb("w_hi", [P, PIECES, 2, 512], F32R)
        w_lo = sb("w_lo", [P, PIECES, 2, 512], F32R)
        x = sb("x", [P, NT, D])
        a_hi, a_lo = sb("a_hi", [P, KT, L], F32R), sb("a_lo", [P, KT, L], F32R)
        b_hi, b_lo = sb("b_hi", [P, KT, L], F32R), sb("b_lo", [P, KT, L], F32R)
        mem_t = sb("mem_t", [P, KT, NM])
        xk = sb("xk", [P, KT, NM])
        xv = sb("xv", [P, NM // P, D])
        junk = sb("junk", [P, 2, 512])
        sp = sb("sp", [P, NT, 512])
        const = sb("const", [P, NCONST])
        mask = sb("mask", [P, len(LEVELS), P], I32)
        prow = sb("prow", [NCOLS, P])
        cols = sb("cols", [P, NCOLS])
        half = sb("half", [P, (TAPS + 1) * XT])
        row = sb("row", [P, NROW])
        sw = sb("sw", [P, KT, 32])
        sw_hi, sw_lo = sb("sw_hi", [P, KT, 32], F32R), sb("sw_lo", [P, KT, 32], F32R)
        w2g = sb("w2g", [RANK + 1, 512])
        glr_t = sb("glr_t", [RANK + 1, L])
        dgs = sb("dgs", [P, NT, 32])
        small = sb("small", [P, 832])
        rbc = {"n0": sb("rbc_x", [P, L]), "mem": sb("rbc_mem", [P, NM])}
        rbc["n1"] = rbc["n0"]
        L_ = [ctx.enter_context(nc.psum_tensor(f"lin{n}", [P, 512], F32)) for n in range(4)]
        X_ = [ctx.enter_context(nc.psum_tensor(f"mix{n}", [P, 512], F32)) for n in range(4)]

        def R(off, *dims):
            return bass.AP(tensor=region, offset=off, ap=[[REG, P], *[list(d) for d in dims]])

        def result(t, n):
            return mem_t[:, 4 * t + 2 * n:4 * t + 2 * n + 2, :].rearrange("p a b -> p (a b)")

        small_at = {}

        def sm(name, n):
            if name not in small_at:
                small_at[name] = (sum(v[1] for v in small_at.values()), n)
            at, n = small_at[name]
            return small[:, at:at + n]

        ident, tri, ones = const[:, C_ID:C_ID + P], const[:, C_TRI:C_TRI + P], const[:, C_ONE:C_ONE + P]
        neghalf = const[:, C_NEG:C_NEG + 16]

        def col(name, k=0):
            return cols[:, COLS[name] + k:COLS[name] + k + 1]

        paired = {first_chunk[g] for g, grp in enumerate(groups) if grp[0] in PAIRS}
        ends = {}
        for g in range(len(groups)):
            if first_chunk[g] in paired:
                ends[first_chunk[g] + 1, 1] = g
            else:
                ends[first_chunk[g] + len(groups[g][2]) - 1, PIECES - 1] = g

        def piece_source(c, j):
            wt, r0, c0, width = chunks[c]
            if c in paired or c - 1 in paired:
                r, cc = 512 * (c - 1 in paired) + 256 * (j % 2), 512 * (j // 2)
            else:
                r, cc = r0 + 256 * j, c0
            return wt[r:r + 256, cc:cc + width].rearrange("(k p) n -> p k n", p=P)

        def piece_free(eng, c, j):
            if (c, j) in ends:
                eng.wait_ge(*after("group_done", ends[c, j] + 1))
            else:
                ended = sum(1 for at in ends if at < (c, j))
                eng.wait_ge(*after("mm_done", PIECES * c + j + 1 - ended))

        def bank_view(g, b, dst):
            bank = banks_of(g)[b][:, :]
            return bank if len(dst.shape) == 2 else bank.rearrange("p (a b) -> p a b", a=2)

        def banks_of(g):
            return L_[2 * (g % 2)], L_[2 * (g % 2) + 1]

        def evac(g, b):
            return sem(f"evac{g % 2}{b}"), g // 2 + 1

        def tracker(eng, own):
            tally, last = {}, []

            def op(ins, name=None, value=None):
                name = name or own
                tally[name] = tally.get(name, 0) + 1
                s, v = after(name, value or tally[name])
                ins.then_inc(s, 1)
                last[:] = [s, v]
                return ins

            def settle():
                eng.wait_ge(last[0], last[1])

            def link(ins, name=None):
                op(ins, name)
                settle()

            return op, settle, link

        block = ctx.enter_context(nc.Block())

        @block.sync
        def _(e):
            def load(dst, src, name):
                e.dma_start(dst, src).then_inc(sem(name), 16)

            def weights(c, pieces=range(PIECES)):
                width = chunks[c][3]
                for j in pieces:
                    if c > 0:
                        e.wait_ge(*after("hi_ready", 4 * (c - 1) + j + 1))
                        e.wait_ge(*after("lo_dve" if j % 2 == 0 else "lo_pool", 2 * (c - 1) + j // 2 + 1))
                    e.dma_start(raw[:, j, :, 0:width], piece_source(c, j)).then_inc(sem(f"raw_ready{j}"), 16)

            load(prow[:], w["prow"], "prow_loaded")
            load(const[:], w["const"], "const_loaded")
            for n in range(2):
                load(x[:, :, n * 512:(n + 1) * 512],
                     w["x"][0, :, n * 512:(n + 1) * 512].rearrange("(t p) d -> p t d", p=P), f"x_loaded{n}")
                weights(0, (2 * n, 2 * n + 1))
            load(sw[:], w["w_small"].rearrange("(k p) n -> p k n", p=P), "sw_loaded")
            load(R(MEM, (D, NT), (1, D)), w["mem"][0].rearrange("(t p) d -> p t d", p=P), "mem_loaded")
            load(row[:], w["row"].to_broadcast([P, NROW]), "row_loaded")
            load(w2g[:], w["gla_w2b"], "w2g_loaded")
            load(mask[:], w["mask"], "mask_loaded")
            for c in range(1, len(chunks)):
                weights(c)
                if c == first_chunk[number["dq0"]] + 1:
                    e.wait_ge(*after("group_done", number["down0_1"] + 1))
                    load(R(BIAS, (1, 2048)), w["bias"], "bias_loaded")
                if c == first_chunk[number["up1_2"]]:
                    e.wait_ge(*after("c1_score", 4))
                    load(xk[:, 0:4, :], w["fnorm"].to_broadcast([P, D]).rearrange("p (a b) -> p a b", a=4), "fnorm_loaded")
            for n in range(2):
                for t in range(NT):
                    half_ = slice(n * 512, (n + 1) * 512)
                    e.wait_ge(*after(f"final{t}", n + 1))
                    e.dma_start(w["out"][0, t * P:(t + 1) * P, half_],
                                result(t, n)).then_inc(sem("stored"), 16)
            e.wait_ge(*after("stored", 2 * 16 * NT))

        @block.tensor
        def _(e):
            freed = [None] * 4

            def take(b):
                if freed[b]:
                    e.wait_ge(*after(freed[b][0], freed[b][1]))
                return X_[b]

            def product(name, act, ready, per=2, before={}):
                g = number[name]
                _, mode, parts = groups[g]
                bank = banks_of(g)
                hi, lo = act
                if g >= 2:
                    for b in range(2):
                        s, v = evac(g - 2, b)
                        e.wait_ge(s, v)
                for n, (_, _, _, width) in enumerate(parts):
                    c = first_chunk[g] + n
                    for j in range(PIECES):
                        if n == len(parts) - 1 and j in before:
                            before[j]()
                        e.wait_ge(*after(ready, per * (PIECES * n + j + 1)))
                        e.wait_ge(*after("hi_ready", 4 * c + j + 1))
                        e.wait_ge(*after("lo_dve" if j % 2 == 0 else "lo_pool", 2 * c + j // 2 + 1))
                        begin, end = n == 0 and j == 0, n == len(parts) - 1 and j == PIECES - 1
                        if mode == "T":
                            for f in range(width // P):
                                out = bank[f // 2][:, (f % 2) * L:(f % 2 + 1) * L]
                                for kk in range(2):
                                    k = 2 * j + kk
                                    wh, wl = (t[:, j, kk, f * P:(f + 1) * P] for t in (w_hi, w_lo))
                                    e.matmul(out, wh, hi[:, k, :], start=begin and kk == 0 and f % 2 == 0,
                                             stop=False, skip_group_check=True)
                                    e.matmul(out, wh, lo[:, k, :], start=False, stop=False, skip_group_check=True)
                                    m = e.matmul(out, wl, hi[:, k, :], start=False, stop=end and kk == 1,
                                                 skip_group_check=True)
                        else:
                            for kk in range(2):
                                k = KT * n + 2 * j + kk
                                for t in range(NT):
                                    ah, al = (a[:, k, t * P:(t + 1) * P] for a in (hi, lo))
                                    out = bank[t][:, :]
                                    e.matmul(out, ah, w_hi[:, j, kk, :], start=begin and kk == 0, stop=False)
                                    e.matmul(out, ah, w_lo[:, j, kk, :], start=False, stop=False)
                                    m = e.matmul(out, al, w_hi[:, j, kk, :], start=False, stop=end and kk == 1)
                        m.then_inc(sem("group_done" if end else "mm_done"), 1)

            def product_pair(name, act, ready, before=({}, {})):
                g = number[name]
                hi, lo = act
                for n in range(2):
                    for j in range(PIECES):
                        if n == 0 and j % 2 == 0:
                            for b in range(2):
                                s, v = evac(g - 2 + j // 2, b)
                                e.wait_ge(s, v)
                        if j in before[n]:
                            before[n][j]()
                        c, part, bank = first_chunk[g] + n, 2 * n + j % 2, banks_of(g + j // 2)
                        e.wait_ge(*after(ready, part + 1))
                        e.wait_ge(*after("hi_ready", 4 * c + j + 1))
                        e.wait_ge(*after("lo_dve" if j % 2 == 0 else "lo_pool", 2 * c + j // 2 + 1))
                        begin, end = part == 0, part == 3
                        for kk in range(2):
                            k = 2 * part + kk
                            for t in range(NT):
                                ah, al = (a[:, k, t * P:(t + 1) * P] for a in (hi, lo))
                                out = bank[t][:, :]
                                e.matmul(out, ah, w_hi[:, j, kk, :], start=begin and kk == 0, stop=False)
                                e.matmul(out, ah, w_lo[:, j, kk, :], start=False, stop=False)
                                m = e.matmul(out, al, w_hi[:, j, kk, :], start=False, stop=end and kk == 1)
                        m.then_inc(sem("group_done" if end else "mm_done"), 1)

            def turn(key, src, done=None, banks=range(4)):
                for b in banks:
                    bank = take(b)
                    for kk in range(2):
                        for t in range(NT):
                            at = (kk * NT + t) * P
                            m = e.transpose(bank[:, at:at + P], src(t, 2 * b + kk), ident)
                    m.then_inc(after(key + "_T", 0)[0], 1)
                    freed[b] = (done or key + "_lo", b + 1 if done else 2 * (b + 1))

            def turn_x(key, last, n):
                for t in range(NT):
                    e.wait_ge(*evac(last - 1 + n, t))
                turn(key, lambda t, k: x[:, t, k * P:(k + 1) * P], banks=(2 * n, 2 * n + 1))

            def turn_mem(n):
                e.wait_ge(*after("mem_loaded", 16))
                turn("mem", lambda t, k: R(MEM + t * D + k * P, (1, P)), "mem_copy", (2 * n, 2 * n + 1))

            def rows(key, b):
                e.wait_ge(*after(key + "_rstd", 1))
                bank = take(b)
                for t in range(NT):
                    m = e.matmul(bank[:, t * P:(t + 1) * P], sm(key + "_r", 2)[:, t:t + 1].to_broadcast([P, P]), ident,
                                 start=True, stop=True)
                m.then_inc(after(key + "_rbcmm", 0)[0], 1)
                freed[b] = (key + "_rbc", 1)

            A, B = (a_hi, a_lo), (b_hi, b_lo)

            e.wait_ge(*after("const_loaded", 16))
            e.wait_ge(*after("prow_loaded", 16))
            e.transpose(take(0)[:, 0:NCOLS], prow[:], const[0:NCOLS, 0:NCOLS]).then_inc(sem("cols_T"), 1)
            freed[0] = ("cols_ready", 1)

            def turn_x0(n):
                e.wait_ge(*after(f"x_loaded{n}", 16))
                turn("n0", lambda t, k: x[:, t, k * P:(k + 1) * P], banks=(2 * n, 2 * n + 1))

            turn_x0(0)
            product("xbc0", A, "n0_lo", before={1: lambda: turn_x0(1)})
            rows("n0", 0)

            def dt_and_gate():
                e.wait_ge(*after("sw_lo", 1))
                bank = take(1)
                for t in range(NT):
                    for k in range(KT):
                        ah, al = (a[:, k, t * P:(t + 1) * P] for a in A)
                        out = bank[:, t * 32:(t + 1) * 32]
                        e.matmul(out, ah, sw_hi[:, k, :], start=k == 0, stop=False)
                        e.matmul(out, ah, sw_lo[:, k, :], start=False, stop=False)
                        m = e.matmul(out, al, sw_hi[:, k, :], start=False, stop=k == KT - 1)
                m.then_inc(sem("dg_mm"), 1)
                freed[1] = ("dg_copy", 1)

            def glr_turn():
                e.wait_ge(*after("dg_copy", 1))
                bank = take(1)
                for t in range(NT):
                    m = e.transpose(bank[0:RANK, t * P:(t + 1) * P], dgs[:, t, 16:32], ident)
                m.then_inc(sem("glr_T"), 1)
                freed[1] = ("glrt_ready", 1)

            def gate():
                e.wait_ge(*after("glrt_ready", 1))
                e.wait_ge(*after("w2g_loaded", 16))
                for t in range(NT):
                    e.matmul(take(2 + t)[:, :], glr_t[:, t * P:(t + 1) * P], w2g[:], start=True,
                             stop=True).then_inc(sem("g_mm"), 1)
                    freed[2 + t] = ("g_max", t + 1)

            product("xbc1", A, "n0_lo", before={1: dt_and_gate})
            product("xbc2", A, "n0_lo", before={1: glr_turn, 3: gate})

            la = sm("loga", 32)

            def cumulate():
                e.wait_ge(*after("loga", 1))
                bank = take(2)
                for t in range(NT):
                    e.matmul(bank[:, t * SH:(t + 1) * SH], tri, la[:, t * SH:(t + 1) * SH], start=True, stop=True)
                e.matmul(bank[:, 2 * SH:3 * SH], ones, la[:, 0:SH], start=True, stop=True).then_inc(sem("cum_mm"), 1)
                freed[2] = ("cum_ready", 1)

            def decay_rows(t):
                for b in range(4):
                    bank = take(b)
                    for i in range(4):
                        h = 4 * b + i
                        m = e.matmul(bank[:, i * P:(i + 1) * P],
                                     la[:, t * SH + h:t * SH + h + 1].to_broadcast([P, P]), tri, start=True, stop=True)
                    m.then_inc(sem("cumb_mm"), 1)
                    freed[b] = ("seg", 4 * t + b + 1)

            def ssd_turn():
                e.wait_ge(*after("conv_silu", 1))
                for b in range(4):
                    bank = take(b)
                    t, hh = b // 2, b % 2
                    for i in range(4):
                        m = e.transpose(bank[:, i * P:(i + 1) * P], R(CV + (4 * hh + i) * L + t * P, (1, P)), ident)
                    m.then_inc(sem("xs_T"), 1)
                    freed[b] = ("xs_ready", b + 1)

            def ssd_scores():
                for g in range(SG):
                    bank = take(g)
                    lo_, hi_ = g * SN, (g + 1) * SN
                    bt, ct = R(CV + 8 * L, (1, L)), R(CV + 9 * L, (1, L))
                    e.matmul(bank[:, 0:L], bt[lo_:hi_, 0:P], ct[lo_:hi_, :], start=True, stop=True)
                    e.matmul(bank[:, L:L + P], bt[lo_:hi_, P:L], ct[lo_:hi_, P:L], start=True,
                             stop=True).then_inc(sem("ssd_score"), 1)
                    freed[g] = ("ssd_g", 3 * (g + 1))

            def ssd_y(t):
                e.wait_ge(*after("ssd_m", 2 * (t + 1)))
                e.wait_ge(*after("xdt", 2))
                for b in range(2):
                    bank = take(2 * t + b)
                    for i in range(8):
                        h = 8 * b + i
                        m = e.matmul(bank[:, i * SP_:(i + 1) * SP_], R(MM + h * P, (1, P)),
                                     R(XDT + t * D + h * SP_, (1, SP_)), start=True, stop=True)
                    m.then_inc(sem("y_mm"), 1)
                    freed[2 * t + b] = ("y_add", 2 * t + b + 1)

            def ssd_cross():
                e.wait_ge(*after("wx", 1))
                for g in range(SG):
                    e.matmul(take(g)[:, :], R(GG + g * 384 + P, (1, P)), R(WX + g * 512, (1, 512)), start=True,
                             stop=True).then_inc(sem("yc_mm"), 1)
                    freed[g] = ("yc_scaled", g + 1)

            product("q0", A, "n0_lo", before={2: cumulate, 3: lambda: decay_rows(0)})
            product("k0", A, "n0_lo", before={1: lambda: turn_mem(0), 3: lambda: (turn_mem(1), rows("mem", 0))})
            product("z0", A, "n0_lo")
            product("z1", A, "n0_lo", before={1: ssd_turn, 2: ssd_scores})
            product("xk0_0", B, "mg0_lo", before={0: lambda: ssd_y(0), 1: lambda: decay_rows(1)})

            def gla_cumulate():
                e.wait_ge(*after("sp_ready", 2))
                for b in range(2):
                    bank = take(2 + b)
                    for i in range(2):
                        h = 2 * b + i
                        for t in range(NT):
                            at = (i * NT + t) * P
                            m = e.matmul(bank[:, at:at + P], sp[:, t, h * GK:(h + 1) * GK], tri, start=True, stop=True)
                    m.then_inc(sem("gcum_mm"), 1)
                    freed[2 + b] = ("gcum", b + 1)

            def gla_diagonal():
                for n in ("q0", "k0"):
                    for b in range(2):
                        e.wait_ge(*evac(number[n], b))
                for t in range(NT):
                    bank = take(t)
                    for h in range(GH):
                        at = h * L + t * P
                        m = e.matmul(bank[:, h * P:(h + 1) * P], R(QK + at, (1, P)), R(QK + 1024 + at, (1, P)),
                                     start=True, stop=True)
                    m.then_inc(sem("diag_mm"), 1)
                    freed[t] = ("gla_diag", t + 1)

            def level(n):
                buf = GXA if n % 2 == 0 else GXB
                e.wait_ge(*after("gx", n + 1))
                if n == 0:
                    bank = take(0)
                    for h in range(GH):
                        m = e.matmul(bank[:, h * P:(h + 1) * P], R(buf + h * L, (1, P)), R(buf + h * L + P, (1, P)),
                                     start=True, stop=True)
                    m.then_inc(sem("level_mm"), 1)
                    freed[0] = ("gla_cross", 1)
                    return
                for t in range(NT):
                    b = 2 * (n % 2) + t
                    bank = take(b)
                    for h in range(GH):
                        xx = R(buf + h * L + t * P, (1, P))
                        m = e.matmul(bank[:, h * P:(h + 1) * P], xx, xx, start=True, stop=True)
                    m.then_inc(sem("level_mm"), 1)
                    freed[b] = ("gla_s", 2 * (n - 1) + t + 1)

            def turn_y():
                e.wait_ge(*after("yn", 4))
                turn("y", lambda t, k: R(XS + t * D + k * P, (1, P)))

            product("xk0_1", B, "mg0_lo", before={1: lambda: ssd_y(1), 2: ssd_cross, 3: gla_cumulate})
            product("xv0_0", B, "mg0_lo", before={0: gla_diagonal})
            product("xv0_1", B, "mg0_lo", before={0: lambda: level(0), 2: lambda: level(1)})
            product("v0", A, "n0_lo", before={0: lambda: level(2), 2: lambda: level(3)})
            product("v1", A, "n0_lo", before={0: lambda: level(4), 2: lambda: level(5)})
            product("r0", A, "n0_lo", before={0: lambda: level(6), 2: lambda: level(7)})
            product("r1", A, "n0_lo", before={1: turn_y})

            def gla_out():
                for n in ("v0", "v1"):
                    for b in range(2):
                        e.wait_ge(*evac(number[n], b))
                e.wait_ge(*after("gla_s", 14))
                for t in range(NT):
                    for b in range(2):
                        bank = take(2 * t + b)
                        for i in range(2):
                            h = 2 * b + i
                            out = bank[:, i * GV:(i + 1) * GV]
                            m = e.matmul(out, R(STT_ + t * 512 + h * P, (1, P)), R(VV + t * D + h * GV, (1, GV)),
                                         start=True, stop=t == 0)
                            if t == 1:
                                m = e.matmul(out, R(SXT + h * P, (1, P)), R(VV + h * GV, (1, GV)), start=False,
                                             stop=True)
                        m.then_inc(sem("o_mm"), 1)
                        freed[2 * t + b] = ("on", 2 * (2 * t + b + 1))

            def turn_o():
                e.wait_ge(*after("on", 8))
                turn("o", lambda t, k: R(OO + t * D + k * P, (1, P)))

            product("outy0", B, "y_lo", before={0: gla_out})
            product("outy1", B, "y_lo", before={2: turn_o})
            product("outo0", A, "o_lo")
            product("outo1", A, "o_lo", before={1: lambda: turn_x("xn0", number["outo1"], 0)})

            def tail(l, one, two):
                def scores(hh):
                    for b in range(2):
                        e.wait_ge(*evac(number[f"xq{l}_{hh}"], b))
                    for t in range(NT):
                        bank = take(2 * hh + t)
                        for i in range(2):
                            h = 2 * hh + i
                            for dd in range(2):
                                m = e.matmul(bank[:, i * NM:(i + 1) * NM], R(CQ + (2 * h + dd) * L + t * P, (1, P)),
                                             xk[:, 2 * h + dd, :], start=dd == 0, stop=dd == 1)
                        m.then_inc(after(f"c{l}_score", 0)[0], 1)
                        freed[2 * hh + t] = (f"c{l}_exp", 4 * hh + 2 * (t + 1))

                def p_turn(hh):
                    e.wait_ge(*after(f"c{l}_p", 4 * (hh + 1)))
                    for mt in range(2):
                        bank = take(2 * hh + mt)
                        for i in range(2):
                            h = 2 * hh + i
                            for t in range(NT):
                                at = (i * NT + t) * P
                                m = e.transpose(bank[:, at:at + P], R(CP + (t * XH + h) * NM + mt * P, (1, P)), ident)
                        m.then_inc(after(f"c{l}_pT", 0)[0], 1)
                        freed[2 * hh + mt] = (f"c{l}_pt", 2 * hh + mt + 1)

                def values(hh):
                    e.wait_ge(*after(f"c{l}_pt", 2 * (hh + 1)))
                    for h in (2 * hh, 2 * hh + 1):
                        bank = take(h)
                        for vv in range(2):
                            for mt in range(2):
                                m = e.matmul(bank[:, vv * L:(vv + 1) * L],
                                             xv[:, mt, h * XHD + vv * P:h * XHD + (vv + 1) * P],
                                             R(CPT + (mt * XH + h) * L, (1, L)), start=mt == 0, stop=mt == 1)
                        m.then_inc(after(f"c{l}_T", 0)[0], 1)
                        freed[h] = (f"c{l}_lo", h + 1)

                product(f"xq{l}_0", one, f"xn{l}_lo",
                        before={1: lambda: turn_x(f"xn{l}", number["outo1" if l == 0 else "dout1"], 1)})
                product(f"xq{l}_1", one, f"xn{l}_lo", before={1: lambda: scores(0), 3: lambda: p_turn(0)})
                values(0)
                scores(1)
                product_pair(f"xo{l}_0", two, f"c{l}_lo", ({2: lambda: p_turn(1), 3: lambda: values(1)},
                                                          {3: lambda: turn_x(f"mn{l}", number[f"xo{l}_1"], 0)}))
                product(f"up{l}_0", one, f"mn{l}_lo", before={1: lambda: turn_x(f"mn{l}", number[f"xo{l}_1"], 1)})
                for n in range(1, 8):
                    product(f"up{l}_{n}", one, f"mn{l}_lo")
                product(f"down{l}_0", (hid_hi, hid_lo), f"hid{l}", 1)
                product(f"down{l}_1", (hid_hi, hid_lo), f"hid{l}", 1,
                        before={1: lambda: turn_x("n1", number["down0_1"], 0)} if l == 0 else {})

            tail(0, B, A)

            def diff_scores(r):
                t, per, first = ROUNDS[r]
                keys = (t + 1) * P
                for n in (("dq0", "dk0"), ("dq1", "dk1"), ())[r]:
                    for b in range(2):
                        e.wait_ge(*evac(number[n], b))
                for pair in range(2):
                    bank = [take(2 * pair + m_) for m_ in range(2)]
                    for i in range(per):
                        h = first + per * pair + i
                        for m_ in range(2):
                            q = R(DQ + h * L + t * P, (1, P))[m_ * DHD:(m_ + 1) * DHD, :]
                            k = R(DK + h * L, (1, keys))[m_ * DHD:(m_ + 1) * DHD, :]
                            m = e.matmul(bank[m_][:, i * keys:(i + 1) * keys], q, k, start=True, stop=True)
                            if i == per - 1:
                                m.then_inc(sem("d_score"), 1)
                    for b in (2 * pair, 2 * pair + 1):
                        freed[b] = ("d_bias", 4 * r + b + 1)

            def diff_turn(r):
                e.wait_ge(*after("d_an", (4, 12, 16)[r]))
                for b in range(2):
                    bank = take(b)
                    for i in range(4):
                        n = 4 * b + i
                        m = e.transpose(bank[:, i * P:(i + 1) * P], R(AN + n * P, (1, P)), ident)
                    m.then_inc(sem("d_anT"), 1)
                    freed[b] = ("d_at", 2 * r + b + 1)

            def diff_out():
                for n in ("dv0", "dv1"):
                    for b in range(2):
                        e.wait_ge(*evac(number[n], b))
                e.wait_ge(*after("d_at", 6))
                for t in range(NT):
                    for b in range(2):
                        bank = take(2 * t + b)
                        for i in range(4):
                            h = 4 * b + i
                            for s in range(t + 1):
                                slot = AT_TILE0 + h if t == 0 else (2 * h + s if h < 4 else 8 + 2 * h + s)
                                m = e.matmul(bank[:, i * P:(i + 1) * P], R(AT + slot * P, (1, P)),
                                             R(DV + s * D + h * P, (1, P)), start=s == 0, stop=s == t)
                        m.then_inc(sem("do_mm"), 1)
                        freed[2 * t + b] = ("d_on", 2 * t + b + 1)

            def turn_d():
                e.wait_ge(*after("d_on", 4))
                turn("d", lambda t, k: R(SC + t * D + k * P, (1, P)))

            product("dq0", A, "n1_lo", before={1: lambda: turn_x("n1", number["down0_1"], 1)})
            product("dk0", A, "n1_lo", before={2: lambda: rows("n1", 2)})
            product("dq1", A, "n1_lo", before={1: lambda: diff_scores(0)})
            product("dk1", A, "n1_lo", before={2: lambda: diff_turn(0)})
            product("dv0", A, "n1_lo", before={1: lambda: diff_scores(1)})
            product("dv1", A, "n1_lo", before={3: lambda: diff_turn(1)})
            product("xk1_0", B, "mg1_lo", before={0: lambda: diff_scores(2)})
            product("xk1_1", B, "mg1_lo", before={1: lambda: diff_turn(2), 2: diff_out})
            product("xv1_0", B, "mg1_lo")
            product("xv1_1", B, "mg1_lo", before={1: turn_d})
            product("dout0", A, "d_lo")
            product("dout1", A, "d_lo", before={1: lambda: turn_x("xn1", number["dout1"], 0)})
            tail(1, B, A)

        @block.scalar
        def _(e):
            op, settle, link = tracker(e, "act_step")

            def split(c, before={}):
                for j in range(PIECES):
                    if j in before:
                        before[j]()
                    if c >= len(chunks):
                        continue
                    width = chunks[c][3]
                    e.wait_ge(sem(f"raw_ready{j}"), 16 * (c + 1))
                    if c > 0:
                        piece_free(e, c - 1, j)
                    op(e.activation(w_hi[:, j, :, 0:width], raw[:, j, :, 0:width], ACT.Copy), "hi_ready")
                if PIECES in before:
                    before[PIECES]()

            def ahead(name, before={}):
                g = number[name]
                n = len(groups[g][2])
                for i in range(n):
                    split(first_chunk[g] + i + 1, before if i == n - 1 else {})
                return g

            def done(g):
                e.wait_ge(*after("group_done", g + 1))

            def copy0(name, dst, scale=1.0, before={}):
                g = ahead(name, before)
                done(g)
                s, v = evac(g, 0)
                op(e.activation(dst, bank_view(g, 0, dst), ACT.Copy, scale=scale), s.name, v)

            def sumsq(key, srcs):
                ss = sm(key + "_ss", 4)
                for n, src, ready in srcs:
                    if ready:
                        e.wait_ge(*ready)
                    width = src.shape[-1]
                    link(e.activation(junk[:].rearrange("p a b -> p (a b)")[:, 0:width], src, ACT.Square,
                                      accum_out=ss[:, n:n + 1]), key + "_sq")

            def hi_parts(key, act, gain, banks=range(4)):
                for b in banks:
                    e.wait_ge(*after(key + "_T", b + 1))
                    for kk in range(2):
                        k = 2 * b + kk
                        op(e.activation(act[:, k, :], X_[b][:, kk * L:(kk + 1) * L], ACT.Copy, scale=gain(k)),
                           key + "_hi")

            def squares_x(key, last, n):
                sumsq(key, [(2 * n + t, x[:, t, n * 512:(n + 1) * 512], evac(last - 1 + n, t)) for t in range(NT)])

            def mem_hi(l):
                for k in range(KT):
                    if l == 0:
                        e.wait_ge(*after("mem_copy", k // 2 + 1))
                    op(e.activation(b_hi[:, k, :], mem_t[:, k, :], ACT.Copy, scale=col(f"mem{l}", k)), f"mg{l}_hi")

            e.wait_ge(*after("cols_T", 1))
            link(e.activation(cols[:], X_[0][:, 0:NCOLS], ACT.Copy), "cols_ready")
            hi_parts("n0", a_hi, lambda k: col("ev", k), (0, 1))
            split(0, {2: lambda: hi_parts("n0", a_hi, lambda k: col("ev", k), (2, 3))})
            ss = sm("n0_ss", 4)
            sumsq("n0", [(2 * n + t, x[:, t, n * 512:(n + 1) * 512], None) for n in range(2) for t in range(NT)])
            e.wait_ge(*after("sw_loaded", 16))
            op(e.activation(sw_hi[:], sw[:], ACT.Copy), "sw_hi")
            e.wait_ge(*after("row_loaded", 16))
            op(e.activation(sm("ea", 16), row[:, 16:32], ACT.Exp), "ea")
            e.wait_ge(*after("mem_loaded", 16))
            ahead("xbc0")
            sumsq("mem", [(2 * n + t, R(MEM + t * D + n * 512, (1, 512)), None) for n in range(2) for t in range(NT)])

            def dg_copy():
                e.wait_ge(*after("dg_mm", 1))
                for t in range(NT):
                    ins = e.activation(dgs[:, t, :], X_[1][:, t * 32:(t + 1) * 32], ACT.Copy,
                                       scale=sm("n0_r", 2)[:, t:t + 1])
                    op(ins, "dg_part" if t == 0 else "dg_copy")

            def glrt_copy():
                e.wait_ge(*after("glr_T", 1))
                op(e.activation(glr_t[0:RANK, :], X_[1][0:RANK, 0:L], ACT.Copy), "glrt_ready")
                e.wait_ge(*after("dt_na", 1))
                op(e.activation(sm("dt_u", 32), sm("dt_n", 32), ACT.Exp), "dt_u")

            e.wait_ge(*after("n0_rstd", 1))
            ahead("xbc1", {2: dg_copy})
            ahead("xbc2", {2: glrt_copy})
            for t in range(NT):
                e.wait_ge(*after("g_mm", t + 1))
                link(e.activation(junk[:, t, :], X_[2 + t][:, :], ACT.Abs), "g_abs")
            link(e.activation(junk[:], junk[:], ACT.Exp, scale=-1.0))
            op(e.activation(junk[:], junk[:], ACT.Ln, bias=1.0), "g_ln")

            def decay_factors():
                e.wait_ge(*after("cum_ready", 2))
                op(e.activation(sm("wts", 16), sm("wts", 16), ACT.Exp), "wts")
                op(e.activation(sm("e1", 16), sm("cc", 48)[:, 16:32], ACT.Exp), "e1")

            def ssd_exp(t):
                e.wait_ge(*after("seg_min", t + 1))
                link(e.activation(R(MM, (1, 2048)), R(MM, (1, 2048)), ACT.Exp), "ssd_exp")

            def tanh_gate(name, n, base, before={}):
                g = ahead(f"{name}{n}", before)
                done(g)
                for t in range(NT):
                    op(e.activation(R(base + t * D + n * 512, (1, 512)), banks_of(g)[t][:, :], ACT.Tanh,
                                    scale=sm("n0_hr", 2)[:, t:t + 1]), name + "_tanh")

            def conv_first(cs):
                for n in ("xbc0", "xbc1"):
                    for b in range(2):
                        e.wait_ge(*evac(number[n], b))
                e.wait_ge(*evac(number["xbc2"], 0))
                e.wait_ge(*after("half", 1))
                for c in cs:
                    op(e.activation(R(CV + c * L, (1, L)), R(XB + c * XBW, (1, L)), ACT.Identity,
                                    bias=half[:, 40 + c:41 + c], scale=half[:, c:c + 1]), "conv_first")

            def mem_copy(bs):
                for b in bs:
                    e.wait_ge(*after("mem_T", b + 1))
                    op(e.activation(mem_t[:, 2 * b:2 * b + 2, :], X_[b][:, :].rearrange("p (a b) -> p a b", a=2),
                                    ACT.Copy), "mem_copy")

            ahead("q0", {0: lambda: conv_first(range(5)), 1: lambda: conv_first(range(5, XT)), 3: decay_factors})
            ahead("k0", {0: lambda: ssd_exp(0), 1: lambda: mem_copy((0, 1)), 3: lambda: mem_copy((2, 3))})
            mem_hi(0)
            def conv_tanh():
                e.wait_ge(*after("conv", 10))
                op(e.activation(R(TT, (1, XT * L)), R(CV, (1, XT * L)), ACT.Tanh), "conv_tanh")

            tanh_gate("z", 0, ZZ, {2: conv_tanh})

            def xs_copy():
                for b in range(4):
                    e.wait_ge(*after("xs_T", b + 1))
                    op(e.activation(R(XS + b * 512, (1, 512)), X_[b][:, :], ACT.Copy), "xs_ready")

            tanh_gate("z", 1, ZZ, {1: xs_copy})
            ahead("xk0_0", {2: lambda: ssd_exp(1)})
            ahead("xk0_1")

            def neg_cum():
                e.wait_ge(*after("gcum", 2))
                op(e.activation(R(CC2, (1, 1024)), R(CC2 + 1024, (1, 1024)), ACT.Copy, scale=-1.0), "gneg")

            def gla_exp(n):
                buf = GXA if n % 2 == 0 else GXB
                e.wait_ge(*after("gd", n + 1))
                if n == 0:
                    op(e.activation(R(buf + P, (L, GH), (1, P)), R(CC2 + 1024 + P, (L, GH), (1, P)), ACT.Exp))
                    link(e.activation(R(buf, (L, GH), (1, P)), R(buf, (L, GH), (1, P)), ACT.Exp), "ge")
                else:
                    link(e.activation(R(buf, (1, 1024)), R(buf, (1, 1024)), ACT.Exp), "ge")

            def y_squares():
                e.wait_ge(*after("yz", 2))
                sumsq("y", [(2 * t + g, R(XS + t * D + g * 512, (1, 512)), None) for t in range(NT) for g in range(SG)])

            rm = sm("mem_r", 2)
            copy0("xv0_0", xv[:, 0, 0:512], rm[:, 0:1],
                  {0: neg_cum, 1: lambda: gla_exp(0), 2: y_squares, 3: lambda: gla_exp(1)})

            copy0("xv0_1", xv[:, 0, 512:1024], rm[:, 0:1], {1: lambda: gla_exp(2), 3: lambda: gla_exp(3)})
            rx = sm("n0_r", 2)
            copy0("v0", R(VV, (1, 512)), rx[:, 0:1], {1: lambda: gla_exp(4), 3: lambda: gla_exp(5)})
            copy0("v1", R(VV + 512, (1, 512)), rx[:, 0:1], {1: lambda: gla_exp(6), 3: lambda: gla_exp(7)})
            tanh_gate("r", 0, RR)
            tanh_gate("r", 1, RR, {1: lambda: hi_parts("y", b_hi, lambda k: col("ssdn", k))})

            def o_squares():
                ss = sm("o_ss", 8)
                for b in range(4):
                    e.wait_ge(*after("o_mm", b + 1))
                    for i in range(2):
                        link(e.activation(junk[:, 0, 0:GV], X_[b][:, i * GV:(i + 1) * GV], ACT.Square,
                                          accum_out=ss[:, 2 * b + i:2 * b + i + 1]), "o_sq")

            ahead("outy0", {0: o_squares})
            ahead("outy1", {2: lambda: hi_parts("o", a_hi, lambda k: col("glan", k % 2))})
            ahead("outo0")

            def half_ready(key, last, dst, gain):
                def f():
                    hi_parts(key, dst, gain, (0, 1))
                    squares_x(key, last, 0)
                return f

            ahead("outo1", {1: half_ready("xn0", number["outo1"], b_hi, lambda k: col("xa0", k))})

            def rest(key, last, dst, gain):
                hi_parts(key, dst, gain, (2, 3))
                squares_x(key, last, 1)

            def tail(l, one, two):
                rest(f"xn{l}", number["outo1" if l == 0 else "dout1"], one[0], lambda k: col(f"xa{l}", k))
                rs = sm(f"c{l}_sum", 8)

                def exps(hh):
                    for t in range(NT):
                        e.wait_ge(*after(f"c{l}_max", 2 * hh + t + 1))
                        for i in range(2):
                            n = t * XH + 2 * hh + i
                            op(e.activation(R(CP + n * NM, (1, NM)), X_[2 * hh + t][:, i * NM:(i + 1) * NM], ACT.Exp,
                                            bias=sm(f"c{l}_nmax", 8)[:, n:n + 1], scale=sm(f"xn{l}_s", 2)[:, t:t + 1],
                                            accum_out=rs[:, n:n + 1]), f"c{l}_exp")

                def pt_copy(hh):
                    for mt in range(2):
                        e.wait_ge(*after(f"c{l}_pT", 2 * hh + mt + 1))
                        op(e.activation(R(CPT + (mt * XH + 2 * hh) * L, (1, 512)), X_[2 * hh + mt][:, :], ACT.Copy),
                           f"c{l}_pt")

                def o_hi(hh):
                    for h in (2 * hh, 2 * hh + 1):
                        e.wait_ge(*after(f"c{l}_T", h + 1))
                        op(e.activation(two[0][:, 2 * h:2 * h + 2, :], X_[h][:, :].rearrange("p (a b) -> p a b", a=2),
                                        ACT.Copy), f"c{l}_hi")

                copy0(f"xq{l}_0", R(CQ, (L, 2), (1, L)))
                copy0(f"xq{l}_1", R(CQ + 4 * L, (L, 2), (1, L)), 1.0, {1: lambda: exps(0), 3: lambda: pt_copy(0)})
                o_hi(0)
                exps(1)
                ahead(f"xo{l}_0", {2: lambda: pt_copy(1), 3: lambda: o_hi(1)})
                ahead(f"xo{l}_1", {3: half_ready(f"mn{l}", number[f"xo{l}_1"], one[0], lambda k: col(f"mlp{l}", k))})
                rest(f"mn{l}", number[f"xo{l}_1"], one[0], lambda k: col(f"mlp{l}", k))
                for n in range(8):
                    g = ahead(f"up{l}_{n}")
                    done(g)
                    for b in range(2):
                        if n > 0:
                            e.wait_ge(*after("hid_sq", 16 * l + 2 * n + b - 1))
                        s, v = evac(g, b)
                        op(e.activation(junk[:, b, :], banks_of(g)[b][:, :], ACT.Relu), s.name, v)
                    for b in range(2):
                        e.wait_ge(*after("hid_sq", 16 * l + 2 * n + b + 1))
                        op(e.activation(hid_hi[:, 4 * n + 2 * b:4 * n + 2 * b + 2, :],
                                        sp[:, b, :].rearrange("p (a c) -> p a c", a=2), ACT.Copy), "hid_hi")
                ahead(f"down{l}_0")
                if l == 0:
                    ahead("down0_1", {1: half_ready("n1", number["down0_1"], a_hi, lambda k: col("od", k))})
                else:
                    ahead("down1_1", {3: lambda: squares_x("fin", number["down1_1"], 0)})

            tail(0, (b_hi, b_lo), (a_hi, a_lo))

            rest("n1", number["down0_1"], a_hi, lambda k: col("od", k))

            def lam_exp():
                e.wait_ge(*after("lam_dot", 1))
                op(e.activation(sm("lam_e", 2), sm("lam_d", 2), ACT.Exp), "lam_e")

            def diff_exp(r, part):
                t, per, _ = ROUNDS[r]
                keys = (t + 1) * P
                at = (0, 8, 24)[r]
                e.wait_ge(*after("d_max", r + 1))
                base = SC + 2048 * (r % 2)
                for n in range(2 * per * part, 2 * per * (part + 1)):
                    v = R(base + n * keys, (1, keys))
                    op(e.activation(v, v, ACT.Exp, bias=sm("d_nmax", 32)[:, at + n:at + n + 1],
                                    accum_out=sm("d_sum", 32)[:, at + n:at + n + 1]), "d_exp")

            def at_copy(r):
                for b in range(2):
                    e.wait_ge(*after("d_anT", 2 * r + b + 1))
                    op(e.activation(R(AT + (2 * r + b) * 512, (1, 512)), X_[b][:, :], ACT.Copy), "d_at")

            r1 = sm("n1_r", 2)
            copy0("dq0", R(DQ, (L, 2), (1, L)), DHD ** -0.5, {2: lam_exp})
            ahead("dk0")
            copy0("dq1", R(DQ + 4 * L, (L, 2), (1, L)), DHD ** -0.5, {2: lambda: diff_exp(0, 0), 3: lambda: diff_exp(0, 1)})
            ahead("dk1", {1: lambda: mem_hi(1), 2: lambda: at_copy(0)})
            copy0("dv0", R(DV, (1, 512)), r1[:, 0:1], {2: lambda: diff_exp(1, 0), 3: lambda: diff_exp(1, 1)})
            copy0("dv1", R(DV + 512, (1, 512)), r1[:, 0:1], {3: lambda: at_copy(1)})
            ahead("xk1_0", {1: lambda: diff_exp(2, 0), 2: lambda: diff_exp(2, 1)})

            def do_squares():
                for b in range(4):
                    e.wait_ge(*after("do_mm", b + 1))
                    if b >= 2:
                        e.wait_ge(*after("do_sum", b - 1))
                    op(e.activation(junk[:, b % 2, :], X_[b][:, :], ACT.Square), "do_sq")

            ahead("xk1_1", {1: lambda: at_copy(2), 2: do_squares})
            copy0("xv1_0", xv[:, 0, 0:512], rm[:, 0:1])
            copy0("xv1_1", xv[:, 0, 512:1024], rm[:, 0:1], {1: lambda: hi_parts("d", a_hi, lambda k: col("subln"))})
            ahead("dout0")
            ahead("dout1", {1: half_ready("xn1", number["dout1"], b_hi, lambda k: col("xa1", k))})
            tail(1, (b_hi, b_lo), (a_hi, a_lo))
            squares_x("fin", number["down1_1"], 1)
            e.wait_ge(*after("fin_rstd", 1))
            e.wait_ge(*after("fin_gain", 4))
            for n in range(2):
                v = result(1, n)
                op(e.activation(v, v, ACT.Copy, scale=sm("fin_r", 2)[:, 1:2]), "final1")

        @block.vector
        def _(e):
            op, settle, link = tracker(e, "dve_step")

            def split(c, before={}):
                for j in range(PIECES):
                    if j in before:
                        before[j]()
                    if c >= len(chunks) or j % 2:
                        continue
                    width = chunks[c][3]
                    e.wait_ge(*after("hi_ready", 4 * c + j + 1))
                    op(e.tensor_tensor(w_lo[:, j, :, 0:width], raw[:, j, :, 0:width],
                                       w_hi[:, j, :, 0:width].bitcast(F32), ALU.subtract), "lo_dve")
                if PIECES in before:
                    before[PIECES]()

            def ahead(name, before={}):
                g = number[name]
                n = len(groups[g][2])
                for i in range(n):
                    split(first_chunk[g] + i + 1, before if i == n - 1 else {})
                return g

            def done(g):
                e.wait_ge(*after("group_done", g + 1))

            def copy1(name, dst, scale=None, before={}):
                g = ahead(name, before)
                done(g)
                s, v = evac(g, 1)
                src = bank_view(g, 1, dst)
                if scale is None:
                    op(e.tensor_copy(dst, src), s.name, v)
                else:
                    op(e.tensor_scalar(dst, src, scale, None, ALU.mult), s.name, v)

            def by_rows(name, dsts, key, scale=1.0, before={}):
                g = ahead(name, before)
                done(g)
                e.wait_ge(*after(key + "_rbc", 1))
                r = rbc[key][:].unsqueeze(1).to_broadcast([P, 2, L])
                for b, dst in enumerate(dsts):
                    s, v = evac(g, b)
                    op(e.scalar_tensor_tensor(out=dst, in0=bank_view(g, b, dst), scalar=scale, in1=r, op0=ALU.mult,
                                              op1=ALU.mult), s.name, v)

            def add_x(name, n, scale=None, before={}):
                add_bank(ahead(name, before), n, scale)

            def add_bank(g, n, scale=None):
                done(g)
                for t in range(NT):
                    s, v = evac(g, t)
                    xx = x[:, t, n * 512:(n + 1) * 512]
                    if scale is None:
                        op(e.tensor_tensor(xx, xx, banks_of(g)[t][:, :], ALU.add), s.name, v)
                    else:
                        op(e.scalar_tensor_tensor(out=xx, in0=banks_of(g)[t][:, :], scalar=scale[:, t:t + 1], in1=xx,
                                                  op0=ALU.mult, op1=ALU.add), s.name, v)

            def lo_parts(key, act, gain, banks=range(4)):
                for b in banks:
                    e.wait_ge(*after(key + "_hi", 2 * (b + 1)))
                    for kk in range(2):
                        k = 2 * b + kk
                        op(e.scalar_tensor_tensor(out=act[1][:, k, :], in0=X_[b][:, kk * L:(kk + 1) * L],
                                                  scalar=gain(k), in1=act[0][:, k, :].bitcast(F32), op0=ALU.mult,
                                                  op1=ALU.subtract), key + "_lo")

            def row_copy(key, b):
                e.wait_ge(*after(key + "_rbcmm", 1))
                link(e.tensor_copy(rbc[key][:], X_[b][:, 0:L]), key + "_rbc")

            def mem_lo(l):
                for k in range(KT):
                    e.wait_ge(*after(f"mg{l}_hi", k + 1))
                    op(e.scalar_tensor_tensor(out=b_lo[:, k, :], in0=mem_t[:, k, :], scalar=col(f"mem{l}", k),
                                              in1=b_hi[:, k, :].bitcast(F32), op0=ALU.mult, op1=ALU.subtract),
                       f"mg{l}_lo")

            A, B = (a_hi, a_lo), (b_hi, b_lo)
            lo_parts("n0", A, lambda k: col("ev", k), (0, 1))
            split(0, {2: lambda: lo_parts("n0", A, lambda k: col("ev", k), (2, 3))})
            op(e.tensor_scalar(half[:], cols[:, COLS["convw"]:COLS["convw"] + 50], 0.5, None, ALU.mult), "half")
            e.wait_ge(*after("sw_hi", 1))
            op(e.tensor_tensor(sw_lo[:], sw[:], sw_hi[:].bitcast(F32), ALU.subtract), "sw_lo")
            ahead("xbc0")
            row_copy("n0", 0)

            def xb(c):
                return R(XB + c * XBW + 3, (XBW, 2), (1, L))

            def evac_rows(name, dsts, key):
                g = number[name]
                done(g)
                r = rbc[key][:].unsqueeze(1).to_broadcast([P, 2, L])
                for b, dst in enumerate(dsts):
                    s, v = evac(g, b)
                    op(e.tensor_tensor(dst, bank_view(g, b, dst), r, ALU.mult), s.name, v)

            e.wait_ge(*after("pad_ready", 1))
            evac_rows("xbc0", (xb(0), xb(2)), "n0")
            by_rows("xbc1", (xb(4), xb(6)), "n0")

            v, n_, u, s1, s2, pp = (sm(k, 32) for k in ("dt_v", "dt_n", "dt_u", "dt_s", "dt_s2", "dt_p"))
            dtb = row[:, 0:16].unsqueeze(1).to_broadcast([P, NT, 16])
            dt = sm("dt", 32)

            def two(a):
                return a.rearrange("p (t h) -> p t h", t=NT)

            def dt_start():
                e.wait_ge(*after("dg_copy", 1))
                link(e.tensor_tensor(two(v), dgs[:, :, 0:16], dtb, ALU.add))
                link(e.scalar_tensor_tensor(out=n_, in0=v, scalar=-1.0, in1=v, op0=ALU.mult, op1=ALU.min), "dt_na")

            g = ahead("xbc2", {0: dt_start})
            done(g)
            s, n = evac(g, 0)
            dst = R(XB + 8 * XBW + 3, (XBW, 2), (1, L))
            op(e.tensor_tensor(dst, bank_view(g, 0, dst), rbc["n0"][:].unsqueeze(1).to_broadcast([P, 2, L]), ALU.mult),
               s.name, n)
            op(e.memset(sm("spare", 1), 0.0), evac(g, 1)[0].name, evac(g, 1)[1])
            e.wait_ge(*after("dt_u", 1))
            link(e.tensor_scalar(s1, u, 2.0, None, ALU.add))
            link(e.reciprocal(s2, s1))
            link(e.tensor_tensor(s1, u, s2, ALU.mult))
            link(e.tensor_tensor(s2, s1, s1, ALU.mult))
            link(e.tensor_scalar(pp, s2, 1.0 / 17, None, ALU.mult))
            for k in (15, 13, 11, 9, 7, 5, 3):
                link(e.scalar_tensor_tensor(out=pp, in0=pp, scalar=1.0 / k, in1=s2, op0=ALU.add, op1=ALU.mult))
            link(e.scalar_tensor_tensor(out=pp, in0=pp, scalar=1.0, in1=s1, op0=ALU.add, op1=ALU.mult))
            link(e.tensor_scalar(v, v, 0.0, None, ALU.max))
            link(e.scalar_tensor_tensor(out=dt, in0=pp, scalar=2.0, in1=v, op0=ALU.mult, op1=ALU.add))
            e.wait_ge(*after("ea", 1))
            ea = sm("ea", 16).unsqueeze(1).to_broadcast([P, NT, 16])
            link(e.tensor_tensor(two(pp), two(dt), ea, ALU.mult))
            link(e.tensor_scalar(sm("loga", 32), pp, -1.0, None, ALU.mult), "loga")
            for t in range(NT):
                e.wait_ge(*after("g_abs", t + 1))
                op(e.tensor_scalar(sp[:, t, :], X_[2 + t][:, :], -1.0, 0.0, ALU.mult, ALU.max), "g_max")

            def tap(j, c):
                return half[:, j * XT + c:j * XT + c + 1]

            def conv(j):
                settle()
                for c in range(XT):
                    if j == 1:
                        e.wait_ge(*after("conv_first", c + 1))
                    dst = R(CV + c * L, (1, L))
                    op(e.scalar_tensor_tensor(out=dst, in0=R(XB + c * XBW + j, (1, L)), scalar=tap(j, c), in1=dst,
                                              op0=ALU.mult, op1=ALU.add), "conv" if j == TAPS - 1 else None)

            cc = sm("cc", 48)

            def cum_copy():
                e.wait_ge(*after("cum_mm", 1))
                link(e.tensor_copy(cc, X_[2][:, 0:48]), "cum_ready")
                link(e.tensor_tensor(sm("wts", 16), cc[:, 32:48], cc[:, 0:16], ALU.subtract), "cum_ready")

            def heads(ap, n=SP_):
                return ap.unsqueeze(2).to_broadcast([P, ap.shape[1], n])

            def decay(t):
                for b in range(4):
                    e.wait_ge(*after("cumb_mm", 4 * t + b + 1))
                    op(e.tensor_tensor(R(MM + b * 512, (P, 4), (1, P)), X_[b][:, :].rearrange("p (h q) -> p h q", h=4),
                                       heads(cc[:, t * SH + 4 * b:t * SH + 4 * b + 4], P), ALU.subtract), "seg")
                settle()
                link(e.tensor_scalar(R(MM, (1, 2048)), R(MM, (1, 2048)), 0.0, None, ALU.min), "seg_min")

            def weigh(t):
                e.wait_ge(*after("ssd_exp", t + 1))
                for g in range(SG):
                    m = R(MM + g * 1024, (P, 8), (1, P))
                    op(e.tensor_tensor(m, m, R(GG + g * 384 + 2 * P * t, (0, 8), (1, P)), ALU.mult), "ssd_m")

            def soft_gate():
                e.wait_ge(*after("g_ln", 1))
                for t in range(NT):
                    op(e.tensor_tensor(sp[:, t, :], sp[:, t, :], junk[:, t, :], ALU.add), "sp_ready")

            qk_rows = lambda base: (R(base, (L, 2), (1, L)), R(base + 512, (L, 2), (1, L)))
            by_rows("q0", qk_rows(QK + 1024), "n0", GK ** -0.5,
                    {2: lambda: (cum_copy(), conv(1)), 3: lambda: decay(0)})
            by_rows("k0", qk_rows(QK), "n0", 1.0,
                    {0: lambda: conv(2), 1: soft_gate, 3: lambda: (conv(3), row_copy("mem", 0))})

            def gated(name, n, base, before={}):
                g = ahead(f"{name}{n}", before)
                for t in range(NT):
                    e.wait_ge(*after(name + "_tanh", 2 * n + t + 1))
                    s, v = evac(g, t)
                    dst = R(base + t * D + n * 512, (1, 512))
                    op(e.scalar_tensor_tensor(out=dst, in0=dst, scalar=1.0, in1=banks_of(g)[t][:, :], op0=ALU.add,
                                              op1=ALU.mult), s.name, v)

            def conv_silu():
                e.wait_ge(*after("conv_tanh", 1))
                link(e.scalar_tensor_tensor(out=R(CV, (1, XT * L)), in0=R(TT, (1, XT * L)), scalar=1.0,
                                            in1=R(CV, (1, XT * L)), op0=ALU.add, op1=ALU.mult), "conv_silu")

            gated("z", 0, ZZ, {1: lambda: mem_lo(0), 3: conv_silu})

            def ssd_g():
                for g in range(SG):
                    e.wait_ge(*after("ssd_score", g + 1))
                    G = GG + g * 384
                    op(e.tensor_tensor(R(G, (1, P)), X_[g][:, 0:P], tri, ALU.mult), "ssd_g")
                    op(e.tensor_copy(R(G + P, (1, P)), X_[g][:, P:2 * P]), "ssd_g")
                    op(e.tensor_tensor(R(G + 2 * P, (1, P)), X_[g][:, 2 * P:3 * P], tri, ALU.mult), "ssd_g")
                settle()
                weigh(0)

            def xdt():
                for t in range(NT):
                    e.wait_ge(*after("xs_ready", 2 * (t + 1)))
                    op(e.tensor_tensor(R(XDT + t * D, (SP_, SH), (1, SP_)), R(XS + t * D, (SP_, SH), (1, SP_)),
                                       heads(dt[:, t * SH:(t + 1) * SH]), ALU.mult), "xdt")

            def skip():
                settle()
                for t in range(NT):
                    op(e.tensor_tensor(R(XS + t * D, (SP_, SH), (1, SP_)), R(XS + t * D, (SP_, SH), (1, SP_)),
                                       heads(row[:, 32:48]), ALU.mult))
                settle()

            gated("z", 1, ZZ, {2: lambda: (xdt(), skip(), ssd_g())})

            def y_add(t):
                for b in range(2):
                    e.wait_ge(*after("y_mm", 2 * t + b + 1))
                    y = R(XS + t * D + b * 512, (1, 512))
                    op(e.tensor_tensor(y, y, X_[2 * t + b][:, :], ALU.add), "y_add")

            def wx():
                e.wait_ge(*after("wts", 1))
                op(e.tensor_tensor(R(WX, (SP_, SH), (1, SP_)), R(XDT, (SP_, SH), (1, SP_)), heads(sm("wts", 16)),
                                   ALU.mult), "wx")

            by_rows("xk0_0", (xk[:, 0:2, :], xk[:, 2:4, :]), "mem", 1.0,
                    {0: lambda: y_add(0), 1: lambda: decay(1), 2: wx, 3: lambda: weigh(1)})

            def y_cross():
                e.wait_ge(*after("e1", 1))
                for g in range(SG):
                    e.wait_ge(*after("yc_mm", g + 1))
                    op(e.tensor_tensor(R(YC + g * 512, (SP_, 8), (1, SP_)),
                                       X_[g][:, :].rearrange("p (h q) -> p h q", h=8),
                                       heads(sm("e1", 16)[:, 8 * g:8 * g + 8]), ALU.mult), "yc_scaled")
                settle()
                link(e.tensor_tensor(R(XS + D, (1, D)), R(XS + D, (1, D)), R(YC, (1, D)), ALU.add))

            def gla_cum():
                for b in range(2):
                    e.wait_ge(*after("gcum_mm", b + 1))
                    op(e.tensor_scalar(R(CC2 + 1024 + b * 512, (1, 512)), X_[2 + b][:, :], -1.0 / TAU, None, ALU.mult),
                       "gcum")

            def gla_diag():
                for t in range(NT):
                    e.wait_ge(*after("diag_mm", t + 1))
                    op(e.tensor_tensor(R(STT_ + t * 512, (P, GH), (1, P)),
                                       X_[t][:, :].rearrange("p (h q) -> p h q", h=4),
                                       ident.unsqueeze(1).to_broadcast([P, GH, P]), ALU.mult), "gla_diag")

            def diff(n):
                buf = GXA if n % 2 == 0 else GXB
                if n >= 2:
                    e.wait_ge(*after("level_mm", 2 * (n - 2) + 1))
                if n == 0:
                    e.wait_ge(*after("gneg", 1))
                    op(e.tensor_tensor(R(buf, (L, GH), (1, P)), R(CC2, (L, GH), (1, P)), R(CC2 + P - 1, (L, GH), (0, P)),
                                       ALU.subtract), "gd")
                else:
                    b = LEVELS[n - 1]
                    m = 1024 // (2 * b)
                    op(e.tensor_tensor(R(buf, (2 * b, m), (b, 2), (1, b)), R(CC2, (2 * b, m), (1024 + b, 2), (1, b)),
                                       R(CC2 + b - 1, (2 * b, m), (1024, 2), (0, b)), ALU.subtract), "gd")

            def mult(n):
                buf = GXA if n % 2 == 0 else GXB
                b = P if n == 0 else LEVELS[n - 1]
                m = 1024 // (2 * b)
                e.wait_ge(*after("ge", n + 1))
                v = R(buf, (2 * b, m), (b, 2), (1, b))
                op(e.tensor_tensor(v, v, R(QK, (2 * b, m), (1024 + b, 2), (1, b)), ALU.mult), "gx")

            def scores(n):
                if n == 0:
                    e.wait_ge(*after("level_mm", 1))
                    op(e.tensor_copy(R(SXT, (1, 512)), X_[0][:, :]), "gla_cross")
                    return
                settle()
                for t in range(NT):
                    e.wait_ge(*after("level_mm", 2 * (n - 1) + t + 2))
                    op(e.copy_predicated(R(STT_ + t * 512, (P, GH), (1, P)),
                                         mask[:, n - 1, :].unsqueeze(1).to_broadcast([P, GH, P]),
                                         X_[2 * (n % 2) + t][:, :].rearrange("p (h q) -> p h q", h=4)), "gla_s")

            def step(n):
                def f():
                    if n < 7:
                        diff(n + 1)
                    if n < 8:
                        mult(n)
                    if n > 0:
                        scores(n - 1)
                return f

            def yz():
                hr = sm("n0_hr", 2)
                for t in range(NT):
                    y = R(XS + t * D, (1, D))
                    op(e.scalar_tensor_tensor(out=y, in0=y, scalar=hr[:, t:t + 1], in1=R(ZZ + t * D, (1, D)),
                                              op0=ALU.mult, op1=ALU.mult), "yz")

            def yn():
                e.wait_ge(*after("y_rstd", 1))
                for t in range(NT):
                    for g in range(SG):
                        y = R(XS + t * D + g * 512, (1, 512))
                        op(e.tensor_scalar(y, y, sm("y_r", 4)[:, 2 * t + g:2 * t + g + 1], None, ALU.mult), "yn")

            by_rows("xk0_1", (xk[:, 4:6, :], xk[:, 6:8, :]), "mem", 1.0,
                    {1: lambda: y_add(1), 2: y_cross, 3: lambda: (gla_cum(), yz())})
            e.wait_ge(*after("mask_loaded", 16))
            rm_ = sm("mem_r", 2)[:, 1:2]
            copy1("xv0_0", xv[:, 1, 0:512], rm_,
                  {0: gla_diag, 1: lambda: diff(0), 2: step(0)})
            copy1("xv0_1", xv[:, 1, 512:1024], rm_, {0: step(1), 1: yn, 2: step(2)})
            rx = sm("n0_r", 2)
            copy1("v0", R(VV + D, (1, 512)), rx[:, 1:2], {0: step(3), 2: step(4)})
            copy1("v1", R(VV + D + 512, (1, 512)), rx[:, 1:2], {0: step(5), 2: step(6)})
            gated("r", 0, RR, {0: step(7), 2: step(8)})
            gated("r", 1, RR, {1: lambda: lo_parts("y", B, lambda k: col("ssdn", k))})

            def o_norm():
                e.wait_ge(*after("o_rstd", 1))
                for n in ("r0", "r1"):
                    e.wait_ge(*evac(number[n], 1))
                for b in range(4):
                    for i in range(2):
                        t, h = b // 2, 2 * (b % 2) + i
                        op(e.scalar_tensor_tensor(out=R(OO + t * D + h * GV, (1, GV)),
                                                  in0=X_[b][:, i * GV:(i + 1) * GV],
                                                  scalar=sm("o_r", 8)[:, 2 * b + i:2 * b + i + 1],
                                                  in1=R(RR + t * D + h * GV, (1, GV)), op0=ALU.mult, op1=ALU.mult),
                           "on")

            add_x("outy0", 0, None, {3: o_norm})
            add_x("outy1", 1, None, {2: lambda: lo_parts("o", A, lambda k: col("glan", k % 2))})
            add_x("outo0", 0)
            add_x("outo1", 1, None, {1: lambda: lo_parts("xn0", B, lambda k: col("xa0", k), (0, 1))})

            def fin_gain(n):
                e.wait_ge(*after("fnorm_loaded", 16))
                for t in range(NT):
                    e.wait_ge(*evac(number[f"down1_{n}"], t))
                    op(e.tensor_tensor(result(t, n), x[:, t, n * 512:(n + 1) * 512],
                                       xk[:, 2 * n:2 * n + 2, :].rearrange("p a b -> p (a b)"), ALU.mult), "fin_gain")

            def tail(l, one, two):
                lo_parts(f"xn{l}", one, lambda k: col(f"xa{l}", k), (2, 3))
                nm, ri = sm(f"c{l}_nmax", 8), sm(f"c{l}_ri", 8)

                def maxima(hh):
                    e.wait_ge(*after(f"xn{l}_rstd", 1))
                    for t in range(NT):
                        e.wait_ge(*after(f"c{l}_score", 2 * hh + t + 1))
                        v = nm[:, t * XH + 2 * hh:t * XH + 2 * hh + 2]
                        link(e.tensor_reduce(v, X_[2 * hh + t][:, :].rearrange("p (h m) -> p h m", h=2), AX, ALU.max,
                                             negate=True))
                        op(e.tensor_scalar(v, v, sm(f"xn{l}_s", 2)[:, t:t + 1], None, ALU.mult), f"c{l}_max")

                def normalise(hh):
                    e.wait_ge(*after(f"c{l}_exp", 4 * (hh + 1)))
                    settle()
                    for t in range(NT):
                        at = t * XH + 2 * hh
                        link(e.reciprocal(ri[:, at:at + 2], sm(f"c{l}_sum", 8)[:, at:at + 2]))
                    for t in range(NT):
                        for i in range(2):
                            n = t * XH + 2 * hh + i
                            v = R(CP + n * NM, (1, NM))
                            op(e.tensor_scalar(v, v, ri[:, n:n + 1], None, ALU.mult), f"c{l}_p")

                def o_lo(hh):
                    for h in (2 * hh, 2 * hh + 1):
                        e.wait_ge(*after(f"c{l}_hi", h + 1))
                        op(e.tensor_tensor(two[1][:, 2 * h:2 * h + 2, :], X_[h][:, :].rearrange("p (a b) -> p a b", a=2),
                                           two[0][:, 2 * h:2 * h + 2, :].bitcast(F32), ALU.subtract), f"c{l}_lo")

                copy1(f"xq{l}_0", R(CQ + 2 * L, (L, 2), (1, L)))
                copy1(f"xq{l}_1", R(CQ + 6 * L, (L, 2), (1, L)), None,
                      {1: lambda: maxima(0), 2: lambda: normalise(0)})
                o_lo(0)
                maxima(1)
                normalise(1)
                ahead(f"xo{l}_0", {3: lambda: o_lo(1)})
                add_x(f"xo{l}_1", 1, None, {2: lambda: add_bank(number[f"xo{l}_0"], 0),
                                            4: lambda: lo_parts(f"mn{l}", one, lambda k: col(f"mlp{l}", k), (0, 1))})
                lo_parts(f"mn{l}", one, lambda k: col(f"mlp{l}", k), (2, 3))
                for n in range(8):
                    g = ahead(f"up{l}_{n}")
                    for b in range(2):
                        e.wait_ge(*evac(g, b))
                        settle()
                        op(e.tensor_tensor(sp[:, b, :], junk[:, b, :], junk[:, b, :], ALU.mult), "hid_sq")
                    for b in range(2):
                        e.wait_ge(*after("hid_hi", 16 * l + 2 * n + b + 1))
                        lo = hid_lo[:, 4 * n + 2 * b:4 * n + 2 * b + 2, :]
                        hi = hid_hi[:, 4 * n + 2 * b:4 * n + 2 * b + 2, :].bitcast(F32)
                        op(e.tensor_tensor(lo, sp[:, b, :].rearrange("p (a c) -> p a c", a=2), hi, ALU.subtract),
                           f"hid{l}")
                e.wait_ge(*after(f"mn{l}_rstd", 1))
                add_x(f"down{l}_0", 0, sm(f"mn{l}_s", 2))
                add_x(f"down{l}_1", 1, sm(f"mn{l}_s", 2),
                      {1: lambda: lo_parts("n1", A, lambda k: col("od", k), (0, 1))} if l == 0
                      else {1: lambda: fin_gain(0)})

            tail(0, B, A)

            lo_parts("n1", A, lambda k: col("od", k), (2, 3))

            def lam_dot():
                lam = row[:, 48:48 + 4 * DHD].rearrange("p (m a d) -> p m a d", m=2, a=2)
                lp = sm("lam_p", 2 * DHD).rearrange("p (m d) -> p m d", m=2)
                link(e.tensor_tensor(lp, lam[:, :, 0, :], lam[:, :, 1, :], ALU.mult))
                op(e.tensor_reduce(sm("lam_d", 2), lp, AX, ALU.add), "lam_dot")

            nl = sm("nlam", 1)

            def lam_end():
                e.wait_ge(*after("lam_e", 1))
                le = sm("lam_e", 2)
                link(e.tensor_tensor(nl, le[:, 1:2], le[:, 0:1], ALU.subtract))
                link(e.tensor_scalar(nl, nl, LAMBDA_INIT, None, ALU.subtract))

            nm, rs = sm("d_nmax", 32), sm("d_sum", 32)
            r1 = sm("n1_r", 2)

            def diff_bias(r):
                t, per, first = ROUNDS[r]
                keys = (t + 1) * P
                at, base = (0, 8, 24)[r], SC + 2048 * (r % 2)
                for b in range(4):
                    e.wait_ge(*after("d_score", 4 * r + b + 1))
                    h0 = first + per * (b // 2)
                    op(e.scalar_tensor_tensor(out=R(base + b * 512, (keys, per), (1, keys)),
                                              in0=X_[b][:, :].rearrange("p (h k) -> p h k", h=per),
                                              scalar=r1[:, t:t + 1],
                                              in1=R(BIAS + h0 * L + L - keys, (L, per), (1, keys)), op0=ALU.mult,
                                              op1=ALU.add), "d_bias")
                settle()
                link(e.tensor_reduce(nm[:, at:at + 4 * per], R(base, (keys, 4 * per), (1, keys)), AX, ALU.max,
                                     negate=True), "d_max")

            def diff_mix(r):
                t, per, _ = ROUNDS[r]
                keys = (t + 1) * P
                at, base = (0, 8, 24)[r], SC + 2048 * (r % 2)
                e.wait_ge(*after("d_exp", (8, 24, 32)[r]))
                ri, rl = sm("d_ri", 32), sm("d_rl", 32)
                link(e.reciprocal(ri[:, at:at + 4 * per], rs[:, at:at + 4 * per]))
                link(e.tensor_scalar(rl[:, at:at + 4 * per], ri[:, at:at + 4 * per], nl, None, ALU.mult))
                if r > 0:
                    e.wait_ge(*after("d_anT", 2 * r))
                for pair in range(2):
                    for i in range(per):
                        n = per * pair + i
                        c0 = at + 2 * per * pair + i
                        p0 = R(base + (c0 - at) * keys, (1, keys))
                        op(e.tensor_scalar(R(AN + n * keys, (1, keys)), p0, ri[:, c0:c0 + 1], None, ALU.mult))
                settle()
                for pair in range(2):
                    for i in range(per):
                        n = per * pair + i
                        c1 = at + 2 * per * pair + i + per
                        an = R(AN + n * keys, (1, keys))
                        p1 = R(base + (c1 - at) * keys, (1, keys))
                        op(e.scalar_tensor_tensor(out=an, in0=p1, scalar=rl[:, c1:c1 + 1], in1=an, op0=ALU.mult,
                                                  op1=ALU.add), "d_an")

            copy1("dq0", R(DQ + 2 * L, (L, 2), (1, L)), DHD ** -0.5, {0: lam_dot})
            by_rows("dk0", qk_rows(DK), "n1", 1.0, {2: lam_end, 3: lambda: row_copy("n1", 2)})
            e.wait_ge(*after("bias_loaded", 16))
            copy1("dq1", R(DQ + 6 * L, (L, 2), (1, L)), DHD ** -0.5, {1: lambda: diff_bias(0)})
            by_rows("dk1", qk_rows(DK + 4 * L), "n1", 1.0, {0: lambda: diff_mix(0), 2: lambda: mem_lo(1)})
            copy1("dv0", R(DV + D, (1, 512)), r1[:, 1:2], {1: lambda: diff_bias(1)})
            copy1("dv1", R(DV + D + 512, (1, 512)), r1[:, 1:2], {0: lambda: diff_mix(1)})
            by_rows("xk1_0", (xk[:, 0:2, :], xk[:, 2:4, :]), "mem", 1.0,
                    {0: lambda: diff_bias(2), 3: lambda: diff_mix(2)})

            def do_sums():
                for b in range(4):
                    e.wait_ge(*after("do_sq", b + 1))
                    op(e.tensor_reduce(sm("do_ss", 16)[:, 4 * b:4 * b + 4],
                                       junk[:, b % 2, :].rearrange("p (h v) -> p h v", h=4), AX, ALU.add), "do_sum")

            def do_norm():
                e.wait_ge(*after("do_rstd", 1))
                for b in range(4):
                    op(e.tensor_tensor(R(SC + b * 512, (P, 4), (1, P)), X_[b][:, :].rearrange("p (h v) -> p h v", h=4),
                                       heads(sm("do_r", 16)[:, 4 * b:4 * b + 4], P), ALU.mult), "d_on")

            by_rows("xk1_1", (xk[:, 4:6, :], xk[:, 6:8, :]), "mem", 1.0, {2: do_sums})
            copy1("xv1_0", xv[:, 1, 0:512], rm_, {3: do_norm})
            copy1("xv1_1", xv[:, 1, 512:1024], rm_, {1: lambda: lo_parts("d", A, lambda k: col("subln"))})
            add_x("dout0", 0)
            add_x("dout1", 1, None, {1: lambda: lo_parts("xn1", B, lambda k: col("xa1", k), (0, 1))})
            tail(1, B, A)
            fin_gain(1)
            e.wait_ge(*after("fin_rstd", 1))
            settle()
            for n in range(2):
                v = result(0, n)
                op(e.tensor_scalar(v, v, sm("fin_r", 2)[:, 0:1], None, ALU.mult), "final0")

        @block.gpsimd
        def _(e):
            op, settle, link = tracker(e, "pool_step")

            def split(c, before={}):
                for j in range(PIECES):
                    if j in before:
                        before[j]()
                    if c >= len(chunks) or j % 2 == 0:
                        continue
                    width = chunks[c][3]
                    e.wait_ge(*after("hi_ready", 4 * c + j + 1))
                    op(e.tensor_tensor(w_lo[:, j, :, 0:width], raw[:, j, :, 0:width],
                                       w_hi[:, j, :, 0:width].bitcast(F32), ALU.subtract), "lo_pool")
                if PIECES in before:
                    before[PIECES]()

            def ahead(name, before={}):
                g = number[name]
                n = len(groups[g][2])
                for i in range(n):
                    split(first_chunk[g] + i + 1, before if i == n - 1 else {})

            def rstd(key, n, width, count, wait="_sq"):
                e.wait_ge(*after(key + wait, count))
                r = sm(key + "_r", n)
                link(e.tensor_scalar(r, sm(key + "_ss", n), 1.0 / width, EPS, ALU.mult, ALU.add))
                link(e.tensor_tensor(r, r, neghalf[:, 0:n], ALU.pow))

            def rstd_x(key, post=None):
                e.wait_ge(*after(key + "_sq", 4))
                r, ss = sm(key + "_r", 2), sm(key + "_ss", 4)
                link(e.tensor_tensor(r, ss[:, 0:2], ss[:, 2:4], ALU.add))
                link(e.tensor_scalar(r, r, 1.0 / D, EPS, ALU.mult, ALU.add))
                last = e.tensor_tensor(r, r, neghalf[:, 0:2], ALU.pow)
                if post is not None:
                    link(last)
                    last = post(r)
                op(last, key + "_rstd")

            op(e.memset(glr_t[:], 1.0), "ones_ready")
            op(e.memset(R(XB, (XBW, XT), (1, 3)), 0.0), "pad_ready")
            e.wait_ge(*after("const_loaded", 16))
            split(0)
            rstd_x("n0", lambda r: e.tensor_scalar(sm("n0_hr", 2), r, 0.5, None, ALU.mult))
            ahead("xbc0")
            rstd_x("mem")
            for name in ("xbc1", "xbc2", "q0", "k0", "z0", "z1", "xk0_0", "xk0_1"):
                ahead(name)

            def y_rstd():
                rstd("y", 4, 512, 4)
                r = sm("y_r", 4)
                op(e.tensor_scalar(r, r, 1.0, None, ALU.mult), "y_rstd")

            ahead("xv0_0", {3: y_rstd})
            for name in ("xv0_1", "v0", "v1", "r0", "r1"):
                ahead(name)

            def o_rstd():
                rstd("o", 8, GV, 8)
                r = sm("o_r", 8).rearrange("p (t h) -> p t h", t=NT)
                hr = sm("n0_hr", 2).unsqueeze(2).to_broadcast([P, NT, GH])
                op(e.tensor_tensor(r, r, hr, ALU.mult), "o_rstd")

            ahead("outy0", {2: o_rstd})
            for name in ("outy1", "outo0", "outo1"):
                ahead(name)

            def tail(l):
                rstd_x(f"xn{l}", lambda r: e.tensor_scalar(sm(f"xn{l}_s", 2), r, XHD ** -0.5, None, ALU.mult))
                for name in (f"xq{l}_0", f"xq{l}_1", f"xo{l}_0", f"xo{l}_1"):
                    ahead(name)
                rstd_x(f"mn{l}", lambda r: e.tensor_tensor(sm(f"mn{l}_s", 2), r, r, ALU.mult))
                for n in range(8):
                    ahead(f"up{l}_{n}")
                ahead(f"down{l}_0")
                ahead(f"down{l}_1")

            tail(0)
            rstd_x("n1")
            for name in ("dq0", "dk0", "dq1", "dk1", "dv0", "dv1", "xk1_0"):
                ahead(name)

            def do_rstd():
                rstd("do", 16, P, 4, "_sum")
                r = sm("do_r", 16)
                op(e.tensor_scalar(r, r, 1.0 - LAMBDA_INIT, None, ALU.mult), "do_rstd")

            ahead("xk1_1")
            ahead("xv1_0", {0: do_rstd})
            for name in ("xv1_1", "dout0", "dout1"):
                ahead(name)
            tail(1)
            rstd_x("fin")


def kernel(x, mem, ev_norm, ev_w_in, ev_conv_w, ev_conv_b, ev_dt_bias, ev_a_log, ev_d_skip, ev_ssd_norm, ev_gla_w2,
           ev_gla_b, ev_gla_norm, ev_w_out, od_norm, od_w_qkv, od_lam_q1, od_lam_k1, od_lam_q2, od_lam_k2, od_subln,
           od_w_o, xa_norm, xa_mem_norm, xa_wq, xa_wkv, xa_wo, mlp_norm, mlp_w1, mlp_w2, final_norm):
    import concourse.bacc as bacc
    from concourse.bass_utils import run_bass_kernel_spmd

    def rows(*arrays):
        return np.concatenate([np.asarray(a).reshape(-1, P) for a in arrays], axis=0)

    prow = rows(ev_norm[0], od_norm[0], xa_norm[0], xa_norm[1], xa_mem_norm[0], xa_mem_norm[1], mlp_norm[0],
                mlp_norm[1], ev_ssd_norm[0], ev_gla_norm[0], od_subln[0], ev_conv_w[0], ev_conv_b[0])
    row = np.concatenate([np.asarray(a).reshape(-1) for a in
                          (ev_dt_bias[0], ev_a_log[0], ev_d_skip[0], od_lam_q1[0], od_lam_k1[0], od_lam_q2[0],
                           od_lam_k2[0])])[None]
    w_in = np.asarray(ev_w_in)[0]
    w_small = np.concatenate([w_in[:, DT0:DT0 + SH], w_in[:, GLR0:GLR0 + RANK]], axis=1)
    gla_w2b = np.concatenate([np.asarray(ev_gla_w2)[0], np.asarray(ev_gla_b)], axis=0)

    i, j = np.arange(P)[:, None], np.arange(P)[None, :]
    const = np.concatenate([i == j, i <= j, np.ones((P, P)), np.full((P, 16), -0.5)], axis=1).astype(np.float32)
    mask = np.stack([(i // (2 * b) == j // (2 * b)) & (i % (2 * b) < b) & (j % (2 * b) >= b) for b in LEVELS],
                    axis=1).astype(np.int32)
    dist = P + np.arange(P)[:, None] - np.arange(L)[None, :]
    slopes = np.array([2.0 ** -(h + 1) for h in range(DH)], np.float32)
    bias = np.where(dist[:, None, :] >= 0, -slopes[None, :, None] * dist[:, None, :], -3e38)
    bias = bias.astype(np.float32).reshape(P, DH * L)

    arrays = {
        "x": x, "mem": mem, "ev_w_in": ev_w_in, "ev_w_out": ev_w_out, "od_w_qkv": od_w_qkv, "od_w_o": od_w_o,
        "xa_wq": xa_wq, "xa_wkv": xa_wkv, "xa_wo": xa_wo, "mlp_w1": mlp_w1, "mlp_w2": mlp_w2,
        "prow": prow, "row": row, "w_small": w_small, "gla_w2b": gla_w2b, "fnorm": np.asarray(final_norm)[None],
        "const": const, "mask": mask, "bias": bias,
    }
    nc = bacc.Bacc("TRN2", target_bir_lowering=False, num_devices=1)
    given, w = {}, {}
    for name, a in arrays.items():
        a = np.ascontiguousarray(a)
        given["in_" + name] = a
        w[name] = nc.dram_tensor("in_" + name, a.shape, mybir.dt.from_np(a.dtype), kind="ExternalInput").ap()
    w["out"] = nc.dram_tensor("out", (1, L, D), F32, kind="ExternalOutput").ap()
    trunk(nc, w)
    result = run_bass_kernel_spmd(nc, [given], core_ids=[0])
    return result.results[0]["out"]
```

```python
import math
from contextlib import ExitStack

import concourse.bass as bass
import numpy as np
from concourse import mybir

F32 = mybir.dt.float32
F32R = mybir.dt.float32r
I32 = mybir.dt.int32
ALU = mybir.AluOpType
ACT = mybir.ActivationFunctionType
AX = mybir.AxisListType.X

P = 128
D = 1024
L = 256
NT = L // P
KT = D // P
EPS = 1e-5
FF = 4 * D
PIECES = 4
SH, SP_, SG, SN = 16, 64, 2, 64
XBC = SH * SP_ + 2 * SG * SN
XT = XBC // P
TAPS = 4
GH, GK, GV, RANK, TAU = 4, 128, 256, 16, 16.0
DH, DHD = 8, 64
PAIR, UP_GROUPS, UP_PEEL = 2, 8, 2
UP_PASSES = (UP_GROUPS - UP_PEEL) // PAIR
PAIRS = ("xo0_0", "xo1_0")
LAMBDA_INIT = 0.8 - 0.6 * math.exp(-0.3 * 1)
XH, XHD, NM = 4, 256, 256
DT_ROW = 32
SMALL = DT_ROW + SH
Z0, XBC0 = 0, 1024
DT0 = XBC0 + XBC
Q0 = DT0 + SH
K0 = Q0 + GH * GK
V0 = K0 + GH * GK
GLR0 = V0 + GH * GV
R0 = GLR0 + RANK

COLS = {}
_n = 0
for _name, _count in [("ev", 8), ("od", 8), ("xa0", 8), ("xa1", 8), ("mem0", 8), ("mem1", 8), ("mlp0", 8),
                      ("mlp1", 8), ("ssdn", 8), ("glan", 2), ("subln", 1), ("convw", TAPS * XT), ("convb", XT)]:
    COLS[_name] = _n
    _n += _count
NCOLS = _n

NROW = 48 + 4 * DHD

C_ID, C_TRI, C_ONE, C_NEG = 0, P, 2 * P, 3 * P
NCONST = 3 * P + 16
LEVELS = [64, 32, 16, 8, 4, 2, 1]

REG = 16672
XB, CV, TT, ZZ, MM, GG, QK, VV = 0, 2592, 5152, 7712, 9760, 11808, 12576, 14624
XBW = L + TAPS - 1
XS, XDT, WX, YC = XB, TT, CV, CV + 1024
CC2, GXA, GXB, STT_, SXT, RR, OO = MM, TT, TT + 1024, CV, CV + 1024, ZZ, XB
MEM = VV
DQ, DK, DV, BIAS, SC, AN, AT = 0, 2048, 4096, 6144, 8192, 12288, 13312
CQ, CP, CPT = 0, 2048, 4096
ROUNDS = [(1, 2, 0), (0, 4, 0), (1, 2, 4)]
AT_TILE0 = 8


def groups_of(w):
    out = []

    def add(name, mode, weights, columns, rows=(0,), width=512):
        for n, c in enumerate(columns):
            out.append((f"{name}{n}", mode, [(weights, r, c, width) for r in rows]))

    def cross(layer):
        add(f"xk{layer}_", "T", w["xa_wkv"][layer], (0, 512))
        add(f"xv{layer}_", "N", w["xa_wkv"][layer], (1024, 1536))

    def tail(layer):
        add(f"xq{layer}_", "T", w["xa_wq"][layer], (0, 512))
        add(f"xo{layer}_", "N", w["xa_wo"][layer], (0, 512))
        add(f"up{layer}_", "T", w["mlp_w1"][layer], range(0, FF, 512))
        add(f"down{layer}_", "N", w["mlp_w2"][layer], (0, 512), range(0, FF, D))

    w_in, w_out = w["ev_w_in"][0], w["ev_w_out"][0]
    add("xbc", "T", w_in, (XBC0, XBC0 + 512))
    out.append(("xbc2", "T", [(w_in, 0, XBC0 + 1024, 256)]))
    add("q", "T", w_in, (Q0,))
    add("k", "T", w_in, (K0,))
    add("z", "N", w_in, (Z0, Z0 + 512))
    cross(0)
    add("v", "N", w_in, (V0, V0 + 512))
    add("r", "N", w_in, (R0, R0 + 512))
    add("outy", "N", w_out, (0, 512))
    add("outo", "N", w_out, (0, 512), (1024,))
    tail(0)
    w_qkv = w["od_w_qkv"][0]
    for n in range(2):
        out.append((f"dq{n}", "T", [(w_qkv, 0, n * 512, 512)]))
        out.append((f"dk{n}", "T", [(w_qkv, 0, 1024 + n * 512, 512)]))
    add("dv", "N", w_qkv, (2048, 2560))
    cross(1)
    add("dout", "N", w["od_w_o"][0], (0, 512))
    tail(1)
    return out


def trunk(nc, w):
    groups = groups_of(w)
    number = {g[0]: n for n, g in enumerate(groups)}
    chunks = [c for g in groups for c in g[2]]
    first_chunk = []
    for g in groups:
        first_chunk.append(first_chunk[-1] + len(groups[len(first_chunk) - 1][2]) if first_chunk else 0)

    ctx = ExitStack()
    with ctx:
        def sb(name, shape, dt=F32):
            return ctx.enter_context(nc.sbuf_tensor(name, shape, dt))

        norms = ["n0", "mem", "y", "o", "xn0", "mn0", "n1", "do", "xn1", "mn1", "fin"]
        halves = ["n0", "mem", "y", "o", "xn0", "c0", "mn0", "n1", "d", "xn1", "c1", "mn1"]
        splits = ["n0", "mg0", "y", "o", "xn0", "c0", "mn0", "n1", "mg1", "d", "xn1", "c1", "mn1"]
        shared = {
            "squares": [(k + "_sq", 8 if k == "o" else 4) for k in norms],
            "rstd": [(k + "_rstd", 1) for k in norms],
            "turned": [(k + "_T", 4) for k in halves],
            "act_hi": [(k + "_hi", 4 if k[0] == "c" else 8) for k in splits],
            "act_lo": [(k + "_lo", 4 if k[0] == "c" else 8) for k in splits],
            "cross_score": [("c0_score", 4), ("c1_score", 4)],
            "cross_exp": [("c0_exp", 8), ("c1_exp", 8)],
            "cross_max": [("c0_max", 4), ("c1_max", 4)],
            "cross_p": [("c0_p", 8), ("c1_p", 8)],
            "cross_pT": [("c0_pT", 4), ("c1_pT", 4)],
            "cross_pt": [("c0_pt", 4), ("c1_pt", 4)],
            "hid_lo_ready": [("hid0", 16), ("hid1", 16)],
            "rbc_mm": [("n0_rbcmm", 1), ("mem_rbcmm", 1), ("n1_rbcmm", 1)],
            "rbc": [("n0_rbc", 1), ("mem_rbc", 1), ("n1_rbc", 1)],
        }
        stage = {}
        for family, parts_ in shared.items():
            base = 0
            for name_, steps in parts_:
                stage[name_] = (family, base)
                base += steps
        sems = {}

        def sem(name):
            if name not in sems:
                sems[name] = ctx.enter_context(nc.semaphore(name))
            return sems[name]

        def after(name, n):
            family, base = stage.get(name, (name, 0))
            return sem(family), base + n

        with nc.sbuf_tensor("region", [P, REG], F32) as region:
            pass
        with nc.sbuf_tensor("hid_hi", [P, FF // P, L], F32R) as hid_hi, \
                nc.sbuf_tensor("hid_lo", [P, FF // P, L], F32R) as hid_lo:
            pass
        sb("region_bytes", [P, REG])
        raw = sb("raw", [P, PIECES, 2, 512])
        w_hi = sb("w_hi", [P, PIECES, 2, 512], F32R)
        w_lo = sb("w_lo", [P, PIECES, 2, 512], F32R)
        x = sb("x", [P, NT, D])
        a_hi, a_lo = sb("a_hi", [P, KT, L], F32R), sb("a_lo", [P, KT, L], F32R)
        b_hi, b_lo = sb("b_hi", [P, KT, L], F32R), sb("b_lo", [P, KT, L], F32R)
        mem_t = sb("mem_t", [P, KT, NM])
        xk = sb("xk", [P, KT, NM])
        xv = sb("xv", [P, NM // P, D])
        junk = sb("junk", [P, 2, 512])
        sp = sb("sp", [P, NT, 512])
        const = sb("const", [P, NCONST])
        mask = sb("mask", [P, len(LEVELS), P], I32)
        prow = sb("prow", [NCOLS, P])
        cols = sb("cols", [P, NCOLS])
        half = sb("half", [P, (TAPS + 1) * XT])
        row = sb("row", [P, NROW])
        sw = sb("sw", [P, KT, SMALL])
        sw_hi, sw_lo = sb("sw_hi", [P, KT, SMALL], F32R), sb("sw_lo", [P, KT, SMALL], F32R)
        w2g = sb("w2g", [RANK + 1, 512])
        glr_t = sb("glr_t", [SMALL, L])
        small = sb("small", [P, 832])
        rbc = {"n0": sb("rbc_x", [P, L]), "mem": sb("rbc_mem", [P, NM])}
        rbc["n1"] = rbc["n0"]
        L_ = [ctx.enter_context(nc.psum_tensor(f"lin{n}", [P, 512], F32)) for n in range(4)]
        X_ = [ctx.enter_context(nc.psum_tensor(f"mix{n}", [P, 512], F32)) for n in range(4)]

        def R(off, *dims):
            return bass.AP(tensor=region, offset=off, ap=[[REG, P], *[list(d) for d in dims]])

        def result(t, n):
            return mem_t[:, 4 * t + 2 * n:4 * t + 2 * n + 2, :].rearrange("p a b -> p (a b)")

        small_at = {}

        def sm(name, n):
            if name not in small_at:
                small_at[name] = (sum(v[1] for v in small_at.values()), n)
            at, n = small_at[name]
            return small[:, at:at + n]

        ident, tri, ones = const[:, C_ID:C_ID + P], const[:, C_TRI:C_TRI + P], const[:, C_ONE:C_ONE + P]
        neghalf = const[:, C_NEG:C_NEG + 16]

        def col(name, k=0):
            return cols[:, COLS[name] + k:COLS[name] + k + 1]

        paired = {first_chunk[g] for g, grp in enumerate(groups) if grp[0] in PAIRS}
        ends = {}
        for g in range(len(groups)):
            if first_chunk[g] in paired:
                ends[first_chunk[g] + 1, 1] = g
            else:
                ends[first_chunk[g] + len(groups[g][2]) - 1, PIECES - 1] = g

        def piece_source(c, j):
            wt, r0, c0, width = chunks[c]
            if c in paired or c - 1 in paired:
                r, cc = 512 * (c - 1 in paired) + 256 * (j % 2), 512 * (j // 2)
            else:
                r, cc = r0 + 256 * j, c0
            return wt[r:r + 256, cc:cc + width].rearrange("(k p) n -> p k n", p=P)

        def first(value, step):
            return value

        def passes(eng, i, needed):
            known = {}
            for value, step in needed:
                if (value, step) not in known:
                    known[value, step] = eng.snap(i * step + value)
            return lambda value, step: known[value, step]

        def later(at, step, now):
            return at[0], now(at[1], step)

        def freed_at(c, j):
            if (c, j) in ends:
                return after("group_done", ends[c, j] + 1), PAIR
            return after("mm_done", PIECES * c + j + 1 - sum(1 for at in ends if at < (c, j))), PAIR * (PIECES - 1)

        def split_steps(c):
            high = [(4 * c + j + 1, PAIR * PIECES) for j in range(PIECES)]
            return high + [(2 * c + j + 1, PAIR * 2) for j in range(2)]

        def bank_view(g, b, dst):
            bank = banks_of(g)[b][:, :]
            return bank if len(dst.shape) == 2 else bank.rearrange("p (a b) -> p a b", a=2)

        def banks_of(g):
            return L_[2 * (g % 2)], L_[2 * (g % 2) + 1]

        def evac(g, b):
            return sem(f"evac{g % 2}{b}"), g // 2 + 1

        def tracker(eng, own):
            tally, last = {}, []

            def op(ins, name=None, value=None):
                name = name or own
                tally[name] = tally.get(name, 0) + 1
                s, v = after(name, value or tally[name])
                ins.then_inc(s, 1)
                last[:] = [s, v]
                return ins

            def settle():
                eng.wait_ge(last[0], last[1])

            def looped(start=None):
                if start is None:
                    return dict(tally)
                for name, n in list(tally.items()):
                    tally[name] = n + (UP_PASSES - 1) * (n - start.get(name, 0))

            def link(ins, name=None):
                op(ins, name)
                settle()

            return op, settle, link, looped

        block = ctx.enter_context(nc.Block())

        @block.sync
        def _(e):
            def load(dst, src, name):
                e.dma_start(dst, src).then_inc(sem(name), 16)

            def weights(c, pieces=range(PIECES)):
                width = chunks[c][3]
                for j in pieces:
                    if c > 0:
                        e.wait_ge(*after("hi_ready", 4 * (c - 1) + j + 1))
                        e.wait_ge(*after("lo_dve" if j % 2 == 0 else "lo_pool", 2 * (c - 1) + j // 2 + 1))
                    e.dma_start(raw[:, j, :, 0:width], piece_source(c, j)).then_inc(sem(f"raw_ready{j}"), 16)

            load(prow[:], w["prow"], "prow_loaded")
            load(const[:], w["const"], "const_loaded")
            for j in range(PIECES):
                load(x[:, :, j * 256:(j + 1) * 256],
                     w["x"][0, :, j * 256:(j + 1) * 256].rearrange("(t p) d -> p t d", p=P), f"x_loaded{j}")
                weights(0, (j,))
            load(sw[:], w["w_small"].rearrange("(k p) n -> p k n", p=P), "sw_loaded")
            load(R(MEM, (D, NT), (1, D)), w["mem"][0].rearrange("(t p) d -> p t d", p=P), "mem_loaded")
            load(row[:], w["row"].to_broadcast([P, NROW]), "row_loaded")
            load(w2g[:], w["gla_w2b"], "w2g_loaded")
            load(mask[:], w["mask"], "mask_loaded")
            for c in range(1, len(chunks)):
                weights(c)
                if c == first_chunk[number["dq0"]] + 1:
                    e.wait_ge(*after("group_done", number["down0_1"] + 1))
                    load(R(BIAS, (1, 2048)), w["bias"], "bias_loaded")
                if c == first_chunk[number["up1_1"]]:
                    e.wait_ge(*after("c1_score", 4))
                    gain = w["fnorm"].to_broadcast([P, D]).rearrange("p (a b) -> p a b", a=4)
                    load(xk[:, 0:4, :], gain, "fnorm_loaded")
            for n in range(2):
                for t in range(NT):
                    half_ = slice(n * 512, (n + 1) * 512)
                    e.wait_ge(*after(f"final{t}", n + 1))
                    e.dma_start(w["out"][0, t * P:(t + 1) * P, half_],
                                result(t, n)).then_inc(sem("stored"), 16)
            e.wait_ge(*after("stored", 2 * 16 * NT))

        @block.tensor
        def _(e):
            freed = [None] * 4

            def take(b):
                if freed[b]:
                    e.wait_ge(*after(freed[b][0], freed[b][1]))
                return X_[b]

            def product(name, act, ready, per=2, before={}, now=first):
                g = number[name]
                _, mode, parts = groups[g]
                bank = banks_of(g)
                hi, lo = act
                if g >= 2:
                    for b in range(2):
                        e.wait_ge(*later(evac(g - 2, b), 1, now))
                for n, (_, _, _, width) in enumerate(parts):
                    c = first_chunk[g] + n
                    for j in range(PIECES):
                        if n == len(parts) - 1 and j in before:
                            before[j]()
                        e.wait_ge(*after(ready, per * (PIECES * n + j + 1)))
                        e.wait_ge(*later(after("hi_ready", 4 * c + j + 1), PAIR * PIECES, now))
                        e.wait_ge(*later(after("lo_dve" if j % 2 == 0 else "lo_pool", 2 * c + j // 2 + 1),
                                         PAIR * 2, now))
                        begin, end = n == 0 and j == 0, n == len(parts) - 1 and j == PIECES - 1
                        if mode == "T":
                            for f in range(width // P):
                                out = bank[f // 2][:, (f % 2) * L:(f % 2 + 1) * L]
                                for kk in range(2):
                                    k = 2 * j + kk
                                    wh, wl = (t[:, j, kk, f * P:(f + 1) * P] for t in (w_hi, w_lo))
                                    e.matmul(out, wh, hi[:, k, :], start=begin and kk == 0 and f % 2 == 0,
                                             stop=False, skip_group_check=True)
                                    e.matmul(out, wh, lo[:, k, :], start=False, stop=False, skip_group_check=True)
                                    m = e.matmul(out, wl, hi[:, k, :], start=False, stop=end and kk == 1,
                                                 skip_group_check=True)
                        else:
                            for kk in range(2):
                                k = KT * n + 2 * j + kk
                                for t in range(NT):
                                    ah, al = (a[:, k, t * P:(t + 1) * P] for a in (hi, lo))
                                    out = bank[t][:, :]
                                    e.matmul(out, ah, w_hi[:, j, kk, :], start=begin and kk == 0, stop=False)
                                    e.matmul(out, ah, w_lo[:, j, kk, :], start=False, stop=False)
                                    m = e.matmul(out, al, w_hi[:, j, kk, :], start=False, stop=end and kk == 1)
                        m.then_inc(sem("group_done" if end else "mm_done"), 1)

            def product_pair(name, act, ready, before=({}, {})):
                g = number[name]
                hi, lo = act
                for n in range(2):
                    for j in range(PIECES):
                        if n == 0 and j % 2 == 0:
                            for b in range(2):
                                s, v = evac(g - 2 + j // 2, b)
                                e.wait_ge(s, v)
                        if j in before[n]:
                            before[n][j]()
                        c, part, bank = first_chunk[g] + n, 2 * n + j % 2, banks_of(g + j // 2)
                        e.wait_ge(*after(ready, part + 1))
                        e.wait_ge(*after("hi_ready", 4 * c + j + 1))
                        e.wait_ge(*after("lo_dve" if j % 2 == 0 else "lo_pool", 2 * c + j // 2 + 1))
                        begin, end = part == 0, part == 3
                        for kk in range(2):
                            k = 2 * part + kk
                            for t in range(NT):
                                ah, al = (a[:, k, t * P:(t + 1) * P] for a in (hi, lo))
                                out = bank[t][:, :]
                                e.matmul(out, ah, w_hi[:, j, kk, :], start=begin and kk == 0, stop=False)
                                e.matmul(out, ah, w_lo[:, j, kk, :], start=False, stop=False)
                                m = e.matmul(out, al, w_hi[:, j, kk, :], start=False, stop=end and kk == 1)
                        m.then_inc(sem("group_done" if end else "mm_done"), 1)

            def turn(key, src, done=None, banks=range(4)):
                for b in banks:
                    bank = take(b)
                    for kk in range(2):
                        for t in range(NT):
                            at = (kk * NT + t) * P
                            m = e.transpose(bank[:, at:at + P], src(t, 2 * b + kk), ident)
                    m.then_inc(after(key + "_T", 0)[0], 1)
                    freed[b] = (done or key + "_lo", b + 1 if done else 2 * (b + 1))

            def turn_x(key, last, n):
                for t in range(NT):
                    e.wait_ge(*evac(last - 1 + n, t))
                turn(key, lambda t, k: x[:, t, k * P:(k + 1) * P], banks=(2 * n, 2 * n + 1))

            def turn_mem(n):
                e.wait_ge(*after("mem_loaded", 16))
                turn("mem", lambda t, k: R(MEM + t * D + k * P, (1, P)), "mem_copy", (2 * n, 2 * n + 1))

            def rows(key, b):
                e.wait_ge(*after(key + "_rstd", 1))
                bank = take(b)
                for t in range(NT):
                    m = e.matmul(bank[:, t * P:(t + 1) * P], sm(key + "_r", 2)[:, t:t + 1].to_broadcast([P, P]), ident,
                                 start=True, stop=True)
                m.then_inc(after(key + "_rbcmm", 0)[0], 1)
                freed[b] = (key + "_rbc", 1)

            A, B = (a_hi, a_lo), (b_hi, b_lo)

            e.wait_ge(*after("const_loaded", 16))
            e.wait_ge(*after("prow_loaded", 16))
            e.transpose(take(0)[:, 0:NCOLS], prow[:], const[0:NCOLS, 0:NCOLS]).then_inc(sem("cols_T"), 1)
            freed[0] = ("cols_ready", 1)

            def turn_x0(j):
                e.wait_ge(*after(f"x_loaded{j}", 16))
                turn("n0", lambda t, k: x[:, t, k * P:(k + 1) * P], banks=(j,))

            turn_x0(0)
            turn_x0(1)
            product("xbc0", A, "n0_lo", before={0: lambda: turn_x0(2), 1: lambda: turn_x0(3)})
            rows("n0", 0)

            def dt_and_gate():
                e.wait_ge(*after("sw_lo", 1))
                out = take(1)[0:SMALL, 0:L]
                for k in range(KT):
                    e.matmul(out, sw_hi[:, k, :], a_hi[:, k, :], start=k == 0, stop=False)
                    e.matmul(out, sw_hi[:, k, :], a_lo[:, k, :], start=False, stop=False)
                    m = e.matmul(out, sw_lo[:, k, :], a_hi[:, k, :], start=False, stop=k == KT - 1)
                m.then_inc(sem("dg_mm"), 1)
                freed[1] = ("glrt_ready", 2)

            def dt_turn():
                e.wait_ge(*after("glrt_ready", 2))
                bank = take(1)
                for t in range(NT):
                    m = e.transpose(bank[:, t * SH:(t + 1) * SH], glr_t[DT_ROW:SMALL, t * P:(t + 1) * P],
                                    const[DT_ROW:SMALL, DT_ROW:SMALL])
                m.then_inc(sem("dt_T"), 1)
                freed[1] = ("dt_read", 1)

            def gate():
                e.wait_ge(*after("w2g_loaded", 16))
                for t in range(NT):
                    e.matmul(take(2 + t)[:, :], glr_t[0:RANK + 1, t * P:(t + 1) * P], w2g[:], start=True,
                             stop=True).then_inc(sem("g_mm"), 1)
                    freed[2 + t] = ("g_max", t + 1)

            product("xbc1", A, "n0_lo", before={1: dt_and_gate})
            product("xbc2", A, "n0_lo", before={0: dt_turn, 2: gate})

            la = sm("loga", 32)

            def cumulate():
                e.wait_ge(*after("loga", 1))
                bank = take(2)
                for t in range(NT):
                    e.matmul(bank[:, t * SH:(t + 1) * SH], tri, la[:, t * SH:(t + 1) * SH], start=True, stop=True)
                e.matmul(bank[:, 2 * SH:3 * SH], ones, la[:, 0:SH], start=True, stop=True).then_inc(sem("cum_mm"), 1)
                freed[2] = ("cum_ready", 1)

            def decay_rows(t):
                for b in range(4):
                    bank = take(b)
                    for i in range(4):
                        h = 4 * b + i
                        m = e.matmul(bank[:, i * P:(i + 1) * P],
                                     la[:, t * SH + h:t * SH + h + 1].to_broadcast([P, P]), tri, start=True, stop=True)
                    m.then_inc(sem("cumb_mm"), 1)
                    freed[b] = ("seg", 4 * t + b + 1)

            def ssd_turn():
                e.wait_ge(*after("conv_silu", 2))
                for b in range(4):
                    bank = take(b)
                    t, hh = b // 2, b % 2
                    for i in range(4):
                        m = e.transpose(bank[:, i * P:(i + 1) * P], R(CV + (4 * hh + i) * L + t * P, (1, P)), ident)
                    m.then_inc(sem("xs_T"), 1)
                    freed[b] = ("xs_ready", b + 1)

            def ssd_scores():
                for g in range(SG):
                    bank = take(g)
                    lo_, hi_ = g * SN, (g + 1) * SN
                    bt, ct = R(CV + 8 * L, (1, L)), R(CV + 9 * L, (1, L))
                    e.matmul(bank[:, 0:L], bt[lo_:hi_, 0:P], ct[lo_:hi_, :], start=True, stop=True)
                    e.matmul(bank[:, L:L + P], bt[lo_:hi_, P:L], ct[lo_:hi_, P:L], start=True,
                             stop=True).then_inc(sem("ssd_score"), 1)
                    freed[g] = ("ssd_g", 3 * (g + 1))

            def ssd_y(t):
                e.wait_ge(*after("ssd_m", 2 * (t + 1)))
                e.wait_ge(*after("xdt", 2))
                for b in range(2):
                    bank = take(2 * t + b)
                    for i in range(8):
                        h = 8 * b + i
                        m = e.matmul(bank[:, i * SP_:(i + 1) * SP_], R(MM + h * P, (1, P)),
                                     R(XDT + t * D + h * SP_, (1, SP_)), start=True, stop=True)
                    m.then_inc(sem("y_mm"), 1)
                    freed[2 * t + b] = ("y_add", 2 * t + b + 1)

            def ssd_cross():
                e.wait_ge(*after("wx", 1))
                for g in range(SG):
                    e.matmul(take(g)[:, :], R(GG + g * 384 + P, (1, P)), R(WX + g * 512, (1, 512)), start=True,
                             stop=True).then_inc(sem("yc_mm"), 1)
                    freed[g] = ("yc_scaled", g + 1)

            product("q0", A, "n0_lo", before={2: cumulate, 3: lambda: decay_rows(0)})
            product("k0", A, "n0_lo", before={1: lambda: turn_mem(0), 3: lambda: (turn_mem(1), rows("mem", 0))})
            product("z0", A, "n0_lo")
            product("z1", A, "n0_lo", before={1: ssd_turn, 2: ssd_scores})
            product("xk0_0", B, "mg0_lo", before={0: lambda: ssd_y(0), 1: lambda: decay_rows(1)})

            def gla_cumulate():
                e.wait_ge(*after("sp_ready", 2))
                for b in range(2):
                    bank = take(2 + b)
                    for i in range(2):
                        h = 2 * b + i
                        for t in range(NT):
                            at = (i * NT + t) * P
                            m = e.matmul(bank[:, at:at + P], sp[:, t, h * GK:(h + 1) * GK], tri, start=True, stop=True)
                    m.then_inc(sem("gcum_mm"), 1)
                    freed[2 + b] = ("gcum", b + 1)

            def gla_diagonal():
                for n in ("q0", "k0"):
                    for b in range(2):
                        e.wait_ge(*evac(number[n], b))
                for t in range(NT):
                    bank = take(t)
                    for h in range(GH):
                        at = h * L + t * P
                        m = e.matmul(bank[:, h * P:(h + 1) * P], R(QK + at, (1, P)), R(QK + 1024 + at, (1, P)),
                                     start=True, stop=True)
                    m.then_inc(sem("diag_mm"), 1)
                    freed[t] = ("gla_diag", t + 1)

            def level(n):
                buf = GXA if n % 2 == 0 else GXB
                e.wait_ge(*after("gx", n + 1))
                if n == 0:
                    bank = take(0)
                    for h in range(GH):
                        m = e.matmul(bank[:, h * P:(h + 1) * P], R(buf + h * L, (1, P)), R(buf + h * L + P, (1, P)),
                                     start=True, stop=True)
                    m.then_inc(sem("level_mm"), 1)
                    freed[0] = ("gla_cross", 1)
                    return
                for t in range(NT):
                    b = 2 * (n % 2) + t
                    bank = take(b)
                    for h in range(GH):
                        xx = R(buf + h * L + t * P, (1, P))
                        m = e.matmul(bank[:, h * P:(h + 1) * P], xx, xx, start=True, stop=True)
                    m.then_inc(sem("level_mm"), 1)
                    freed[b] = ("gla_s", 2 * (n - 1) + t + 1)

            def turn_y():
                e.wait_ge(*after("yn", 4))
                turn("y", lambda t, k: R(XS + t * D + k * P, (1, P)))

            product("xk0_1", B, "mg0_lo", before={1: lambda: ssd_y(1), 2: ssd_cross, 3: gla_cumulate})
            product("xv0_0", B, "mg0_lo", before={0: gla_diagonal})
            product("xv0_1", B, "mg0_lo", before={0: lambda: level(0), 2: lambda: level(1)})
            product("v0", A, "n0_lo", before={0: lambda: level(2), 2: lambda: level(3)})
            product("v1", A, "n0_lo", before={0: lambda: level(4), 2: lambda: level(5)})
            product("r0", A, "n0_lo", before={0: lambda: level(6), 2: lambda: level(7)})
            product("r1", A, "n0_lo", before={1: turn_y})

            def gla_out():
                for n in ("v0", "v1"):
                    for b in range(2):
                        e.wait_ge(*evac(number[n], b))
                e.wait_ge(*after("gla_s", 14))
                for t in range(NT):
                    for b in range(2):
                        bank = take(2 * t + b)
                        for i in range(2):
                            h = 2 * b + i
                            out = bank[:, i * GV:(i + 1) * GV]
                            m = e.matmul(out, R(STT_ + t * 512 + h * P, (1, P)), R(VV + t * D + h * GV, (1, GV)),
                                         start=True, stop=t == 0)
                            if t == 1:
                                m = e.matmul(out, R(SXT + h * P, (1, P)), R(VV + h * GV, (1, GV)), start=False,
                                             stop=True)
                        m.then_inc(sem("o_mm"), 1)
                        freed[2 * t + b] = ("on", 2 * (2 * t + b + 1))

            def turn_o():
                e.wait_ge(*after("on", 8))
                turn("o", lambda t, k: R(OO + t * D + k * P, (1, P)))

            product("outy0", B, "y_lo", before={0: gla_out})
            product("outy1", B, "y_lo", before={2: turn_o})
            product("outo0", A, "o_lo")
            product("outo1", A, "o_lo", before={1: lambda: turn_x("xn0", number["outo1"], 0)})

            def tail(l, one, two):
                def scores(hh):
                    for b in range(2):
                        e.wait_ge(*evac(number[f"xq{l}_{hh}"], b))
                    for t in range(NT):
                        bank = take(2 * hh + t)
                        for i in range(2):
                            h = 2 * hh + i
                            for dd in range(2):
                                m = e.matmul(bank[:, i * NM:(i + 1) * NM], R(CQ + (2 * h + dd) * L + t * P, (1, P)),
                                             xk[:, 2 * h + dd, :], start=dd == 0, stop=dd == 1)
                        m.then_inc(after(f"c{l}_score", 0)[0], 1)
                        freed[2 * hh + t] = (f"c{l}_exp", 4 * hh + 2 * (t + 1))

                def p_turn(hh):
                    e.wait_ge(*after(f"c{l}_p", 4 * (hh + 1)))
                    for mt in range(2):
                        bank = take(2 * hh + mt)
                        for i in range(2):
                            h = 2 * hh + i
                            for t in range(NT):
                                at = (i * NT + t) * P
                                m = e.transpose(bank[:, at:at + P], R(CP + (t * XH + h) * NM + mt * P, (1, P)), ident)
                        m.then_inc(after(f"c{l}_pT", 0)[0], 1)
                        freed[2 * hh + mt] = (f"c{l}_pt", 2 * hh + mt + 1)

                def values(hh):
                    e.wait_ge(*after(f"c{l}_pt", 2 * (hh + 1)))
                    for h in (2 * hh, 2 * hh + 1):
                        bank = take(h)
                        for vv in range(2):
                            for mt in range(2):
                                m = e.matmul(bank[:, vv * L:(vv + 1) * L],
                                             xv[:, mt, h * XHD + vv * P:h * XHD + (vv + 1) * P],
                                             R(CPT + (mt * XH + h) * L, (1, L)), start=mt == 0, stop=mt == 1)
                        m.then_inc(after(f"c{l}_T", 0)[0], 1)
                        freed[h] = (f"c{l}_lo", h + 1)

                product(f"xq{l}_0", one, f"xn{l}_lo",
                        before={1: lambda: turn_x(f"xn{l}", number["outo1" if l == 0 else "dout1"], 1)})
                product(f"xq{l}_1", one, f"xn{l}_lo", before={1: lambda: scores(0), 3: lambda: p_turn(0)})
                values(0)
                scores(1)
                product_pair(f"xo{l}_0", two, f"c{l}_lo", ({2: lambda: p_turn(1), 3: lambda: values(1)},
                                                          {3: lambda: turn_x(f"mn{l}", number[f"xo{l}_1"], 0)}))
                product(f"up{l}_0", one, f"mn{l}_lo", before={1: lambda: turn_x(f"mn{l}", number[f"xo{l}_1"], 1)})
                for n in range(1, UP_PEEL):
                    product(f"up{l}_{n}", one, f"mn{l}_lo")
                looped_groups = [number[f"up{l}_{n}"] for n in range(UP_PEEL, UP_PEEL + PAIR)]
                with e.Fori(0, UP_PASSES) as i:
                    now = passes(e, i, [at for g in looped_groups for at in
                                     [(evac(g - 2, 0)[1], 1)] + split_steps(first_chunk[g])])
                    for n in range(UP_PEEL, UP_PEEL + PAIR):
                        product(f"up{l}_{n}", one, f"mn{l}_lo", now=now)
                product(f"down{l}_0", (hid_hi, hid_lo), f"hid{l}", 1)
                product(f"down{l}_1", (hid_hi, hid_lo), f"hid{l}", 1,
                        before={1: lambda: turn_x("n1", number["down0_1"], 0)} if l == 0 else {})

            tail(0, B, A)

            def diff_scores(r):
                t, per, first = ROUNDS[r]
                keys = (t + 1) * P
                for n in (("dq0", "dk0"), ("dq1", "dk1"), ())[r]:
                    for b in range(2):
                        e.wait_ge(*evac(number[n], b))
                for pair in range(2):
                    bank = [take(2 * pair + m_) for m_ in range(2)]
                    for i in range(per):
                        h = first + per * pair + i
                        for m_ in range(2):
                            q = R(DQ + h * L + t * P, (1, P))[m_ * DHD:(m_ + 1) * DHD, :]
                            k = R(DK + h * L, (1, keys))[m_ * DHD:(m_ + 1) * DHD, :]
                            m = e.matmul(bank[m_][:, i * keys:(i + 1) * keys], q, k, start=True, stop=True)
                            if i == per - 1:
                                m.then_inc(sem("d_score"), 1)
                    for b in (2 * pair, 2 * pair + 1):
                        freed[b] = ("d_bias", 4 * r + b + 1)

            def diff_turn(r):
                e.wait_ge(*after("d_an", (4, 12, 16)[r]))
                for b in range(2):
                    bank = take(b)
                    for i in range(4):
                        n = 4 * b + i
                        m = e.transpose(bank[:, i * P:(i + 1) * P], R(AN + n * P, (1, P)), ident)
                    m.then_inc(sem("d_anT"), 1)
                    freed[b] = ("d_at", 2 * r + b + 1)

            def diff_out():
                for n in ("dv0", "dv1"):
                    for b in range(2):
                        e.wait_ge(*evac(number[n], b))
                e.wait_ge(*after("d_at", 6))
                for t in range(NT):
                    for b in range(2):
                        bank = take(2 * t + b)
                        for i in range(4):
                            h = 4 * b + i
                            for s in range(t + 1):
                                slot = AT_TILE0 + h if t == 0 else (2 * h + s if h < 4 else 8 + 2 * h + s)
                                m = e.matmul(bank[:, i * P:(i + 1) * P], R(AT + slot * P, (1, P)),
                                             R(DV + s * D + h * P, (1, P)), start=s == 0, stop=s == t)
                        m.then_inc(sem("do_mm"), 1)
                        freed[2 * t + b] = ("d_on", 2 * t + b + 1)

            def turn_d():
                e.wait_ge(*after("d_on", 4))
                turn("d", lambda t, k: R(SC + t * D + k * P, (1, P)))

            product("dq0", A, "n1_lo", before={1: lambda: turn_x("n1", number["down0_1"], 1)})
            product("dk0", A, "n1_lo", before={2: lambda: rows("n1", 2)})
            product("dq1", A, "n1_lo", before={1: lambda: diff_scores(0)})
            product("dk1", A, "n1_lo", before={2: lambda: diff_turn(0)})
            product("dv0", A, "n1_lo", before={1: lambda: diff_scores(1)})
            product("dv1", A, "n1_lo", before={3: lambda: diff_turn(1)})
            product("xk1_0", B, "mg1_lo", before={0: lambda: diff_scores(2)})
            product("xk1_1", B, "mg1_lo", before={2: lambda: diff_turn(2), 3: diff_out})
            product("xv1_0", B, "mg1_lo")
            product("xv1_1", B, "mg1_lo", before={1: turn_d})
            product("dout0", A, "d_lo")
            product("dout1", A, "d_lo", before={1: lambda: turn_x("xn1", number["dout1"], 0)})
            tail(1, B, A)

        @block.scalar
        def _(e):
            op, settle, link, looped = tracker(e, "act_step")

            def split(c, before={}, now=first):
                for j in range(PIECES):
                    if j in before:
                        before[j]()
                    if c >= len(chunks):
                        continue
                    width = chunks[c][3]
                    e.wait_ge(*later(after(f"raw_ready{j}", 16 * (c + 1)), 16 * PAIR, now))
                    if c > 0:
                        e.wait_ge(*later(*freed_at(c - 1, j), now))
                    op(e.activation(w_hi[:, j, :, 0:width], raw[:, j, :, 0:width], ACT.Copy), "hi_ready")
                if PIECES in before:
                    before[PIECES]()

            def ahead(name, before={}, now=first):
                g = number[name]
                n = len(groups[g][2])
                for k in range(n):
                    split(first_chunk[g] + k + 1, before if k == n - 1 else {}, now)
                return g

            def done(g, now=first):
                e.wait_ge(*later(after("group_done", g + 1), PAIR, now))

            def copy0(name, dst, scale=1.0, before={}):
                g = ahead(name, before)
                done(g)
                s, v = evac(g, 0)
                op(e.activation(dst, bank_view(g, 0, dst), ACT.Copy, scale=scale), s.name, v)

            def sumsq(key, srcs):
                ss = sm(key + "_ss", 4)
                for n, src, ready in srcs:
                    if ready:
                        e.wait_ge(*ready)
                    width = src.shape[-1]
                    link(e.activation(junk[:].rearrange("p a b -> p (a b)")[:, 0:width], src, ACT.Square,
                                      accum_out=ss[:, n:n + 1]), key + "_sq")

            def hi_parts(key, act, gain, banks=range(4)):
                for b in banks:
                    e.wait_ge(*after(key + "_T", b + 1))
                    for kk in range(2):
                        k = 2 * b + kk
                        op(e.activation(act[:, k, :], X_[b][:, kk * L:(kk + 1) * L], ACT.Copy, scale=gain(k)),
                           key + "_hi")

            def squares_x(key, last, n):
                sumsq(key, [(2 * n + t, x[:, t, n * 512:(n + 1) * 512], evac(last - 1 + n, t)) for t in range(NT)])

            def mem_hi(l):
                for k in range(KT):
                    if l == 0:
                        e.wait_ge(*after("mem_copy", k // 2 + 1))
                    op(e.activation(b_hi[:, k, :], mem_t[:, k, :], ACT.Copy, scale=col(f"mem{l}", k)), f"mg{l}_hi")

            e.wait_ge(*after("cols_T", 1))
            link(e.activation(cols[:], X_[0][:, 0:NCOLS], ACT.Copy), "cols_ready")
            split(0, {j: lambda j=j: hi_parts("n0", a_hi, lambda k: col("ev", k), (j,)) for j in range(PIECES)})
            ss = sm("n0_ss", 4)
            sumsq("n0", [(2 * n + t, x[:, t, n * 512:(n + 1) * 512], None) for n in range(2) for t in range(NT)])
            e.wait_ge(*after("sw_loaded", 16))
            op(e.activation(sw_hi[:], sw[:], ACT.Copy), "sw_hi")
            e.wait_ge(*after("row_loaded", 16))
            op(e.activation(sm("ea", 16), row[:, 16:32], ACT.Exp), "ea")
            e.wait_ge(*after("mem_loaded", 16))
            ahead("xbc0")
            sumsq("mem", [(2 * n + t, R(MEM + t * D + n * 512, (1, 512)), None) for n in range(2) for t in range(NT)])

            def dt_exp():
                e.wait_ge(*after("dt_na", 1))
                op(e.activation(sm("dt_u", 32), sm("dt_n", 32), ACT.Exp), "dt_u")

            ahead("xbc1")
            ahead("xbc2", {1: dt_exp})
            for t in range(NT):
                e.wait_ge(*after("g_mm", t + 1))
                link(e.activation(junk[:, t, :], X_[2 + t][:, :], ACT.Abs), "g_abs")

            def gate_ln():
                link(e.activation(junk[:], junk[:], ACT.Exp, scale=-1.0))
                op(e.activation(junk[:], junk[:], ACT.Ln, bias=1.0), "g_ln")

            def decay_factors():
                e.wait_ge(*after("cum_ready", 2))
                op(e.activation(sm("wts", 16), sm("wts", 16), ACT.Exp), "wts")
                op(e.activation(sm("e1", 16), sm("cc", 48)[:, 16:32], ACT.Exp), "e1")

            def ssd_exp(t):
                e.wait_ge(*after("seg_min", t + 1))
                link(e.activation(R(MM, (1, 2048)), R(MM, (1, 2048)), ACT.Exp), "ssd_exp")

            def tanh_gate(name, n, base, before={}):
                g = ahead(f"{name}{n}", before)
                done(g)
                for t in range(NT):
                    op(e.activation(R(base + t * D + n * 512, (1, 512)), banks_of(g)[t][:, :], ACT.Tanh,
                                    scale=sm("n0_hr", 2)[:, t:t + 1]), name + "_tanh")

            def conv_first(cs):
                for n in ("xbc0", "xbc1"):
                    for b in range(2):
                        e.wait_ge(*evac(number[n], b))
                e.wait_ge(*evac(number["xbc2"], 0))
                e.wait_ge(*after("half", 1))
                for c in cs:
                    op(e.activation(R(CV + c * L, (1, L)), R(XB + c * XBW, (1, L)), ACT.Identity,
                                    bias=half[:, 40 + c:41 + c], scale=half[:, c:c + 1]), "conv_first")

            def mem_copy(bs):
                for b in bs:
                    e.wait_ge(*after("mem_T", b + 1))
                    op(e.activation(mem_t[:, 2 * b:2 * b + 2, :], X_[b][:, :].rearrange("p (a b) -> p a b", a=2),
                                    ACT.Copy), "mem_copy")

            ahead("q0", {0: lambda: conv_first(range(5)), 1: lambda: conv_first(range(5, XT)),
                         3: lambda: (decay_factors(), gate_ln())})
            ahead("k0", {0: lambda: ssd_exp(0), 1: lambda: mem_copy((0, 1)), 3: lambda: mem_copy((2, 3))})
            mem_hi(0)
            def conv_tanh():
                for n in range(2):
                    at, size = n * XT // 2 * L, XT // 2 * L
                    e.wait_ge(*after("conv", (n + 1) * XT // 2))
                    op(e.activation(R(TT + at, (1, size)), R(CV + at, (1, size)), ACT.Tanh), "conv_tanh")

            tanh_gate("z", 0, ZZ, {1: conv_tanh})

            def xs_copy():
                for b in range(4):
                    e.wait_ge(*after("xs_T", b + 1))
                    op(e.activation(R(XS + b * 512, (1, 512)), X_[b][:, :], ACT.Copy), "xs_ready")

            tanh_gate("z", 1, ZZ, {1: xs_copy})
            ahead("xk0_0", {2: lambda: ssd_exp(1)})
            ahead("xk0_1")

            def neg_cum():
                e.wait_ge(*after("gcum", 2))
                op(e.activation(R(CC2, (1, 1024)), R(CC2 + 1024, (1, 1024)), ACT.Copy, scale=-1.0), "gneg")

            def gla_exp(n):
                buf = GXA if n % 2 == 0 else GXB
                e.wait_ge(*after("gd", n + 1))
                if n == 0:
                    op(e.activation(R(buf + P, (L, GH), (1, P)), R(CC2 + 1024 + P, (L, GH), (1, P)), ACT.Exp))
                    link(e.activation(R(buf, (L, GH), (1, P)), R(buf, (L, GH), (1, P)), ACT.Exp), "ge")
                else:
                    link(e.activation(R(buf, (1, 1024)), R(buf, (1, 1024)), ACT.Exp), "ge")

            def y_squares():
                e.wait_ge(*after("yz", 2))
                sumsq("y", [(2 * t + g, R(XS + t * D + g * 512, (1, 512)), None) for t in range(NT) for g in range(SG)])

            rm = sm("mem_r", 2)
            copy0("xv0_0", xv[:, 0, 0:512], rm[:, 0:1],
                  {0: neg_cum, 1: lambda: gla_exp(0), 2: y_squares, 3: lambda: gla_exp(1)})

            copy0("xv0_1", xv[:, 0, 512:1024], rm[:, 0:1], {1: lambda: gla_exp(2), 3: lambda: gla_exp(3)})
            rx = sm("n0_r", 2)
            copy0("v0", R(VV, (1, 512)), rx[:, 0:1], {1: lambda: gla_exp(4), 3: lambda: gla_exp(5)})
            copy0("v1", R(VV + 512, (1, 512)), rx[:, 0:1], {1: lambda: gla_exp(6), 3: lambda: gla_exp(7)})
            tanh_gate("r", 0, RR)
            tanh_gate("r", 1, RR, {1: lambda: hi_parts("y", b_hi, lambda k: col("ssdn", k))})

            def o_squares():
                ss = sm("o_ss", 8)
                for b in range(4):
                    e.wait_ge(*after("o_mm", b + 1))
                    for i in range(2):
                        link(e.activation(junk[:, 0, 0:GV], X_[b][:, i * GV:(i + 1) * GV], ACT.Square,
                                          accum_out=ss[:, 2 * b + i:2 * b + i + 1]), "o_sq")

            ahead("outy0", {0: o_squares})
            ahead("outy1", {2: lambda: hi_parts("o", a_hi, lambda k: col("glan", k % 2))})
            ahead("outo0")

            def half_ready(key, last, dst, gain):
                def f():
                    hi_parts(key, dst, gain, (0, 1))
                    squares_x(key, last, 0)
                return f

            ahead("outo1", {1: half_ready("xn0", number["outo1"], b_hi, lambda k: col("xa0", k))})

            def rest(key, last, dst, gain):
                hi_parts(key, dst, gain, (2, 3))
                squares_x(key, last, 1)

            def tail(l, one, two):
                rest(f"xn{l}", number["outo1" if l == 0 else "dout1"], one[0], lambda k: col(f"xa{l}", k))
                rs = sm(f"c{l}_sum", 8)

                def exps(hh):
                    for t in range(NT):
                        e.wait_ge(*after(f"c{l}_max", 2 * hh + t + 1))
                        for i in range(2):
                            n = t * XH + 2 * hh + i
                            op(e.activation(R(CP + n * NM, (1, NM)), X_[2 * hh + t][:, i * NM:(i + 1) * NM], ACT.Exp,
                                            bias=sm(f"c{l}_nmax", 8)[:, n:n + 1], scale=sm(f"xn{l}_s", 2)[:, t:t + 1],
                                            accum_out=rs[:, n:n + 1]), f"c{l}_exp")

                def pt_copy(hh):
                    for mt in range(2):
                        e.wait_ge(*after(f"c{l}_pT", 2 * hh + mt + 1))
                        op(e.activation(R(CPT + (mt * XH + 2 * hh) * L, (1, 512)), X_[2 * hh + mt][:, :], ACT.Copy),
                           f"c{l}_pt")

                def o_hi(hh):
                    for h in (2 * hh, 2 * hh + 1):
                        e.wait_ge(*after(f"c{l}_T", h + 1))
                        op(e.activation(two[0][:, 2 * h:2 * h + 2, :], X_[h][:, :].rearrange("p (a b) -> p a b", a=2),
                                        ACT.Copy), f"c{l}_hi")

                copy0(f"xq{l}_0", R(CQ, (L, 2), (1, L)))
                copy0(f"xq{l}_1", R(CQ + 4 * L, (L, 2), (1, L)), 1.0, {1: lambda: exps(0), 3: lambda: pt_copy(0)})
                o_hi(0)
                exps(1)
                ahead(f"xo{l}_0", {2: lambda: pt_copy(1), 3: lambda: o_hi(1)})
                ahead(f"xo{l}_1", {3: half_ready(f"mn{l}", number[f"xo{l}_1"], one[0], lambda k: col(f"mlp{l}", k))})
                rest(f"mn{l}", number[f"xo{l}_1"], one[0], lambda k: col(f"mlp{l}", k))

                def hidden(n, now=first):
                    g = ahead(f"up{l}_{n}", {}, now)
                    done(g, now)
                    for b in range(2):
                        if n > 0:
                            e.wait_ge(*later(after("hid_sq", 16 * l + 2 * n + b - 1), 2 * PAIR, now))
                        s, v = evac(g, b)
                        op(e.activation(junk[:, b, :], banks_of(g)[b][:, :], ACT.Relu), s.name, v)
                    for b in range(2):
                        e.wait_ge(*later(after("hid_sq", 16 * l + 2 * n + b + 1), 2 * PAIR, now))
                        op(e.activation(hid_hi[:, bass.ds(now(4 * n + 2 * b, 4 * PAIR), 2), :],
                                        sp[:, b, :].rearrange("p (a c) -> p a c", a=2), ACT.Copy), "hid_hi")

                def act_steps(n):
                    g = number[f"up{l}_{n}"]
                    c = first_chunk[g] + 1
                    squares = [(after("hid_sq", 16 * l + 2 * n + b)[1], 2 * PAIR) for b in (-1, 0, 1, 2)]
                    places = [(4 * n + 2 * b, 4 * PAIR) for b in range(2)]
                    free = [(at[1], step) for at, step in (freed_at(c - 1, j) for j in range(PIECES))]
                    return [(16 * (c + 1), 16 * PAIR), (g + 1, PAIR)] + squares + places + free

                for n in range(UP_PEEL):
                    hidden(n)
                start = looped()
                with e.Fori(0, UP_PASSES) as i:
                    now = passes(e, i, [at for n in range(UP_PEEL, UP_PEEL + PAIR) for at in act_steps(n)])
                    for n in range(UP_PEEL, UP_PEEL + PAIR):
                        hidden(n, now)
                looped(start)
                ahead(f"down{l}_0")
                if l == 0:
                    ahead("down0_1", {1: half_ready("n1", number["down0_1"], a_hi, lambda k: col("od", k))})
                else:
                    ahead("down1_1", {3: lambda: squares_x("fin", number["down1_1"], 0)})

            tail(0, (b_hi, b_lo), (a_hi, a_lo))

            rest("n1", number["down0_1"], a_hi, lambda k: col("od", k))

            def lam_exp():
                e.wait_ge(*after("lam_dot", 1))
                op(e.activation(sm("lam_e", 2), sm("lam_d", 2), ACT.Exp), "lam_e")

            def diff_exp(r, part):
                t, per, _ = ROUNDS[r]
                keys = (t + 1) * P
                at = (0, 8, 24)[r]
                e.wait_ge(*after("d_max", r + 1))
                base = SC + 2048 * (r % 2)
                for n in range(2 * per * part, 2 * per * (part + 1)):
                    v = R(base + n * keys, (1, keys))
                    op(e.activation(v, v, ACT.Exp, bias=sm("d_nmax", 32)[:, at + n:at + n + 1],
                                    accum_out=sm("d_sum", 32)[:, at + n:at + n + 1]), "d_exp")

            def at_copy(r):
                for b in range(2):
                    e.wait_ge(*after("d_anT", 2 * r + b + 1))
                    op(e.activation(R(AT + (2 * r + b) * 512, (1, 512)), X_[b][:, :], ACT.Copy), "d_at")

            r1 = sm("n1_r", 2)
            copy0("dq0", R(DQ, (L, 2), (1, L)), DHD ** -0.5, {2: lam_exp})
            ahead("dk0")
            copy0("dq1", R(DQ + 4 * L, (L, 2), (1, L)), DHD ** -0.5, 
                  {2: lambda: diff_exp(0, 0), 3: lambda: diff_exp(0, 1)})
            ahead("dk1", {1: lambda: mem_hi(1), 2: lambda: at_copy(0)})
            copy0("dv0", R(DV, (1, 512)), r1[:, 0:1], {2: lambda: diff_exp(1, 0), 3: lambda: diff_exp(1, 1)})
            copy0("dv1", R(DV + 512, (1, 512)), r1[:, 0:1], {3: lambda: at_copy(1)})
            ahead("xk1_0", {1: lambda: diff_exp(2, 0), 2: lambda: diff_exp(2, 1)})

            def do_squares():
                for b in range(4):
                    e.wait_ge(*after("do_mm", b + 1))
                    if b >= 2:
                        e.wait_ge(*after("do_sum", b - 1))
                    op(e.activation(junk[:, b % 2, :], X_[b][:, :], ACT.Square), "do_sq")

            ahead("xk1_1", {2: lambda: at_copy(2), 3: do_squares})
            copy0("xv1_0", xv[:, 0, 0:512], rm[:, 0:1])
            copy0("xv1_1", xv[:, 0, 512:1024], rm[:, 0:1], {1: lambda: hi_parts("d", a_hi, lambda k: col("subln"))})
            ahead("dout0")
            ahead("dout1", {1: half_ready("xn1", number["dout1"], b_hi, lambda k: col("xa1", k))})
            tail(1, (b_hi, b_lo), (a_hi, a_lo))
            squares_x("fin", number["down1_1"], 1)
            e.wait_ge(*after("fin_rstd", 1))
            e.wait_ge(*after("fin_gain", 4))
            for n in range(2):
                v = result(1, n)
                op(e.activation(v, v, ACT.Copy, scale=sm("fin_r", 2)[:, 1:2]), "final1")

        @block.vector
        def _(e):
            op, settle, link, looped = tracker(e, "dve_step")

            def split(c, before={}, now=first):
                for j in range(PIECES):
                    if j in before:
                        before[j]()
                    if c >= len(chunks) or j % 2:
                        continue
                    width = chunks[c][3]
                    e.wait_ge(*later(after("hi_ready", 4 * c + j + 1), PAIR * PIECES, now))
                    op(e.tensor_tensor(w_lo[:, j, :, 0:width], raw[:, j, :, 0:width],
                                       w_hi[:, j, :, 0:width].bitcast(F32), ALU.subtract), "lo_dve")
                if PIECES in before:
                    before[PIECES]()

            def ahead(name, before={}, now=first):
                g = number[name]
                n = len(groups[g][2])
                for k in range(n):
                    split(first_chunk[g] + k + 1, before if k == n - 1 else {}, now)
                return g

            def done(g, now=first):
                e.wait_ge(*later(after("group_done", g + 1), PAIR, now))

            def copy1(name, dst, scale=None, before={}):
                g = ahead(name, before)
                done(g)
                s, v = evac(g, 1)
                src = bank_view(g, 1, dst)
                if scale is None:
                    op(e.tensor_copy(dst, src), s.name, v)
                else:
                    op(e.tensor_scalar(dst, src, scale, None, ALU.mult), s.name, v)

            def by_rows(name, dsts, key, scale=1.0, before={}):
                g = ahead(name, before)
                done(g)
                e.wait_ge(*after(key + "_rbc", 1))
                r = rbc[key][:].unsqueeze(1).to_broadcast([P, 2, L])
                for b, dst in enumerate(dsts):
                    s, v = evac(g, b)
                    op(e.scalar_tensor_tensor(out=dst, in0=bank_view(g, b, dst), scalar=scale, in1=r, op0=ALU.mult,
                                              op1=ALU.mult), s.name, v)

            def add_x(name, n, scale=None, before={}):
                add_bank(ahead(name, before), n, scale)

            def add_bank(g, n, scale=None):
                done(g)
                for t in range(NT):
                    s, v = evac(g, t)
                    xx = x[:, t, n * 512:(n + 1) * 512]
                    if scale is None:
                        op(e.tensor_tensor(xx, xx, banks_of(g)[t][:, :], ALU.add), s.name, v)
                    else:
                        op(e.scalar_tensor_tensor(out=xx, in0=banks_of(g)[t][:, :], scalar=scale[:, t:t + 1], in1=xx,
                                                  op0=ALU.mult, op1=ALU.add), s.name, v)

            def lo_parts(key, act, gain, banks=range(4)):
                for b in banks:
                    e.wait_ge(*after(key + "_hi", 2 * (b + 1)))
                    for kk in range(2):
                        k = 2 * b + kk
                        op(e.scalar_tensor_tensor(out=act[1][:, k, :], in0=X_[b][:, kk * L:(kk + 1) * L],
                                                  scalar=gain(k), in1=act[0][:, k, :].bitcast(F32), op0=ALU.mult,
                                                  op1=ALU.subtract), key + "_lo")

            def row_copy(key, b):
                e.wait_ge(*after(key + "_rbcmm", 1))
                link(e.tensor_copy(rbc[key][:], X_[b][:, 0:L]), key + "_rbc")

            A, B = (a_hi, a_lo), (b_hi, b_lo)
            split(0, {j: lambda j=j: lo_parts("n0", A, lambda k: col("ev", k), (j,)) for j in range(PIECES)})
            op(e.tensor_scalar(half[:], cols[:, COLS["convw"]:COLS["convw"] + 50], 0.5, None, ALU.mult), "half")
            e.wait_ge(*after("sw_hi", 1))
            op(e.tensor_tensor(sw_lo[:], sw[:], sw_hi[:].bitcast(F32), ALU.subtract), "sw_lo")
            ahead("xbc0")
            row_copy("n0", 0)

            def xb(c):
                return R(XB + c * XBW + 3, (XBW, 2), (1, L))

            def evac_rows(name, dsts, key):
                g = number[name]
                done(g)
                r = rbc[key][:].unsqueeze(1).to_broadcast([P, 2, L])
                for b, dst in enumerate(dsts):
                    s, v = evac(g, b)
                    op(e.tensor_tensor(dst, bank_view(g, b, dst), r, ALU.mult), s.name, v)

            e.wait_ge(*after("pad_ready", 1))
            evac_rows("xbc0", (xb(0), xb(2)), "n0")

            def small_rows():
                e.wait_ge(*after("ones_ready", 1))
                e.wait_ge(*after("dg_mm", 1))
                for rows in (slice(0, RANK), slice(DT_ROW, SMALL)):
                    op(e.tensor_tensor(glr_t[rows, :], X_[1][rows, 0:L], rbc["n0"][rows, :], ALU.mult), "glrt_ready")

            by_rows("xbc1", (xb(4), xb(6)), "n0", 1.0, {2: small_rows})

            v, n_, u, s1, s2, pp = (sm(k, 32) for k in ("dt_v", "dt_n", "dt_u", "dt_s", "dt_s2", "dt_p"))
            dtb = row[:, 0:16].unsqueeze(1).to_broadcast([P, NT, 16])
            dt = sm("dt", 32)

            def two(a):
                return a.rearrange("p (t h) -> p t h", t=NT)

            def dt_start():
                e.wait_ge(*after("dt_T", 1))
                link(e.tensor_tensor(two(v), two(X_[1][:, 0:2 * SH]), dtb, ALU.add), "dt_read")
                link(e.scalar_tensor_tensor(out=n_, in0=v, scalar=-1.0, in1=v, op0=ALU.mult, op1=ALU.min), "dt_na")

            def dt_end():
                e.wait_ge(*after("dt_u", 1))
                link(e.tensor_scalar(s1, u, 2.0, None, ALU.add))
                link(e.reciprocal(s2, s1))
                link(e.tensor_tensor(s1, u, s2, ALU.mult))
                link(e.tensor_tensor(s2, s1, s1, ALU.mult))
                link(e.tensor_scalar(pp, s2, 1.0 / 17, None, ALU.mult))
                for k in (15, 13, 11, 9, 7, 5, 3):
                    link(e.scalar_tensor_tensor(out=pp, in0=pp, scalar=1.0 / k, in1=s2, op0=ALU.add, op1=ALU.mult))
                link(e.scalar_tensor_tensor(out=pp, in0=pp, scalar=1.0, in1=s1, op0=ALU.add, op1=ALU.mult))
                link(e.tensor_scalar(v, v, 0.0, None, ALU.max))
                link(e.scalar_tensor_tensor(out=dt, in0=pp, scalar=2.0, in1=v, op0=ALU.mult, op1=ALU.add))
                e.wait_ge(*after("ea", 1))
                ea = sm("ea", 16).unsqueeze(1).to_broadcast([P, NT, 16])
                link(e.tensor_tensor(two(pp), two(dt), ea, ALU.mult))
                link(e.tensor_scalar(sm("loga", 32), pp, -1.0, None, ALU.mult), "loga")

            g = ahead("xbc2", {0: dt_start, 2: dt_end})
            done(g)
            s, n = evac(g, 0)
            dst = R(XB + 8 * XBW + 3, (XBW, 2), (1, L))
            op(e.tensor_tensor(dst, bank_view(g, 0, dst), rbc["n0"][:].unsqueeze(1).to_broadcast([P, 2, L]), ALU.mult),
               s.name, n)
            op(e.memset(sm("spare", 1), 0.0), evac(g, 1)[0].name, evac(g, 1)[1])
            for t in range(NT):
                e.wait_ge(*after("g_abs", t + 1))
                op(e.tensor_scalar(sp[:, t, :], X_[2 + t][:, :], -1.0, 0.0, ALU.mult, ALU.max), "g_max")

            def tap(j, c):
                return half[:, j * XT + c:j * XT + c + 1]

            def conv(j):
                settle()
                for c in range(XT):
                    if j == 1:
                        e.wait_ge(*after("conv_first", c + 1))
                    dst = R(CV + c * L, (1, L))
                    op(e.scalar_tensor_tensor(out=dst, in0=R(XB + c * XBW + j, (1, L)), scalar=tap(j, c), in1=dst,
                                              op0=ALU.mult, op1=ALU.add), "conv" if j == TAPS - 1 else None)

            cc = sm("cc", 48)

            def cum_copy():
                e.wait_ge(*after("cum_mm", 1))
                link(e.tensor_copy(cc, X_[2][:, 0:48]), "cum_ready")
                link(e.tensor_tensor(sm("wts", 16), cc[:, 32:48], cc[:, 0:16], ALU.subtract), "cum_ready")

            def heads(ap, n=SP_):
                return ap.unsqueeze(2).to_broadcast([P, ap.shape[1], n])

            def decay(t):
                for b in range(4):
                    e.wait_ge(*after("cumb_mm", 4 * t + b + 1))
                    op(e.tensor_tensor(R(MM + b * 512, (P, 4), (1, P)), X_[b][:, :].rearrange("p (h q) -> p h q", h=4),
                                       heads(cc[:, t * SH + 4 * b:t * SH + 4 * b + 4], P), ALU.subtract), "seg")
                settle()
                link(e.tensor_scalar(R(MM, (1, 2048)), R(MM, (1, 2048)), 0.0, None, ALU.min), "seg_min")

            def weigh(t):
                e.wait_ge(*after("ssd_exp", t + 1))
                for g in range(SG):
                    m = R(MM + g * 1024, (P, 8), (1, P))
                    op(e.tensor_tensor(m, m, R(GG + g * 384 + 2 * P * t, (0, 8), (1, P)), ALU.mult), "ssd_m")

            def soft_gate():
                e.wait_ge(*after("g_ln", 1))
                for t in range(NT):
                    op(e.tensor_tensor(sp[:, t, :], sp[:, t, :], junk[:, t, :], ALU.add), "sp_ready")

            qk_rows = lambda base: (R(base, (L, 2), (1, L)), R(base + 512, (L, 2), (1, L)))
            by_rows("q0", qk_rows(QK + 1024), "n0", GK ** -0.5,
                    {2: lambda: (cum_copy(), conv(1)), 3: lambda: decay(0)})
            by_rows("k0", qk_rows(QK), "n0", 1.0,
                    {0: lambda: conv(2), 1: soft_gate, 3: lambda: (conv(3), row_copy("mem", 0))})

            def gated(name, n, base, before={}):
                g = ahead(f"{name}{n}", before)
                for t in range(NT):
                    e.wait_ge(*after(name + "_tanh", 2 * n + t + 1))
                    s, v = evac(g, t)
                    dst = R(base + t * D + n * 512, (1, 512))
                    op(e.scalar_tensor_tensor(out=dst, in0=dst, scalar=1.0, in1=banks_of(g)[t][:, :], op0=ALU.add,
                                              op1=ALU.mult), s.name, v)

            def conv_silu():
                for n in range(2):
                    at, size = n * XT // 2 * L, XT // 2 * L
                    e.wait_ge(*after("conv_tanh", n + 1))
                    op(e.scalar_tensor_tensor(out=R(CV + at, (1, size)), in0=R(TT + at, (1, size)), scalar=1.0,
                                              in1=R(CV + at, (1, size)), op0=ALU.add, op1=ALU.mult), "conv_silu")

            gated("z", 0, ZZ, {2: conv_silu})

            def ssd_g():
                for g in range(SG):
                    e.wait_ge(*after("ssd_score", g + 1))
                    G = GG + g * 384
                    op(e.tensor_tensor(R(G, (1, P)), X_[g][:, 0:P], tri, ALU.mult), "ssd_g")
                    op(e.tensor_copy(R(G + P, (1, P)), X_[g][:, P:2 * P]), "ssd_g")
                    op(e.tensor_tensor(R(G + 2 * P, (1, P)), X_[g][:, 2 * P:3 * P], tri, ALU.mult), "ssd_g")
                settle()
                weigh(0)

            def xdt():
                for t in range(NT):
                    e.wait_ge(*after("xs_ready", 2 * (t + 1)))
                    op(e.tensor_tensor(R(XDT + t * D, (SP_, SH), (1, SP_)), R(XS + t * D, (SP_, SH), (1, SP_)),
                                       heads(dt[:, t * SH:(t + 1) * SH]), ALU.mult), "xdt")

            def skip():
                settle()
                for t in range(NT):
                    op(e.tensor_tensor(R(XS + t * D, (SP_, SH), (1, SP_)), R(XS + t * D, (SP_, SH), (1, SP_)),
                                       heads(row[:, 32:48]), ALU.mult))
                settle()

            gated("z", 1, ZZ, {2: lambda: (xdt(), skip(), ssd_g())})

            def y_add(t):
                for b in range(2):
                    e.wait_ge(*after("y_mm", 2 * t + b + 1))
                    y = R(XS + t * D + b * 512, (1, 512))
                    op(e.tensor_tensor(y, y, X_[2 * t + b][:, :], ALU.add), "y_add")

            def wx():
                e.wait_ge(*after("wts", 1))
                op(e.tensor_tensor(R(WX, (SP_, SH), (1, SP_)), R(XDT, (SP_, SH), (1, SP_)), heads(sm("wts", 16)),
                                   ALU.mult), "wx")

            by_rows("xk0_0", (xk[:, 0:2, :], xk[:, 2:4, :]), "mem", 1.0,
                    {0: lambda: y_add(0), 1: lambda: decay(1), 2: wx, 3: lambda: weigh(1)})

            def y_cross():
                e.wait_ge(*after("e1", 1))
                for g in range(SG):
                    e.wait_ge(*after("yc_mm", g + 1))
                    op(e.tensor_tensor(R(YC + g * 512, (SP_, 8), (1, SP_)),
                                       X_[g][:, :].rearrange("p (h q) -> p h q", h=8),
                                       heads(sm("e1", 16)[:, 8 * g:8 * g + 8]), ALU.mult), "yc_scaled")
                settle()
                link(e.tensor_tensor(R(XS + D, (1, D)), R(XS + D, (1, D)), R(YC, (1, D)), ALU.add))

            def gla_cum():
                for b in range(2):
                    e.wait_ge(*after("gcum_mm", b + 1))
                    op(e.tensor_scalar(R(CC2 + 1024 + b * 512, (1, 512)), X_[2 + b][:, :], -1.0 / TAU, None, ALU.mult),
                       "gcum")

            def gla_diag():
                for t in range(NT):
                    e.wait_ge(*after("diag_mm", t + 1))
                    op(e.tensor_tensor(R(STT_ + t * 512, (P, GH), (1, P)),
                                       X_[t][:, :].rearrange("p (h q) -> p h q", h=4),
                                       ident.unsqueeze(1).to_broadcast([P, GH, P]), ALU.mult), "gla_diag")

            def diff(n):
                buf = GXA if n % 2 == 0 else GXB
                if n >= 2:
                    e.wait_ge(*after("level_mm", 2 * (n - 2) + 1))
                if n == 0:
                    e.wait_ge(*after("gneg", 1))
                    op(e.tensor_tensor(R(buf, (L, GH), (1, P)), R(CC2, (L, GH), (1, P)), R(CC2 + P - 1, (L, GH), (0, P)),
                                       ALU.subtract), "gd")
                else:
                    b = LEVELS[n - 1]
                    m = 1024 // (2 * b)
                    op(e.tensor_tensor(R(buf, (2 * b, m), (b, 2), (1, b)), R(CC2, (2 * b, m), (1024 + b, 2), (1, b)),
                                       R(CC2 + b - 1, (2 * b, m), (1024, 2), (0, b)), ALU.subtract), "gd")

            def mult(n):
                buf = GXA if n % 2 == 0 else GXB
                b = P if n == 0 else LEVELS[n - 1]
                m = 1024 // (2 * b)
                e.wait_ge(*after("ge", n + 1))
                v = R(buf, (2 * b, m), (b, 2), (1, b))
                op(e.tensor_tensor(v, v, R(QK, (2 * b, m), (1024 + b, 2), (1, b)), ALU.mult), "gx")

            def scores(n):
                if n == 0:
                    e.wait_ge(*after("level_mm", 1))
                    op(e.tensor_copy(R(SXT, (1, 512)), X_[0][:, :]), "gla_cross")
                    return
                settle()
                for t in range(NT):
                    e.wait_ge(*after("level_mm", 2 * (n - 1) + t + 2))
                    op(e.copy_predicated(R(STT_ + t * 512, (P, GH), (1, P)),
                                         mask[:, n - 1, :].unsqueeze(1).to_broadcast([P, GH, P]),
                                         X_[2 * (n % 2) + t][:, :].rearrange("p (h q) -> p h q", h=4)), "gla_s")

            def step(n):
                def f():
                    if n < 7:
                        diff(n + 1)
                    if n < 8:
                        mult(n)
                    if n > 0:
                        scores(n - 1)
                return f

            def yz():
                hr = sm("n0_hr", 2)
                for t in range(NT):
                    y = R(XS + t * D, (1, D))
                    op(e.scalar_tensor_tensor(out=y, in0=y, scalar=hr[:, t:t + 1], in1=R(ZZ + t * D, (1, D)),
                                              op0=ALU.mult, op1=ALU.mult), "yz")

            def yn():
                e.wait_ge(*after("y_rstd", 1))
                for t in range(NT):
                    for g in range(SG):
                        y = R(XS + t * D + g * 512, (1, 512))
                        op(e.tensor_scalar(y, y, sm("y_r", 4)[:, 2 * t + g:2 * t + g + 1], None, ALU.mult), "yn")

            by_rows("xk0_1", (xk[:, 4:6, :], xk[:, 6:8, :]), "mem", 1.0,
                    {1: lambda: y_add(1), 2: y_cross, 3: lambda: (gla_cum(), yz())})
            e.wait_ge(*after("mask_loaded", 16))
            rm_ = sm("mem_r", 2)[:, 1:2]
            copy1("xv0_0", xv[:, 1, 0:512], rm_,
                  {0: gla_diag, 1: lambda: diff(0), 2: step(0)})
            copy1("xv0_1", xv[:, 1, 512:1024], rm_, {0: step(1), 1: yn, 2: step(2)})
            rx = sm("n0_r", 2)
            copy1("v0", R(VV + D, (1, 512)), rx[:, 1:2], {0: step(3), 2: step(4)})
            copy1("v1", R(VV + D + 512, (1, 512)), rx[:, 1:2], {0: step(5), 2: step(6)})
            gated("r", 0, RR, {0: step(7), 2: step(8)})
            gated("r", 1, RR, {1: lambda: lo_parts("y", B, lambda k: col("ssdn", k))})

            def o_norm():
                e.wait_ge(*after("o_rstd", 1))
                for n in ("r0", "r1"):
                    e.wait_ge(*evac(number[n], 1))
                for b in range(4):
                    for i in range(2):
                        t, h = b // 2, 2 * (b % 2) + i
                        op(e.scalar_tensor_tensor(out=R(OO + t * D + h * GV, (1, GV)),
                                                  in0=X_[b][:, i * GV:(i + 1) * GV],
                                                  scalar=sm("o_r", 8)[:, 2 * b + i:2 * b + i + 1],
                                                  in1=R(RR + t * D + h * GV, (1, GV)), op0=ALU.mult, op1=ALU.mult),
                           "on")

            add_x("outy0", 0, None, {3: o_norm})
            add_x("outy1", 1, None, {2: lambda: lo_parts("o", A, lambda k: col("glan", k % 2))})
            add_x("outo0", 0)
            add_x("outo1", 1, None, {1: lambda: lo_parts("xn0", B, lambda k: col("xa0", k), (0, 1))})

            def fin_gain(n):
                e.wait_ge(*after("fnorm_loaded", 16))
                for t in range(NT):
                    e.wait_ge(*evac(number[f"down1_{n}"], t))
                    op(e.tensor_tensor(result(t, n), x[:, t, n * 512:(n + 1) * 512],
                                       xk[:, 2 * n:2 * n + 2, :].rearrange("p a b -> p (a b)"), ALU.mult), "fin_gain")

            def tail(l, one, two):
                lo_parts(f"xn{l}", one, lambda k: col(f"xa{l}", k), (2, 3))
                nm, ri = sm(f"c{l}_nmax", 8), sm(f"c{l}_ri", 8)

                def maxima(hh):
                    e.wait_ge(*after(f"xn{l}_rstd", 1))
                    for t in range(NT):
                        e.wait_ge(*after(f"c{l}_score", 2 * hh + t + 1))
                        v = nm[:, t * XH + 2 * hh:t * XH + 2 * hh + 2]
                        link(e.tensor_reduce(v, X_[2 * hh + t][:, :].rearrange("p (h m) -> p h m", h=2), AX, ALU.max,
                                             negate=True))
                        op(e.tensor_scalar(v, v, sm(f"xn{l}_s", 2)[:, t:t + 1], None, ALU.mult), f"c{l}_max")

                def normalise(hh):
                    e.wait_ge(*after(f"c{l}_exp", 4 * (hh + 1)))
                    settle()
                    for t in range(NT):
                        at = t * XH + 2 * hh
                        link(e.reciprocal(ri[:, at:at + 2], sm(f"c{l}_sum", 8)[:, at:at + 2]))
                    for t in range(NT):
                        for i in range(2):
                            n = t * XH + 2 * hh + i
                            v = R(CP + n * NM, (1, NM))
                            op(e.tensor_scalar(v, v, ri[:, n:n + 1], None, ALU.mult), f"c{l}_p")

                def o_lo(hh):
                    for h in (2 * hh, 2 * hh + 1):
                        e.wait_ge(*after(f"c{l}_hi", h + 1))
                        op(e.tensor_tensor(two[1][:, 2 * h:2 * h + 2, :], X_[h][:, :].rearrange("p (a b) -> p a b", a=2),
                                           two[0][:, 2 * h:2 * h + 2, :].bitcast(F32), ALU.subtract), f"c{l}_lo")

                copy1(f"xq{l}_0", R(CQ + 2 * L, (L, 2), (1, L)))
                copy1(f"xq{l}_1", R(CQ + 6 * L, (L, 2), (1, L)), None,
                      {1: lambda: maxima(0), 2: lambda: normalise(0)})
                o_lo(0)
                maxima(1)
                normalise(1)
                ahead(f"xo{l}_0", {3: lambda: o_lo(1)})
                add_x(f"xo{l}_1", 1, None, {2: lambda: add_bank(number[f"xo{l}_0"], 0),
                                            4: lambda: lo_parts(f"mn{l}", one, lambda k: col(f"mlp{l}", k), (0, 1))})
                lo_parts(f"mn{l}", one, lambda k: col(f"mlp{l}", k), (2, 3))

                def hidden(n, now=first):
                    g = ahead(f"up{l}_{n}", {}, now)
                    if n > 0 or l > 0:
                        e.wait_ge(*later(after(f"hid{l}", 2 * n), 2 * PAIR, now))
                    for b in range(2):
                        e.wait_ge(*later(evac(g, b), 1, now))
                        op(e.tensor_tensor(sp[:, b, :], junk[:, b, :], junk[:, b, :], ALU.mult), "hid_sq")
                    for b in range(2):
                        e.wait_ge(*later(after("hid_hi", 16 * l + 2 * n + b + 1), 2 * PAIR, now))
                        at = bass.ds(now(4 * n + 2 * b, 4 * PAIR), 2)
                        op(e.tensor_tensor(hid_lo[:, at, :], sp[:, b, :].rearrange("p (a c) -> p a c", a=2),
                                           hid_hi[:, at, :].bitcast(F32), ALU.subtract), f"hid{l}")

                def dve_steps(n):
                    g = number[f"up{l}_{n}"]
                    high = split_steps(first_chunk[g] + 1)[0:PIECES:2]
                    own = [(after(f"hid{l}", 2 * n)[1], 2 * PAIR), (evac(g, 0)[1], 1)]
                    hid = [(after("hid_hi", 16 * l + 2 * n + b + 1)[1], 2 * PAIR) for b in range(2)]
                    return high + own + hid + [(4 * n + 2 * b, 4 * PAIR) for b in range(2)]

                for n in range(UP_PEEL):
                    hidden(n)
                start = looped()
                with e.Fori(0, UP_PASSES) as i:
                    now = passes(e, i, [at for n in range(UP_PEEL, UP_PEEL + PAIR) for at in dve_steps(n)])
                    for n in range(UP_PEEL, UP_PEEL + PAIR):
                        hidden(n, now)
                looped(start)
                e.wait_ge(*after(f"mn{l}_rstd", 1))
                add_x(f"down{l}_0", 0, sm(f"mn{l}_s", 2))
                add_x(f"down{l}_1", 1, sm(f"mn{l}_s", 2),
                      {1: lambda: lo_parts("n1", A, lambda k: col("od", k), (0, 1))} if l == 0
                      else {1: lambda: fin_gain(0)})

            tail(0, B, A)

            lo_parts("n1", A, lambda k: col("od", k), (2, 3))

            def lam_dot():
                lam = row[:, 48:48 + 4 * DHD].rearrange("p (m a d) -> p m a d", m=2, a=2)
                lp = sm("lam_p", 2 * DHD).rearrange("p (m d) -> p m d", m=2)
                link(e.tensor_tensor(lp, lam[:, :, 0, :], lam[:, :, 1, :], ALU.mult))
                op(e.tensor_reduce(sm("lam_d", 2), lp, AX, ALU.add), "lam_dot")

            nl = sm("nlam", 1)

            def lam_end():
                e.wait_ge(*after("lam_e", 1))
                le = sm("lam_e", 2)
                link(e.tensor_tensor(nl, le[:, 1:2], le[:, 0:1], ALU.subtract))
                link(e.tensor_scalar(nl, nl, LAMBDA_INIT, None, ALU.subtract))

            nm, rs = sm("d_nmax", 32), sm("d_sum", 32)
            r1 = sm("n1_r", 2)

            def diff_bias(r):
                t, per, first = ROUNDS[r]
                keys = (t + 1) * P
                at, base = (0, 8, 24)[r], SC + 2048 * (r % 2)
                for b in range(4):
                    e.wait_ge(*after("d_score", 4 * r + b + 1))
                    h0 = first + per * (b // 2)
                    op(e.scalar_tensor_tensor(out=R(base + b * 512, (keys, per), (1, keys)),
                                              in0=X_[b][:, :].rearrange("p (h k) -> p h k", h=per),
                                              scalar=r1[:, t:t + 1],
                                              in1=R(BIAS + h0 * L + L - keys, (L, per), (1, keys)), op0=ALU.mult,
                                              op1=ALU.add), "d_bias")
                settle()
                link(e.tensor_reduce(nm[:, at:at + 4 * per], R(base, (keys, 4 * per), (1, keys)), AX, ALU.max,
                                     negate=True), "d_max")

            def diff_mix(r):
                t, per, _ = ROUNDS[r]
                keys = (t + 1) * P
                at, base = (0, 8, 24)[r], SC + 2048 * (r % 2)
                e.wait_ge(*after("d_exp", (8, 24, 32)[r]))
                ri, rl = sm("d_ri", 32), sm("d_rl", 32)
                link(e.reciprocal(ri[:, at:at + 4 * per], rs[:, at:at + 4 * per]))
                link(e.tensor_scalar(rl[:, at:at + 4 * per], ri[:, at:at + 4 * per], nl, None, ALU.mult))
                if r > 0:
                    e.wait_ge(*after("d_anT", 2 * r))
                for pair in range(2):
                    for i in range(per):
                        n = per * pair + i
                        c0 = at + 2 * per * pair + i
                        p0 = R(base + (c0 - at) * keys, (1, keys))
                        op(e.tensor_scalar(R(AN + n * keys, (1, keys)), p0, ri[:, c0:c0 + 1], None, ALU.mult))
                settle()
                for pair in range(2):
                    for i in range(per):
                        n = per * pair + i
                        c1 = at + 2 * per * pair + i + per
                        an = R(AN + n * keys, (1, keys))
                        p1 = R(base + (c1 - at) * keys, (1, keys))
                        op(e.scalar_tensor_tensor(out=an, in0=p1, scalar=rl[:, c1:c1 + 1], in1=an, op0=ALU.mult,
                                                  op1=ALU.add), "d_an")

            copy1("dq0", R(DQ + 2 * L, (L, 2), (1, L)), DHD ** -0.5, {0: lam_dot})
            by_rows("dk0", qk_rows(DK), "n1", 1.0, {2: lam_end, 3: lambda: row_copy("n1", 2)})
            e.wait_ge(*after("bias_loaded", 16))
            copy1("dq1", R(DQ + 6 * L, (L, 2), (1, L)), DHD ** -0.5, {1: lambda: diff_bias(0)})
            by_rows("dk1", qk_rows(DK + 4 * L), "n1", 1.0, {0: lambda: diff_mix(0)})
            copy1("dv0", R(DV + D, (1, 512)), r1[:, 1:2], {1: lambda: diff_bias(1)})
            copy1("dv1", R(DV + D + 512, (1, 512)), r1[:, 1:2], {0: lambda: diff_mix(1)})
            by_rows("xk1_0", (xk[:, 0:2, :], xk[:, 2:4, :]), "mem", 1.0,
                    {0: lambda: diff_bias(2), 3: lambda: diff_mix(2)})

            def do_sums():
                for b in range(4):
                    e.wait_ge(*after("do_sq", b + 1))
                    op(e.tensor_reduce(sm("do_ss", 16)[:, 4 * b:4 * b + 4],
                                       junk[:, b % 2, :].rearrange("p (h v) -> p h v", h=4), AX, ALU.add), "do_sum")

            def do_norm():
                e.wait_ge(*after("do_rstd", 1))
                for b in range(4):
                    op(e.tensor_tensor(R(SC + b * 512, (P, 4), (1, P)), X_[b][:, :].rearrange("p (h v) -> p h v", h=4),
                                       heads(sm("do_r", 16)[:, 4 * b:4 * b + 4], P), ALU.mult), "d_on")

            by_rows("xk1_1", (xk[:, 4:6, :], xk[:, 6:8, :]), "mem", 1.0, {3: do_sums})
            copy1("xv1_0", xv[:, 1, 0:512], rm_, {3: do_norm})
            copy1("xv1_1", xv[:, 1, 512:1024], rm_, {1: lambda: lo_parts("d", A, lambda k: col("subln"))})
            add_x("dout0", 0)
            add_x("dout1", 1, None, {1: lambda: lo_parts("xn1", B, lambda k: col("xa1", k), (0, 1))})
            tail(1, B, A)
            fin_gain(1)
            e.wait_ge(*after("fin_rstd", 1))
            settle()
            for n in range(2):
                v = result(0, n)
                op(e.tensor_scalar(v, v, sm("fin_r", 2)[:, 0:1], None, ALU.mult), "final0")

        @block.gpsimd
        def _(e):
            op, settle, link, looped = tracker(e, "pool_step")

            def split(c, before={}, now=first):
                for j in range(PIECES):
                    if j in before:
                        before[j]()
                    if c >= len(chunks) or j % 2 == 0:
                        continue
                    width = chunks[c][3]
                    e.wait_ge(*later(after("hi_ready", 4 * c + j + 1), PAIR * PIECES, now))
                    op(e.tensor_tensor(w_lo[:, j, :, 0:width], raw[:, j, :, 0:width],
                                       w_hi[:, j, :, 0:width].bitcast(F32), ALU.subtract), "lo_pool")
                if PIECES in before:
                    before[PIECES]()

            def ahead(name, before={}, now=first):
                g = number[name]
                n = len(groups[g][2])
                for k in range(n):
                    split(first_chunk[g] + k + 1, before if k == n - 1 else {}, now)

            def rstd(key, n, width, count, wait="_sq"):
                e.wait_ge(*after(key + wait, count))
                r = sm(key + "_r", n)
                link(e.tensor_scalar(r, sm(key + "_ss", n), 1.0 / width, EPS, ALU.mult, ALU.add))
                link(e.tensor_tensor(r, r, neghalf[:, 0:n], ALU.pow))

            def rstd_x(key, post=None):
                e.wait_ge(*after(key + "_sq", 4))
                r, ss = sm(key + "_r", 2), sm(key + "_ss", 4)
                link(e.tensor_tensor(r, ss[:, 0:2], ss[:, 2:4], ALU.add))
                link(e.tensor_scalar(r, r, 1.0 / D, EPS, ALU.mult, ALU.add))
                last = e.tensor_tensor(r, r, neghalf[:, 0:2], ALU.pow)
                if post is not None:
                    link(last)
                    last = post(r)
                op(last, key + "_rstd")

            def mem_gain(l):
                for k in range(KT):
                    if l == 0:
                        e.wait_ge(*after("mem_copy", k // 2 + 1))
                    op(e.tensor_scalar(xk[:, k, :], mem_t[:, k, :], col(f"mem{l}", k), None, ALU.mult))

            def mem_lo(l):
                settle()
                for k in range(KT):
                    e.wait_ge(*after(f"mg{l}_hi", k + 1))
                    op(e.tensor_tensor(b_lo[:, k, :], xk[:, k, :], b_hi[:, k, :].bitcast(F32), ALU.subtract),
                       f"mg{l}_lo")

            op(e.memset(glr_t[:], 1.0), "ones_ready")
            op(e.memset(R(XB, (XBW, XT), (1, 3)), 0.0), "pad_ready")
            e.wait_ge(*after("const_loaded", 16))
            split(0)
            rstd_x("n0", lambda r: e.tensor_scalar(sm("n0_hr", 2), r, 0.5, None, ALU.mult))
            ahead("xbc0")
            rstd_x("mem")
            for name in ("xbc1", "xbc2", "q0", "k0"):
                ahead(name)
            ahead("z0", {1: lambda: mem_gain(0)})
            ahead("z1", {0: lambda: mem_lo(0)})
            for name in ("xk0_0", "xk0_1"):
                ahead(name)

            def y_rstd():
                rstd("y", 4, 512, 4)
                r = sm("y_r", 4)
                op(e.tensor_scalar(r, r, 1.0, None, ALU.mult), "y_rstd")

            ahead("xv0_0", {3: y_rstd})
            for name in ("xv0_1", "v0", "v1", "r0", "r1"):
                ahead(name)

            def o_rstd():
                rstd("o", 8, GV, 8)
                r = sm("o_r", 8).rearrange("p (t h) -> p t h", t=NT)
                hr = sm("n0_hr", 2).unsqueeze(2).to_broadcast([P, NT, GH])
                op(e.tensor_tensor(r, r, hr, ALU.mult), "o_rstd")

            ahead("outy0", {2: o_rstd})
            for name in ("outy1", "outo0", "outo1"):
                ahead(name)

            def tail(l):
                rstd_x(f"xn{l}", lambda r: e.tensor_scalar(sm(f"xn{l}_s", 2), r, XHD ** -0.5, None, ALU.mult))
                for name in (f"xq{l}_0", f"xq{l}_1", f"xo{l}_0", f"xo{l}_1"):
                    ahead(name)
                rstd_x(f"mn{l}", lambda r: e.tensor_tensor(sm(f"mn{l}_s", 2), r, r, ALU.mult))
                for n in range(UP_PEEL):
                    ahead(f"up{l}_{n}")
                start = looped()
                with e.Fori(0, UP_PASSES) as i:
                    now = passes(e, i, [at for n in range(PAIR) for at in
                                     split_steps(first_chunk[number[f"up{l}_{UP_PEEL + n}"]] + 1)[1:PIECES:2]])
                    for n in range(UP_PEEL, UP_PEEL + PAIR):
                        ahead(f"up{l}_{n}", {}, now)
                looped(start)
                ahead(f"down{l}_0")
                ahead(f"down{l}_1")

            tail(0)
            rstd_x("n1")
            for name in ("dq0", "dk0", "dq1", "dk1"):
                ahead(name)
            ahead("dv0", {0: lambda: mem_gain(1)})
            ahead("dv1", {0: lambda: mem_lo(1)})
            ahead("xk1_0")

            def do_rstd():
                rstd("do", 16, P, 4, "_sum")
                r = sm("do_r", 16)
                op(e.tensor_scalar(r, r, 1.0 - LAMBDA_INIT, None, ALU.mult), "do_rstd")

            ahead("xk1_1")
            ahead("xv1_0", {0: do_rstd})
            for name in ("xv1_1", "dout0", "dout1"):
                ahead(name)
            tail(1)
            rstd_x("fin")


def kernel(x, mem, ev_norm, ev_w_in, ev_conv_w, ev_conv_b, ev_dt_bias, ev_a_log, ev_d_skip, ev_ssd_norm, ev_gla_w2,
           ev_gla_b, ev_gla_norm, ev_w_out, od_norm, od_w_qkv, od_lam_q1, od_lam_k1, od_lam_q2, od_lam_k2, od_subln,
           od_w_o, xa_norm, xa_mem_norm, xa_wq, xa_wkv, xa_wo, mlp_norm, mlp_w1, mlp_w2, final_norm):
    import concourse.bacc as bacc
    from concourse.bass_utils import run_bass_kernel_spmd

    def rows(*arrays):
        return np.concatenate([np.asarray(a).reshape(-1, P) for a in arrays], axis=0)

    prow = rows(ev_norm[0], od_norm[0], xa_norm[0], xa_norm[1], xa_mem_norm[0], xa_mem_norm[1], mlp_norm[0],
                mlp_norm[1], ev_ssd_norm[0], ev_gla_norm[0], od_subln[0], ev_conv_w[0], ev_conv_b[0])
    row = np.concatenate([np.asarray(a).reshape(-1) for a in
                          (ev_dt_bias[0], ev_a_log[0], ev_d_skip[0], od_lam_q1[0], od_lam_k1[0], od_lam_q2[0],
                           od_lam_k2[0])])[None]
    w_in = np.asarray(ev_w_in)[0]
    w_small = np.concatenate([w_in[:, GLR0:GLR0 + RANK], np.zeros((D, DT_ROW - RANK), np.float32),
                              w_in[:, DT0:DT0 + SH]], axis=1)
    gla_w2b = np.concatenate([np.asarray(ev_gla_w2)[0], np.asarray(ev_gla_b)], axis=0)

    i, j = np.arange(P)[:, None], np.arange(P)[None, :]
    const = np.concatenate([i == j, i <= j, np.ones((P, P)), np.full((P, 16), -0.5)], axis=1).astype(np.float32)
    mask = np.stack([(i // (2 * b) == j // (2 * b)) & (i % (2 * b) < b) & (j % (2 * b) >= b) for b in LEVELS],
                    axis=1).astype(np.int32)
    dist = P + np.arange(P)[:, None] - np.arange(L)[None, :]
    slopes = np.array([2.0 ** -(h + 1) for h in range(DH)], np.float32)
    bias = np.where(dist[:, None, :] >= 0, -slopes[None, :, None] * dist[:, None, :], -3e38)
    bias = bias.astype(np.float32).reshape(P, DH * L)

    arrays = {
        "x": x, "mem": mem, "ev_w_in": ev_w_in, "ev_w_out": ev_w_out, "od_w_qkv": od_w_qkv, "od_w_o": od_w_o,
        "xa_wq": xa_wq, "xa_wkv": xa_wkv, "xa_wo": xa_wo, "mlp_w1": mlp_w1, "mlp_w2": mlp_w2,
        "prow": prow, "row": row, "w_small": w_small, "gla_w2b": gla_w2b, "fnorm": np.asarray(final_norm)[None],
        "const": const, "mask": mask, "bias": bias,
    }
    nc = bacc.Bacc("TRN2", target_bir_lowering=False, num_devices=1)
    given, w = {}, {}
    for name, a in arrays.items():
        a = np.ascontiguousarray(a)
        given["in_" + name] = a
        w[name] = nc.dram_tensor("in_" + name, a.shape, mybir.dt.from_np(a.dtype), kind="ExternalInput").ap()
    w["out"] = nc.dram_tensor("out", (1, L, D), F32, kind="ExternalOutput").ap()
    trunk(nc, w)
    result = run_bass_kernel_spmd(nc, [given], core_ids=[0])
    return result.results[0]["out"]
```
